# Optimizing a Trainium2 kernel written in Bass

```python
import math
import jax, jax.numpy as jnp
from jax import lax
import numpy as np

D_MODEL = 1024
BATCH = 1
SEQ = 512
DEPTH = 2

CHUNK = 64
N_META = 16
N_MIXERS = 2
ATTN_WINDOW = 128
WINDOW_CHUNKS = ATTN_WINDOW // CHUNK
HEAD_DIM = 64
N_Q_HEADS = D_MODEL // HEAD_DIM
N_KV_HEADS = N_Q_HEADS // 4
GQA_GROUP = N_Q_HEADS // N_KV_HEADS
Q_DIM = N_Q_HEADS * HEAD_DIM
KV_DIM = N_KV_HEADS * HEAD_DIM
QKV_DIM = Q_DIM + 2 * KV_DIM
GLA_HEADS = 4
GLA_KEY_DIM = D_MODEL // 2
GLA_VAL_DIM = D_MODEL
GLA_DK = GLA_KEY_DIM // GLA_HEADS
GLA_DV = GLA_VAL_DIM // GLA_HEADS
GLA_GATE_RANK = 16
GLA_TAU = 16.0
GLA_IN_DIM = 2 * GLA_KEY_DIM + 2 * GLA_VAL_DIM + GLA_GATE_RANK
N_GROUPS = 4
EXPERTS_PER_GROUP = 4
N_EXPERTS = N_GROUPS * EXPERTS_PER_GROUP
TOP_K = 2
D_EXPERT = D_MODEL // 4
DEEPNORM_ALPHA = (2 * DEPTH) ** 0.25
DEEPNORM_BETA = (8 * DEPTH) ** -0.25
LN_EPS = 1e-5
RMS_EPS = 1e-6
N_ATTN_LAYERS = (DEPTH + 1) // 2
N_GLA_LAYERS = DEPTH // 2

kernel_name = "hybrid_swa_sink_gla_hier_moe_deepnorm"

def layer_norm(x, g, b):
    xf = x.astype(jnp.float32)
    mu = jnp.mean(xf, axis=-1, keepdims=True)
    xc = xf - mu
    var = jnp.mean(xc * xc, axis=-1, keepdims=True)
    y = xc * lax.rsqrt(var + LN_EPS) * g.astype(jnp.float32) + b.astype(jnp.float32)
    return y.astype(x.dtype)

def alibi_slopes(n_heads):
    return jnp.exp2(-8.0 * jnp.arange(1, n_heads + 1, dtype=jnp.float32) / n_heads)

def sink_softmax(s, sink):
    m = jnp.maximum(jnp.max(s, axis=-1, keepdims=True), sink)
    p = jnp.exp(s - m)
    return p / (jnp.sum(p, axis=-1, keepdims=True) + jnp.exp(sink - m))

def sliding_sink_attention(h, w_in, sinks, w_out):
    B, L, _ = h.shape
    nc = (L - N_META) // CHUNK
    qkv = h @ w_in
    q, k, v = jnp.split(qkv, [Q_DIM, Q_DIM + KV_DIM], axis=-1)
    q = q.astype(jnp.float32).reshape(B, L, N_KV_HEADS, GQA_GROUP, HEAD_DIM) * (HEAD_DIM ** -0.5)
    k = k.astype(jnp.float32).reshape(B, L, N_KV_HEADS, HEAD_DIM)
    v = v.astype(jnp.float32).reshape(B, L, N_KV_HEADS, HEAD_DIM)
    slopes = alibi_slopes(N_Q_HEADS).reshape(N_KV_HEADS, GQA_GROUP)[:, :, None, None]
    sink = sinks.astype(jnp.float32).reshape(N_KV_HEADS, GQA_GROUP)[:, :, None, None]

    pos_m = jnp.arange(N_META)
    dist_m = jnp.abs(pos_m[:, None] - pos_m[None, :]).astype(jnp.float32)
    s_m = jnp.einsum('bqhgd,bkhd->bhgqk', q[:, :N_META], k[:, :N_META]) - slopes * dist_m
    p_m = sink_softmax(s_m, sink)
    o_m = jnp.einsum('bhgqk,bkhd->bqhgd', p_m, v[:, :N_META]).reshape(B, N_META, Q_DIM)

    def band(t):
        meta = jnp.broadcast_to(t[:, None, :N_META], (B, nc, N_META) + t.shape[2:])
        real = t[:, N_META:].reshape((B, nc, CHUNK) + t.shape[2:])
        padded = jnp.pad(real, ((0, 0), (WINDOW_CHUNKS - 1, 0), (0, 0), (0, 0), (0, 0)))
        parts = [padded[:, j:j + nc] for j in range(WINDOW_CHUNKS)]
        return jnp.concatenate([meta] + parts, axis=2)

    kb = band(k)
    vb = band(v)
    q_r = q[:, N_META:].reshape(B, nc, CHUNK, N_KV_HEADS, GQA_GROUP, HEAD_DIM)
    c_idx = jnp.arange(nc)
    offs = jnp.arange(CHUNK)
    q_pos = N_META + c_idx[:, None] * CHUNK + offs[None, :]
    band_chunk = c_idx[:, None] - (WINDOW_CHUNKS - 1) + jnp.arange(WINDOW_CHUNKS)[None, :]
    band_pos = (N_META + band_chunk[:, :, None] * CHUNK + offs[None, None, :]).reshape(nc, -1)
    k_pos = jnp.concatenate([jnp.broadcast_to(pos_m[None, :], (nc, N_META)), band_pos], axis=1)
    k_valid = jnp.concatenate([jnp.ones((nc, N_META), dtype=bool),
                               jnp.repeat(band_chunk >= 0, CHUNK, axis=1)], axis=1)
    dist = jnp.abs(q_pos[:, :, None] - k_pos[:, None, :]).astype(jnp.float32)
    s = jnp.einsum('bcqhgd,bckhd->bchgqk', q_r, kb)
    s = s - slopes * dist[:, None, None]
    s = jnp.where(k_valid[:, None, None, None, :], s, -jnp.inf)
    p = sink_softmax(s, sink)
    o_r = jnp.einsum('bchgqk,bckhd->bcqhgd', p, vb).reshape(B, nc * CHUNK, Q_DIM)
    o = jnp.concatenate([o_m, o_r], axis=1).astype(h.dtype)
    return o @ w_out

def gla_mixer(h, w_in, w_gate_up, b_gate, norm_g, w_out):
    B, L, _ = h.shape
    proj = h @ w_in
    q, k, v, r, g_low = jnp.split(
        proj, [GLA_KEY_DIM, 2 * GLA_KEY_DIM, 2 * GLA_KEY_DIM + GLA_VAL_DIM,
               2 * GLA_KEY_DIM + 2 * GLA_VAL_DIM], axis=-1)
    log_a = jax.nn.log_sigmoid((g_low @ w_gate_up + b_gate).astype(jnp.float32)) / GLA_TAU
    pad = (-L) % CHUNK

    def to_chunks(t, dh):
        t = jnp.pad(t.astype(jnp.float32), ((0, 0), (pad, 0), (0, 0)))
        return t.reshape(B, -1, CHUNK, GLA_HEADS, dh)

    q_c = to_chunks(q, GLA_DK) * (GLA_DK ** -0.5)
    k_c = to_chunks(k, GLA_DK)
    v_c = to_chunks(v, GLA_DV)
    b_cum = jnp.cumsum(to_chunks(log_a, GLA_DK), axis=2)
    b_last = b_cum[:, :, -1:]
    q_dec = q_c * jnp.exp(b_cum)
    k_inv = k_c * jnp.exp(-b_cum)
    k_end = k_c * jnp.exp(b_last - b_cum)
    causal = jnp.tril(jnp.ones((CHUNK, CHUNK), dtype=bool))
    a = jnp.where(causal, jnp.einsum('bnchd,bnshd->bnhcs', q_dec, k_inv), 0.0)
    o_intra = jnp.einsum('bnhcs,bnshv->bnchv', a, v_c)

    def step(state, inp):
        q_n, k_n, v_n, dec_n = inp
        o_n = jnp.einsum('bchd,bhdv->bchv', q_n, state)
        state = dec_n[..., None] * state + jnp.einsum('bchd,bchv->bhdv', k_n, v_n)
        return state, o_n

    s0 = jnp.zeros((B, GLA_HEADS, GLA_DK, GLA_DV), jnp.float32)
    xs = (jnp.moveaxis(q_dec, 1, 0), jnp.moveaxis(k_end, 1, 0), jnp.moveaxis(v_c, 1, 0),
          jnp.moveaxis(jnp.exp(b_last[:, :, 0]), 1, 0))
    _, o_inter = lax.scan(step, s0, xs)
    o = o_intra + jnp.moveaxis(o_inter, 0, 1)
    o = o.reshape(B, -1, GLA_HEADS, GLA_DV)[:, pad:]
    o = o * lax.rsqrt(jnp.mean(o * o, axis=-1, keepdims=True) + RMS_EPS)
    o = o.reshape(B, L, GLA_VAL_DIM) * norm_g.astype(jnp.float32) * jax.nn.silu(r.astype(jnp.float32))
    return o.astype(h.dtype) @ w_out

def hier_moe(h, w_group, b_group, w_router, b_router, w_gate, w_up, w_down):
    B, L, D = h.shape
    t = h.reshape(-1, D)
    g_logits = (t @ w_group).astype(jnp.float32) + b_group.astype(jnp.float32)
    g_prob = jax.nn.softmax(g_logits, axis=-1)
    g_top, g_idx = lax.top_k(g_prob, 1)
    e_all = jnp.einsum('td,gde->tge', t, w_router).astype(jnp.float32) + b_router.astype(jnp.float32)
    e_logits = jnp.take_along_axis(e_all, g_idx[:, :, None], axis=1)[:, 0]
    e_top, e_idx = lax.top_k(jax.nn.softmax(e_logits, axis=-1), TOP_K)
    weight = g_top * (e_top / jnp.sum(e_top, axis=-1, keepdims=True))
    expert_id = g_idx * EXPERTS_PER_GROUP + e_idx
    combine = jnp.sum(jax.nn.one_hot(expert_id, N_EXPERTS, dtype=jnp.float32) * weight[..., None], axis=1)
    hid = jax.nn.silu(jnp.einsum('td,edf->tef', t, w_gate)) * jnp.einsum('td,edf->tef', t, w_up)
    y = jnp.einsum('tef,efd->td', hid * combine[:, :, None], w_down)
    return y.astype(h.dtype).reshape(B, L, D)

def setup_inputs(seed: int = 0) -> dict:
    key = jax.random.key(seed)
    ks = jax.random.split(key, 24)

    def w(k, shape, fan_in, gain=1.0):
        return jax.random.normal(k, shape, jnp.float32) * (fan_in ** -0.5) * gain

    na, ng = N_ATTN_LAYERS, N_GLA_LAYERS
    return {
        'x': jax.random.normal(ks[0], (BATCH, SEQ, D_MODEL), jnp.float32),
        'meta_tokens': jax.random.normal(ks[1], (N_META, D_MODEL), jnp.float32),
        'attn_w_in': w(ks[2], (na, D_MODEL, QKV_DIM), D_MODEL),
        'attn_sinks': 0.5 * jax.random.normal(ks[3], (na, N_Q_HEADS), jnp.float32),
        'attn_w_out': w(ks[4], (na, Q_DIM, D_MODEL), Q_DIM, DEEPNORM_BETA),
        'gla_w_in': w(ks[5], (ng, D_MODEL, GLA_IN_DIM), D_MODEL),
        'gla_w_gate_up': w(ks[6], (ng, GLA_GATE_RANK, GLA_KEY_DIM), GLA_GATE_RANK),
        'gla_b_gate': 0.1 * jax.random.normal(ks[7], (ng, GLA_KEY_DIM), jnp.float32),
        'gla_norm_g': 1.0 + 0.02 * jax.random.normal(ks[8], (ng, GLA_VAL_DIM), jnp.float32),
        'gla_w_out': w(ks[9], (ng, GLA_VAL_DIM, D_MODEL), GLA_VAL_DIM, DEEPNORM_BETA),
        'moe_w_group': w(ks[10], (DEPTH, D_MODEL, N_GROUPS), D_MODEL),
        'moe_b_group': 0.01 * jax.random.normal(ks[11], (DEPTH, N_GROUPS), jnp.float32),
        'moe_w_router': w(ks[12], (DEPTH, N_GROUPS, D_MODEL, EXPERTS_PER_GROUP), D_MODEL),
        'moe_b_router': 0.01 * jax.random.normal(ks[13], (DEPTH, N_GROUPS, EXPERTS_PER_GROUP), jnp.float32),
        'moe_w_gate': w(ks[14], (DEPTH, N_EXPERTS, D_MODEL, D_EXPERT), D_MODEL),
        'moe_w_up': w(ks[15], (DEPTH, N_EXPERTS, D_MODEL, D_EXPERT), D_MODEL),
        'moe_w_down': w(ks[16], (DEPTH, N_EXPERTS, D_EXPERT, D_MODEL), D_EXPERT, DEEPNORM_BETA),
        'ln_g': 1.0 + 0.02 * jax.random.normal(ks[17], (DEPTH, 2, D_MODEL), jnp.float32),
        'ln_b': 0.02 * jax.random.normal(ks[18], (DEPTH, 2, D_MODEL), jnp.float32),
    }

def reference(x, meta_tokens, attn_w_in, attn_sinks, attn_w_out, gla_w_in, gla_w_gate_up,
              gla_b_gate, gla_norm_g, gla_w_out, moe_w_group, moe_b_group, moe_w_router,
              moe_b_router, moe_w_gate, moe_w_up, moe_w_down, ln_g, ln_b):
    B = x.shape[0]
    meta = jnp.broadcast_to(meta_tokens.astype(x.dtype)[None], (B, N_META, D_MODEL))
    h = jnp.concatenate([meta, x], axis=1)
    for i in range(DEPTH):
        j = i // N_MIXERS
        if i % N_MIXERS == 0:
            mix = sliding_sink_attention(h, attn_w_in[j], attn_sinks[j], attn_w_out[j])
        else:
            mix = gla_mixer(h, gla_w_in[j], gla_w_gate_up[j], gla_b_gate[j], gla_norm_g[j], gla_w_out[j])
        h = layer_norm(DEEPNORM_ALPHA * h + mix, ln_g[i, 0], ln_b[i, 0])
        ffn = hier_moe(h, moe_w_group[i], moe_b_group[i], moe_w_router[i], moe_b_router[i],
                       moe_w_gate[i], moe_w_up[i], moe_w_down[i])
        h = layer_norm(DEEPNORM_ALPHA * h + ffn, ln_g[i, 1], ln_b[i, 1])
    return h[:, N_META:]


_drawn_inputs = setup_inputs


def setup_inputs(seed=0):
    import zlib

    import numpy as np

    out = dict(_drawn_inputs(seed))
    spreads = {}
    factors = {'attn_sinks': 6.341,
     'gla_b_gate': 4.829,
     'gla_norm_g': 8.0,
     'moe_b_group': 5.502,
     'moe_b_router': 8.0}
    for name, (base, spread) in spreads.items():
        noise = np.random.default_rng([zlib.crc32(name.encode()), seed]).standard_normal(out[name].shape)
        drawn = base * np.exp(spread * noise) if base else spread * noise
        out[name] = __import__('jax').numpy.asarray(drawn.astype(out[name].dtype))
    for name, factor in factors.items():
        out[name] = (out[name] * factor).astype(out[name].dtype)
    return out
```

```python
from contextlib import ExitStack

import concourse.bass as bass
from concourse import mybir

F32 = mybir.dt.float32
F32R = mybir.dt.float32r
BF16 = mybir.dt.bfloat16
I32 = mybir.dt.int32
U32 = mybir.dt.uint32
ALU = mybir.AluOpType
ACT = mybir.ActivationFunctionType
X = mybir.AxisListType.X

P = 128
D = 1024
KD = D // P
SEQ = 512
META = 16
L = SEQ + META
TILES = SEQ // P
MT = TILES
HALF = L // 2
XW = SEQ + P
NH = 16
NKV = 4
GQ = NH // NKV
HD = 64
CHUNK = 64
ALPHA = 4 ** 0.25
LN_EPS = 1e-5
RMS_EPS = 1e-6
NG = 4
EPG = 4
NE = NG * EPG
FE = 256
KF = FE // P
GH = 4
DK = 128
DV = 256
GCH = SEQ // CHUNK
RANK = 16
GLA_LOW = 2 * GH * DK + 2 * GH * DV
TAU = 16.0
ROUNDS = -(-L // P)
BIG = 1e30

RING = 8
UNIT = 1024

U_Q = 0
U_K = 8
U_V = 10
U_AO = 12
U_MOE0 = 20
U_GL = U_MOE0 + 6 * NE
U_GV = U_GL + 9
U_GR = U_GV + 8
U_GO = U_GR + 8
U_MOE1 = U_GO + 8
U_END = U_MOE1 + 6 * NE


def build_trunk(nc, x, meta_tokens, attn_w_in, attn_sinks, attn_w_out, gla_w_in, gla_w_gate_up, gla_b_gate,
                gla_norm_g, gla_w_out, moe_w_group, moe_b_group, moe_w_router, moe_b_router, moe_w_gate,
                moe_w_up, moe_w_down, ln_g, ln_b, out):
    ctx = ExitStack()
    with ctx:
        def sb(name, shape, dt):
            return ctx.enter_context(nc.sbuf_tensor(name, shape, dt))



        def sem(name):

            return ctx.enter_context(nc.semaphore(name))

        def scratch(name, shape):
            return nc.dram_tensor(name, shape, F32, kind="Internal").ap()

        h1_d = scratch("h1_d", (L, D))
        h2_d = scratch("h2_d", (L, D))
        h3_d = scratch("h3_d", (SEQ, D))
        r_d = scratch("r_d", (SEQ, D))
        y_d = [scratch(f"y{l}_d", (2 * L, D)) for l in range(2)]

        w_raw = sb("w_raw", [P, RING, UNIT], F32)
        w_hi = sb("w_hi", [P, RING, UNIT], F32R)
        w_lo = sb("w_lo", [P, RING, UNIT], F32R)
        xT_hi = sb("xT_hi", [P, KD, XW], F32R)
        xT_lo = sb("xT_lo", [P, KD, XW], F32R)
        ident = sb("ident", [P, P], F32)
        tri = sb("tri", [P, P], BF16)
        ones = sb("ones", [P, P], BF16)
        ids = sb("ids", [P, TILES + 1, NE, 3], BF16)
        slot_id = sb("slot_id", [P, P], BF16)
        rev4 = sb("rev4", [P, EPG], F32)
        wgt = sb("wgt", [P, TILES + 1, 2], F32)
        rounds = sb("rounds", [P, 1], I32)
        idx = sb("idx", [P, 2, NE], I32)
        causal = sb("causal", [P, P], BF16)
        lg_sb = sb("lg_sb", [P, TILES + 1, NG + NE], F32)
        w_rt = sb("w_rt", [P, 2, KD, NG + NE], F32)
        b_rt = sb("b_rt", [P, 2, NG + NE], F32)
        sink_b = sb("sink_b", [P, NH], F32)
        zrow = sb("zrow", [P, 2, D], F32)
        gb = sb("gb", [P, 2, D], F32)
        ln_st = sb("ln_st", [P, 24], F32)
        ARENA = 13056
        arena = sb("arena", [P, ARENA], F32)

        def carve():
            at = [0]

            def take(n):
                a = arena[:, at[0]:at[0] + n]
                at[0] += n
                assert at[0] <= ARENA, at[0]
                return a
            return take

        take = carve()
        qT = take(8 * L).rearrange("p (f n) -> p f n", f=8)
        kT = take(2 * L).rearrange("p (f n) -> p f n", f=2)
        kside = take(TILES * 2 * P).rearrange("p (t f n) -> p t f n", t=TILES, f=2)
        v_sb = take((TILES + 1) * 256).rearrange("p (t n) -> p t n", t=TILES + 1)
        vside = take(TILES * 256).rearrange("p (t n) -> p t n", t=TILES)
        dist = take(TILES * 256).rearrange("p (t n) -> p t n", t=TILES)
        prob = take(2 * GQ * 256).rearrange("p (b j n) -> p b j n", b=2, j=GQ)
        tpose = take(KD * P).rearrange("p (k n) -> p k n", k=KD)
        sm_st = take(2 * 24).rearrange("p (b n) -> p b n", b=2)

        take = carve()
        xg = take(2 * D).rearrange("p (b n) -> p b n", b=2)
        sil = take(2 * FE).rearrange("p (b n) -> p b n", b=2)
        hid = take(2 * FE).rearrange("p (b n) -> p b n", b=2)
        rt = take(2048)
        hot_at = take(TILES * D + D)
        hot = hot_at.bitcast(BF16).rearrange("p (t e n) -> p t e n", t=TILES + 1, e=NE)
        ysb = hot_at[:, 0:2 * D].rearrange("p (b n) -> p b n", b=2)
        take(D)
        ov_gu = hot_at[:, 0:KD * 2 * FE].rearrange("p (k m c) -> p k m c", k=KD, m=2)
        ov_dn = hot_at[:, KD * 2 * FE:KD * 2 * FE + D]
        ov_dn2 = take(D)
        ov_hot = take((TILES + 1) * P // 2).bitcast(BF16).rearrange("p (t n) -> p t n", t=TILES + 1)
        ov_ids = take(2 * (TILES + 1)).bitcast(BF16)[:, 0:3 * (TILES + 1)].rearrange("p (t c) -> p t c", t=TILES + 1)
        ov_rm = take(TILES + 1)
        ov_tab = take(4)
        ov_idx = take(2).bitcast(I32)
        ov_hT = take(KF * P).rearrange("p (f n) -> p f n", f=KF)
        ov_y = xg[:, 0, :]
        ov_xT = xg[:, 1, :].rearrange("p (k n) -> p k n", k=KD)
        ycomb = arena[:, ARENA - 4 * D:ARENA].rearrange("p (b k n) -> p b k n", b=2, k=2)

        take = carve()
        qdec = take(GH * L).rearrange("p (h n) -> p h n", h=GH)
        kinv = take(GH * L).rearrange("p (h n) -> p h n", h=GH)
        gv_at = take(TILES * D)
        gv = gv_at.rearrange("p (t n) -> p t n", t=TILES)
        la, lm, cb, eb, fb, scan0, gl_t = (gv_at[:, i * L:(i + 1) * L] for i in range(7))
        o_sb = take(D)
        vm = o_sb[0:META, :]
        state = take(GH * DV).rearrange("p (h n) -> p h n", h=GH)
        rbuf = take(D)
        at_sb = take(2 * P).rearrange("p (b n) -> p b n", b=2)
        ktok = take(P)
        kend = take(P)
        junk = take(DV)
        gup = take(GH * DK)[0:RANK, :]
        bg = take(GH)
        dec = take(GH * (GCH + 1)).rearrange("p (h c) -> p h c", h=GH)
        ssq = take(3 * GH).rearrange("p (k h) -> p k h", k=3)

        bank = ctx.enter_context(nc.psum_tensor("bank", [P, 8, 512], F32))
        ps_q = [bank[:, 2 * b:2 * b + 2, :] for b in range(2)]
        ps_s = bank[:, 0:2, :].rearrange("p b (j n) -> p (b j) n", j=2)
        ps_t = bank[:, 2:4, :].rearrange("p b (k n) -> p (b k) n", k=4)
        ps_o = bank[:, 4, 0:2 * P].rearrange("p (j n) -> p j n", j=2)
        ps_r = bank[:, 5, :]
        ps_y = bank[:, 6:8, :]
        ps_gu = bank[:, 0, :]
        ps_h = bank[:, 1, 0:2 * P].rearrange("p (f n) -> p f n", f=KF)
        ps_rank = bank[:, 4, 0:(TILES + 2) * NE].rearrange("p (t e) -> p t e", e=NE)
        ps_tab = bank[:, 4, 256:256 + 3 * NE].rearrange("p (e c) -> p e c", c=3)

        raw_landed = [sem(f"raw_landed{s}") for s in range(RING)]
        hi_done = sem("hi_done")
        lo_done = sem("lo_done")
        ao_used = sem("ao_used")
        var_ready = sem("var_ready")
        rstd_ready = sem("rstd_ready")

        def unit_src(u):
            if u < U_K:
                a = (u // 2) % 2 + 4 * (u // 4) + 2 * (u % 2)
                return attn_w_in[0][:, a * P:(a + 1) * P].rearrange("(k p) c -> p k c", p=P), (KD, P)
            if u < U_V:
                c = NH * HD + (u - U_K) * P
                return attn_w_in[0][:, c:c + P].rearrange("(k p) c -> p k c", p=P), (KD, P)
            if u < U_AO:
                c = (NH + NKV) * HD
                k = 4 * (u - U_V)
                return attn_w_in[0][k * P:(k + 4) * P, c:c + 256].rearrange("(k p) c -> p k c", p=P), (4, 256)
            if u < U_MOE0:
                k = u - U_AO
                return attn_w_out[0][k * P:(k + 1) * P, :], None
            g = u - U_GL
            if g == 0:
                return gla_w_in[0][:, GLA_LOW:GLA_LOW + RANK].rearrange("(k p) c -> p k c", p=P), (KD, P)
            if u < U_GV:
                c = (g - 1) % 2 * GH * DK + (g - 1) // 2 * DK
                return gla_w_in[0][:, c:c + P].rearrange("(k p) c -> p k c", p=P), (KD, P)
            if u < U_GO:
                v = u - U_GV
                c = 2 * GH * DK + 512 * (v // 4)
                k = 2 * (v % 4)
                return gla_w_in[0][k * P:(k + 2) * P, c:c + 512].rearrange("(k p) c -> p k c", p=P), (2, 512)
            k = u - U_GO
            return gla_w_out[0][k * P:(k + 1) * P, :], None

        order = [MT] + list(range(TILES))
        steps = [(i, order[i], g) for i in range(len(order)) for g in range(NKV)]
        NS = len(steps)

        def rows(t):
            return META if t == MT else P

        def cols(t):
            return slice(t * P, t * P + rows(t))

        def blocks(t):
            return 1 if t == MT else 2

        def width(t):
            return META if t == MT else 2 * P

        tp_order = [("x", t) for t in order]
        for n in range(NS):
            tp_order.append(("p", n))
            if n % NKV == 1 and n >= 9:
                tp_order.append(("h", n // NKV - 2))
        tp_order += [("h", len(order) - 2), ("h", len(order) - 1)]
        tp_at = {k: n for n, k in enumerate(tp_order)}

        def moe_stream():
            out = [("gu", 0, j) for j in range(4)]
            for b in range(NE + 1):
                if b >= 1:
                    out += [("dn", b - 1, f) for f in range(KF)]
                if b + 1 < NE:
                    out += [("gu", b + 1, j) for j in range(4)]
            return out

        x_landed = [sem(f"x_landed{i}") for i in range(2)]
        cst = sem("cst")
        prm = [sem(f"prm{i}") for i in range(3)]
        tp_full = sem("tp_full")
        tp_hi = sem("tp_hi")
        tp_lo = sem("tp_lo")
        q_full = sem("q_full")
        q_out = sem("q_out")
        kv_full = sem("kv_full")
        v_out = sem("v_out")
        side_done = sem("side_done")
        s_full = sem("s_full")
        s_read = sem("s_read")
        front_done = sem("front_done")
        exp_done = sem("exp_done")
        p_ready = sem("p_ready")
        o_full = sem("o_full")
        o_hi = sem("o_hi")
        o_lo = sem("o_lo")
        y_full = sem("y_full")
        y_read = sem("y_read")
        h_ready = sem("h_ready")
        h_stored = [sem(f"h_stored{i}") for i in range(2)]
        rt_full = sem("rt_full")
        dve_order = sem("dve_order")
        act_order = sem("act_order")
        zero_done = sem("zero_done")

        def per_layer(name):
            return [sem(f"{name}{l}") for l in range(2)]

        exp_asked = per_layer("exp_asked")
        exp_given = per_layer("exp_given")
        chosen = per_layer("chosen")
        rank_full = per_layer("rank_full")
        hot_ready = per_layer("hot_ready")
        tab_full = per_layer("tab_full")
        idx_ready = per_layer("idx_ready")
        gathered = [sem(f"gathered{b}") for b in range(2)]
        xt_full = sem("xt_full")
        x_hi_done = sem("x_hi_done")
        x_lo_done = sem("x_lo_done")
        gu_used = sem("gu_used")
        silu_done = sem("silu_done")
        mul_done = sem("mul_done")
        ht_full = sem("ht_full")
        h_hi_done = sem("h_hi_done")
        h_lo_done = sem("h_lo_done")
        dn_used = sem("dn_used")
        y_out = sem("y_out")
        y_stored = [sem(f"y_stored{b}") for b in range(2)]
        comb_landed = [per_layer(f"comb_landed{b}_") for b in range(2)]
        gb_landed = per_layer("gb_landed")
        h2_ready = per_layer("h2_ready")
        h2_stored = [per_layer(f"h2_stored{b}_") for b in range(2)]
        ov_w = per_layer("ov_w")
        ov_g = per_layer("ov_g")
        ov_s = per_layer("ov_s")
        ov_dve = per_layer("ov_dve")
        ov_pe = per_layer("ov_pe")
        ov_act = per_layer("ov_act")
        h2_tp = sem("h2_tp")
        h2_hi = sem("h2_hi")
        h2_lo = sem("h2_lo")

        gprm = sem("gprm")
        gb_ng = sem("gb_ng")
        glow_full = sem("glow_full")
        glow_out = sem("glow_out")
        gate_full = sem("gate_full")
        qk_full = sem("qk_full")
        abs_done = sem("abs_done")
        ln_done = sem("ln_done")
        cum_done = sem("cum_done")
        ef_done = sem("ef_done")
        dec_done = sem("dec_done")
        gv_full = sem("gv_full")
        gv_out = sem("gv_out")
        r_ready = sem("r_ready")
        r_stored = [sem(f"r_stored{i}") for i in range(4)]
        r_landed = sem("r_landed")
        kend_done = sem("kend_done")
        kt_full = sem("kt_full")
        ktok_done = sem("ktok_done")
        at_done = sem("at_done")
        o_part = sem("o_part")
        ua_full = sem("ua_full")
        ub_full = sem("ub_full")
        sa_done = sem("sa_done")
        sb_done = sem("sb_done")
        go_full = sem("go_full")
        o_copied = sem("o_copied")
        sq_done = sem("sq_done")
        gated = sem("gated")
        gtp_full = sem("gtp_full")
        gtp_hi = sem("gtp_hi")
        gtp_lo = sem("gtp_lo")
        gy_full = sem("gy_full")
        gy_read = sem("gy_read")
        go_used = sem("go_used")
        z_landed = [sem(f"z_landed{i}") for i in range(2)]
        gb_l3 = sem("gb_l3")
        h3_ready = sem("h3_ready")
        lm_done = sem("lm_done")
        qd_done = sem("qd_done")
        um_full = sem("um_full")
        h3_stored = [sem(f"h3_stored{i}") for i in range(2)]
        lg_full = sem("lg_full")
        lg_read = sem("lg_read")
        gtp_order = []
        for t in range(TILES):
            if t >= 1:
                gtp_order.append(("o", t - 1))
            if t >= 2:
                gtp_order.append(("h", t - 2))
        gtp_order += [("o", TILES - 1), ("h", TILES - 2), ("h", TILES - 1)]
        gtp_at = {k: n for n, k in enumerate(gtp_order)}
        GM = TILES * GH

        def ub_wait(eng, m):
            if m // GH < TILES - 1:
                eng.wait_ge(ub_full, m + 1)

        def o_at(t):
            return o_sb if t == 0 else gv[:, t - 1, :]

        def r_piece(m):
            return zrow[:, (m % 4) // 2, 512 * (m % 2):512 * (m % 2) + 512]

        def further(eng, l, body, unroll=False):
            eng.wait_ge(idx_ready[l], 1)
            n = eng.value_load(rounds[0:1, 0:1], min_val=0, max_val=ROUNDS - 1)
            for r in range(1, ROUNDS):
                with eng.If(n >= r):
                    if unroll:
                        for e in range(NE):
                            body(r, e)
                    else:
                        with eng.Fori(0, NE) as e:
                            body(r, e)

        def moe_tiles(l):
            return list(range(TILES)) + ([MT] if l == 0 else [])

        block = ctx.enter_context(nc.Block())

        @block.sync
        def _(sp):
            def load_unit(u):
                s = u % RING
                if u >= RING:
                    sp.wait_ge(lo_done, u - RING + 1)
                src, shape = unit_src(u)
                dst = w_raw[:, s, :]
                if shape:
                    n = shape[0] // 2
                    dst = dst.rearrange("p (k c) -> p k c", k=shape[0])[:, :, 0:src.shape[2]]
                    halves = [(dst[:, h * n:h * n + n, :], src[:, h * n:h * n + n, :]) for h in range(2)]
                else:
                    n = UNIT // 2
                    halves = [(dst[:, h * n:h * n + n], src[:, h * n:h * n + n]) for h in range(2)]
                for d, a in halves:
                    sp.dma_start(d, a).then_inc(raw_landed[s], 16)

            def load_gu(l, s, e, j, ready):
                sp.wait_ge(lo_done, ready)
                dst = w_raw[:, s, :].rearrange("p (k m c) -> p k m c", k=2, m=2)
                for m, w in enumerate((moe_w_gate, moe_w_up)):
                    src = w[l, e, 2 * j * P:(2 * j + 2) * P, :] if isinstance(e, int) else \
                        w[l].rearrange("e d f -> (e d) f")[bass.ds(e * D + 2 * j * P, 2 * P), :]
                    sp.dma_start(dst[:, :, m, :], src.rearrange("(k p) c -> p k c", p=P)).then_inc(raw_landed[s], 16)

            def load_dn(l, s, e, f, ready):
                sp.wait_ge(lo_done, ready)
                for h in range(2):
                    src = moe_w_down[l, e, f * P:(f + 1) * P, h * 512:h * 512 + 512]
                    sp.dma_start(w_raw[:, s, h * 512:h * 512 + 512], src).then_inc(raw_landed[s], 16)

            def load_moe(l):
                u = (U_MOE0, U_MOE1)[l]
                for kind, b, j in moe_stream():
                    (load_gu if kind == "gu" else load_dn)(l, u % RING, b, j, u - RING + 1)
                    u += 1

            for u in range(U_MOE0):
                load_unit(u)
            load_moe(0)
            with nc.allow_non_contiguous_dma(reason="the low-rank gate's 16 columns"):
                for u in range(U_GL, U_MOE1):
                    load_unit(u)
            load_moe(1)

        @block.gpsimd
        def _(pool):
            def load_x(i):
                t = order[i]
                src = meta_tokens if t == MT else x[0][t * P:(t + 1) * P, :]
                return pool.dma_start(zrow[:rows(t), i % 2, :], src).then_inc(x_landed[i % 2], 16)

            load_x(0)
            load_x(1)
            nc.gpsimd.memset(ident[:], 0.0).then_inc(cst, 1)
            nc.gpsimd.memset(tri[:], 1.0).then_inc(cst, 1)
            nc.gpsimd.memset(ones[:], 1.0).then_inc(cst, 1)
            pool.wait_ge(cst, 3)
            nc.gpsimd.affine_select(out=ident[:], in_=ident[:], compare_op=ALU.not_equal, fill=1.0, base=0,
                                    pattern=[[-1, P]], channel_multiplier=1).then_inc(cst, 1)
            nc.gpsimd.affine_select(out=tri[:], in_=tri[:], compare_op=ALU.is_gt, fill=0.0, base=0,
                                    pattern=[[1, P]], channel_multiplier=-1).then_inc(cst, 1)
            for t in range(TILES):
                nc.gpsimd.iota(dist[:, t, 0:P], [[-1, P]], base=0, channel_multiplier=1,
                               allow_small_or_imprecise_dtypes=True).then_inc(cst, 1)
                nc.gpsimd.iota(dist[:, t, P:P + META], [[-1, META]], base=META + P * t, channel_multiplier=1,
                               allow_small_or_imprecise_dtypes=True).then_inc(cst, 1)
                nc.gpsimd.iota(dist[:, t, P + CHUNK:2 * P], [[-1, CHUNK]], base=CHUNK, channel_multiplier=1,
                               allow_small_or_imprecise_dtypes=True).then_inc(cst, 1)
            nc.gpsimd.memset(causal[:], 1.0).then_inc(cst, 1)
            pool.wait_ge(cst, 6 + 3 * TILES)
            nc.gpsimd.affine_select(out=causal[:], in_=causal[:], compare_op=ALU.is_ge, fill=0.0, base=0,
                                    pattern=[[1, P]], channel_multiplier=-1).then_inc(cst, 1)
            pool.wait_ge(cst, 7 + 3 * TILES)
            nc.gpsimd.memset(causal[0:CHUNK, CHUNK:P], 0.0).then_inc(cst, 1)
            nc.gpsimd.iota(slot_id[:], [[1, P]], base=0, channel_multiplier=0,
                           allow_small_or_imprecise_dtypes=True).then_inc(cst, 1)
            nc.gpsimd.iota(rev4[:], [[-1, EPG]], base=EPG, channel_multiplier=0,
                           allow_small_or_imprecise_dtypes=True).then_inc(cst, 1)
            nc.gpsimd.iota(ids[:, :, :, 0], [[P, TILES + 1], [0, NE]], base=0, channel_multiplier=0,
                           allow_small_or_imprecise_dtypes=True).then_inc(cst, 1)
            nc.gpsimd.iota(ids[:, :, :, 1], [[0, TILES + 1], [0, NE]], base=1, channel_multiplier=1,
                           allow_small_or_imprecise_dtypes=True).then_inc(cst, 1)
            pool.dma_start(sink_b[:], attn_sinks.rearrange("a h -> (a h)").partition_broadcast(P)).then_inc(prm[0], 16)
            for i in range(2, len(order)):
                pool.wait_ge(tp_full, i - 1)
                load_x(i)
            for l in range(2):
                with nc.allow_non_contiguous_dma(reason="router columns"):
                    pool.dma_start(w_rt[:, l, :, 0:NG],
                                   moe_w_group[l].rearrange("(k p) c -> p k c", p=P)).then_inc(prm[1], 16)
                    for g in range(NG):
                        pool.dma_start(w_rt[:, l, :, NG + EPG * g:NG + EPG * g + EPG],
                                       moe_w_router[l, g].rearrange("(k p) c -> p k c", p=P)).then_inc(prm[1], 16)
                pool.dma_start(b_rt[:, l, 0:NG], moe_b_group[l].partition_broadcast(P)).then_inc(prm[1], 16)
                pool.dma_start(b_rt[:, l, NG:], moe_b_router[l].rearrange("g e -> (g e)").partition_broadcast(P)
                               ).then_inc(prm[1], 16)
            pool.dma_start(gb[:, 0, :], ln_g[0, 0].partition_broadcast(P)).then_inc(prm[2], 16)
            pool.dma_start(gb[:, 1, :], ln_b[0, 0].partition_broadcast(P)).then_inc(prm[2], 16)
            pool.wait_ge(tp_full, len(order))
            for i in range(len(order)):
                if i >= 2:
                    pool.wait_ge(h_stored[i % 2], 16 * (i // 2))
                    pool.wait_ge(tp_full, tp_at[("h", i - 2)] + 1)
                t = order[i]
                src = meta_tokens if t == MT else x[0][t * P:(t + 1) * P, :]
                k = (len(order) + 1 - i % 2) // 2
                pool.dma_start(zrow[:rows(t), i % 2, :], src).then_inc(x_landed[i % 2], 16)

            def moe_pool(l, src, before):
                before()
                pool.dma_start(gb[:, 0, :], ln_g[l, 1].partition_broadcast(P)).then_inc(gb_landed[l], 16)
                pool.dma_start(gb[:, 1, :], ln_b[l, 1].partition_broadcast(P)).then_inc(gb_landed[l], 16)
                pool.wait_ge(idx_ready[l], 1)
                def gather(b):
                    if b >= 2:
                        pool.wait_ge(xt_full, NE * l + b - 1)
                    pool.indirect_dma_start(xg[:, b % 2, :], None, src,
                                            bass.IndirectOffsetOnAxis(ap=idx[:, 0, b:b + 1].bitcast(U32), axis=0),
                                            bounds_check=src.shape[0] - 1, oob_is_err=False).then_inc(gathered[b % 2], 16)

                gather(0)
                gather(1)
                for b in range(NE):
                    if b + 2 < NE:
                        gather(b + 2)
                    pool.wait_ge(y_out, NE * l + b + 1)
                    pool.indirect_dma_start(y_d[l], bass.IndirectOffsetOnAxis(ap=idx[:, 1, b:b + 1].bitcast(U32),
                                                                              axis=0),
                                            ysb[:, b % 2, :], None, bounds_check=2 * L - 1,
                                            oob_is_err=False).then_inc(y_stored[b % 2], 16)
                for b in range(2):
                    pool.wait_ge(y_stored[b], 8 * NE * l + 16 * NE // 2)

                def more(r, e):
                    q = e + NE * (r - 1)
                    pool.wait_ge(ov_dve[l], 9 * q + 8)
                    pool.indirect_dma_start(ov_y, None, src,
                                            bass.IndirectOffsetOnAxis(ap=ov_idx[:, 0:1].bitcast(U32), axis=0),
                                            bounds_check=src.shape[0] - 1, oob_is_err=False).then_inc(ov_g[l], 16)
                    pool.wait_ge(ov_act[l], 4 * q + 4)
                    pool.indirect_dma_start(y_d[l], bass.IndirectOffsetOnAxis(ap=ov_idx[:, 1:2].bitcast(U32), axis=0),
                                            ov_y, None, bounds_check=2 * L - 1,
                                            oob_is_err=False).then_inc(ov_s[l], 16)
                    if e == NE - 1:
                        pool.wait_ge(ov_s[l], 16 * q + 16)

                further(pool, l, more, unroll=True)
                for n, t in enumerate(moe_tiles(l)):
                    if n >= 2:
                        pool.wait_ge(h2_stored[n % 2][l], 16 * (n // 2))
                        if l == 0:
                            pool.wait_ge(h2_tp, n - 1)
                    R = rows(t)
                    pool.dma_start(zrow[:R, n % 2, :], src[cols(t), :]).then_inc(comb_landed[n % 2][l], 16)
                    for k in range(2):
                        pool.dma_start(ycomb[:R, n % 2, k, :], y_d[l][k * L + t * P:k * L + t * P + R, :]
                                       ).then_inc(comb_landed[n % 2][l], 16)

            def norm0_done():
                pool.wait_ge(h_ready, len(order))
                for b in range(2):
                    pool.wait_ge(h_stored[b], 16 * ((len(order) + 1 - b) // 2))
                pool.wait_ge(tp_full, len(tp_order))

            moe_pool(0, h1_d, norm0_done)

            pool.wait_ge(h2_ready[0], len(order))
            pool.dma_start(gb[:, 0, :], gla_norm_g[0].partition_broadcast(P)).then_inc(gb_ng, 16)
            pool.dma_start(gup, gla_w_gate_up[0]).then_inc(gprm, 16)
            with nc.allow_non_contiguous_dma(reason="the gate's bias, by partition"):
                pool.dma_start(bg, gla_b_gate[0].rearrange("(h p) -> p h", p=P)).then_inc(gprm, 16)
            pool.wait_ge(r_ready, 8)
            for c in range(2):
                src = (ln_g, ln_b)[c]
                pool.dma_start(gb[:, c, :], src[1, 0].partition_broadcast(P)).then_inc(gb_l3, 16)
            for i in range(4):
                pool.wait_ge(r_stored[i], 32)
            pool.wait_ge(sb_done, GH)
            pool.dma_start(rbuf, r_d[0:P, :]).then_inc(r_landed, 16)
            for t in range(TILES):
                if t >= 2:
                    pool.wait_ge(h3_stored[t % 2], 16 * (t // 2))
                    pool.wait_ge(gtp_full, gtp_at[("h", t - 2)] + 1)
                pool.dma_start(zrow[:, t % 2, :], h2_d[cols(t), :]).then_inc(z_landed[t % 2], 16)
                if t + 1 < TILES:
                    pool.wait_ge(gated, t + 1)
                    pool.dma_start(rbuf, r_d[cols(t + 1), :]).then_inc(r_landed, 16)

            def norm2_done():
                pool.wait_ge(h3_ready, TILES)
                for b in range(2):
                    pool.wait_ge(h3_stored[b], 16 * (TILES // 2))
                pool.wait_ge(gtp_full, len(gtp_order))

            moe_pool(1, h3_d, norm2_done)

        def x_count(i, again):
            n = i // 2 + 1
            return 16 * (n + ((len(order) + 1 - i % 2) // 2 if again else 0))

        def raw_unit(u):
            raw = w_raw[:, u % RING, :]
            return raw.rearrange("p (k f c) -> p f k c", k=KD, f=2) if u < U_K else raw

        def split_unit(w, u):
            s = u % RING
            if u >= U_K:
                return w[:, s, :]
            pair = w[:, s - u % 2:s - u % 2 + 2, :]
            return pair.rearrange("p f (k h c) -> p f k h c", h=2, c=HD)[:, :, :, u % 2, :]

        def unit_used(eng, u):
            if u < U_K:
                eng.wait_ge(q_full, 2 * (u // 2) + 2)
            elif u < U_V:
                eng.wait_ge(q_full, u + 1)
            elif u < U_AO:
                eng.wait_ge(kv_full, len(order))
            elif u < U_MOE0:
                eng.wait_ge(ao_used, u - U_AO + 1)
            elif u < U_GL:
                eng.wait_ge(dn_used, 2 * NE - (U_GL - 1 - u))
            elif u == U_GL:
                eng.wait_ge(glow_full, 1)
            elif u < U_GV:
                eng.wait_ge(qk_full, u - U_GL)
            elif u < U_GO:
                n = (u - U_GV) // 4
                eng.wait_ge(gv_full, (5, 10, 14, 18)[n])
            elif u < U_MOE1:
                eng.wait_ge(go_used, u - U_GO + 1)

        def ahead_used(eng, l, b, j):
            if j >= 4:
                eng.wait_ge(gu_used, 4 * NE * l + 4 * (b + 1) + j - 3)
            elif isinstance(b, int) and b == 0:
                eng.wait_ge(gu_used, 4 * NE * l + j + 1)
            elif j >= 2:
                eng.wait_ge(dn_used, 2 * NE * l + 2 * b + j - 3)
            else:
                eng.wait_ge(gu_used, 4 * NE * l + 4 * b + j + 3)

        RTW = TILES + 1
        rt_at = [0]

        def rt_take(*shape):
            n = 1
            for d in shape:
                n *= d
            a = rt[:, rt_at[0]:rt_at[0] + n]
            rt_at[0] += n
            names = "abcd"[:len(shape)]
            if len(shape) > 1:
                a = a.rearrange(f"p ({' '.join(names)}) -> p {' '.join(names)}", **dict(zip(names, shape)))
            return a

        rt_lg = rt_take(RTW, NG + NE)
        rt_g = rt_take(RTW, 1)
        rt_a = rt_take(RTW, EPG)
        rt_c = rt_take(RTW, EPG)
        rt_m = rt_take(RTW, 1)
        rt_ohg = rt_take(RTW, NG)
        rt_dg = rt_take(RTW, NG)
        rt_pr = rt_take(RTW, NG, EPG)
        rt_z = rt_take(RTW, EPG)
        rt_m1 = rt_take(RTW, 1)
        rt_m2 = rt_take(RTW, 1)
        rt_oh = [rt_take(RTW, EPG) for _ in range(2)]
        rt_both = rt_take(RTW, EPG)
        rt_dm = rt_take(RTW, 1)
        rt_gt = rt_take(RTW, 1)
        rt_w = rt_take(RTW, 2)
        rt_M = [rt_take(RTW, NE) for _ in range(2)]
        rt_rank = rt_take(RTW, NE)
        rt_q = rt_take(RTW, NE)
        rt_q2 = rt_take(RTW, NE)
        rt_rm = rt_take(RTW, NE)
        rt_p = rt_take(RTW, 2)
        rt_Mb = rt_take(RTW * NE // 2).bitcast(BF16).rearrange("p (t e) -> p t e", e=NE)

        def rt_exp(k, NT):
            return (rt_dg[:, 0:NT, :], rt_dm[:, 0:NT, :])[k]

        def store_h(act, j):
            t = order[j]
            act.wait_ge(h_ready, j + 1)
            act.dma_start(h1_d[cols(t), :], zrow[:rows(t), j % 2, :]).then_inc(h_stored[j % 2], 16)

        @block.scalar
        def _(act):
            norms = [0]

            def rsqrt(v, r):
                norms[0] += 1
                act.wait_ge(var_ready, norms[0])
                nc.scalar.activation(r, v, ACT.Ln).then_inc(act_order, 1)
                act.wait_ge(act_order, norms[0])
                nc.scalar.activation(r, r, ACT.Exp, scale=-0.5).then_inc(rstd_ready, 1)

            def split_hi(u):
                s = u % RING
                act.wait_ge(raw_landed[s], 32 * (u // RING + 1))
                if u >= RING:
                    unit_used(act, u - RING)
                nc.scalar.activation(split_unit(w_hi, u), raw_unit(u), ACT.Copy).then_inc(hi_done, 1)

            def x_hi(i):
                act.wait_ge(tp_full, i + 1)
                nc.scalar.activation(xT_hi[:, :, cols(order[i])], ps_t[:, :, 0:rows(order[i])],
                                     ACT.Copy).then_inc(tp_hi, 1)

            act.wait_ge(zero_done, 1)
            u = 0
            for i in range(len(order)):
                x_hi(i)
                if i >= 1:
                    split_hi(u)
                    u += 1
            while u < RING:
                split_hi(u)
                u += 1
            for f in range(8):
                act.wait_ge(q_full, f + 1)
                nc.scalar.activation(qT[:, f, :].rearrange("p (h n) -> p h n", h=2), ps_q[f % 2][:, :, 0:HALF],
                                     ACT.Copy, scale=HD ** -0.5).then_inc(q_out, 1)
                if f % 2:
                    split_hi(u)
                    split_hi(u + 1)
                    u += 2
            for f in range(2):
                act.wait_ge(q_full, 9 + f)
                nc.scalar.activation(kT[:, f, :].rearrange("p (h n) -> p h n", h=2), ps_q[f % 2][:, :, 0:HALF],
                                     ACT.Copy).then_inc(q_out, 1)
                split_hi(u)
                u += 1
            assert u == 18

            def exps(n):
                i, t, g = steps[n]
                R, W = rows(t), width(t)
                act.wait_ge(front_done, n + 1)
                for j in range(GQ):
                    nc.scalar.activation(prob[:R, n % 2, j, 0:W], prob[:R, n % 2, j, 0:W], ACT.Exp,
                                         bias=sm_st[:R, n % 2, 8 + j:9 + j],
                                         accum_out=sm_st[:R, n % 2, 16 + j:17 + j])
                nc.scalar.activation(sm_st[:R, n % 2, 12:16], sm_st[:R, n % 2, 12:16], ACT.Exp).then_inc(exp_done, 1)

            def copy_t(key, R, sub=None):
                m = tp_at[key]
                act.wait_ge(tp_full, m + 1)
                what, k = tp_order[m - 1]
                if what == "p":
                    act.wait_ge(o_full, k + 1)
                elif what == "h":
                    act.wait_ge(rt_full, k + 1)
                if sub:
                    src, dst = ps_t[0:META, 0::2, 0:R], tpose[0:META, 0::2, 0:R]
                else:
                    src, dst = ps_t[:, :, 0:R], tpose[:, :, 0:R]
                nc.scalar.activation(dst, src, ACT.Copy).then_inc(tp_hi, 1)

            act.wait_ge(side_done, 1)
            exps(0)
            n_h = 0
            for n in range(NS):
                i, t, g = steps[n]
                if n + 1 < NS:
                    exps(n + 1)
                if g == 0 and i >= 2:
                    rsqrt(ln_st[:, 13:14], ln_st[:, 14:15])
                copy_t(("p", n), rows(t), sub=(t == MT))
                act.wait_ge(o_full, n + 1)
                nc.scalar.activation(xT_hi[:, 2 * g:2 * g + 2, cols(t)], ps_o[:, :, 0:rows(t)],
                                     ACT.Copy).then_inc(o_hi, 1)
                if n < 2:
                    split_hi(18 + n)
                if n % NKV == 1 and n >= 9:
                    j = n // NKV - 2
                    store_h(act, j)
                    copy_t(("h", j), rows(order[j]))
            j = len(order) - 2
            rsqrt(ln_st[:, 13:14], ln_st[:, 14:15])
            store_h(act, j)
            for u in range(U_MOE0, U_MOE0 + RING):
                split_hi(u)
            copy_t(("h", j), P)
            rsqrt(ln_st[:, 13:14], ln_st[:, 14:15])
            store_h(act, j + 1)
            copy_t(("h", j + 1), P)
            for b in range(2):
                act.wait_ge(h_stored[b], 16 * ((len(order) + 1 - b) // 2))

            def hi_ahead(l, u0, b, c, j):
                r = RING + 6 * c + j
                s = (u0 + r) % RING
                act.wait_ge(raw_landed[s], 32 * ((u0 + r) // RING + 1) + 24 * (b - c))
                ahead_used(act, l, b, j)
                nc.scalar.activation(w_hi[:, s, :], w_raw[:, s, :], ACT.Copy).then_inc(hi_done, 1)

            def moe_act(l, u0):
                NT = len(moe_tiles(l))
                for k in range(2):
                    act.wait_ge(exp_asked[l], k + 1)
                    e = rt_exp(k, NT)
                    nc.scalar.activation(e, e, ACT.Exp).then_inc(exp_given[l], 1)

                def x_high(b):
                    act.wait_ge(xt_full, NE * l + b + 1)
                    c = slice((b % 2) * P, (b % 2) * P + P)
                    nc.scalar.activation(xT_hi[:, :, c], ps_t[:, :, :], ACT.Copy).then_inc(x_hi_done, 1)

                def y_evac(b):
                    act.wait_ge(dn_used, 2 * NE * l + 2 * b + 2)
                    if b >= 2:
                        act.wait_ge(y_stored[b % 2], 8 * NE * l + 16 * (b // 2))
                    nc.scalar.activation(ysb[:, b % 2, :].rearrange("p (h n) -> p h n", h=2), ps_y[:, :, :],
                                         ACT.Copy).then_inc(y_out, 1)

                def h_high(b):
                    act.wait_ge(ht_full, NE * l + b + 1)
                    c = slice((2 + b % 2) * P, (3 + b % 2) * P)
                    nc.scalar.activation(xT_hi[:, 0:KF, c], ps_h[:, :, :], ACT.Copy).then_inc(h_hi_done, 1)

                x_high(0)
                for b in range(NE):
                    act.wait_ge(gu_used, 4 * NE * l + 4 * b + 4)
                    if b >= 2:
                        act.wait_ge(mul_done, NE * l + b - 1)
                    nc.scalar.activation(sil[:, b % 2, :], ps_gu[:, 0:FE], ACT.Silu).then_inc(silu_done, 1)
                    if b + 1 < NE:
                        x_high(b + 1)
                    js = [j for j in range(6) if l == 0 or 8 + 6 * b + j < 6 * NE]
                    if b == NE - 1:
                        js = [j for j in js if j < 4]
                    for j in js[0:3]:
                        hi_ahead(l, u0, b, b % 4, j)
                    if b:
                        y_evac(b - 1)
                    for j in js[3:4]:
                        hi_ahead(l, u0, b, b % 4, j)
                    h_high(b)
                    for j in js[4:6]:
                        hi_ahead(l, u0, b, b % 4, j)
                y_evac(NE - 1)
                for b in range(2):
                    act.wait_ge(y_stored[b], 8 * NE * (l + 1))

                def more(r, e):
                    q = e + NE * (r - 1)
                    for m, w in enumerate((moe_w_gate, moe_w_up)):
                        rows_e = w[l].rearrange("e d f -> (e d) f")[bass.ds(e * D, D), :]
                        act.dma_start(ov_gu[:, :, m, :], rows_e.rearrange("(k p) c -> p k c", p=P)
                                      ).then_inc(ov_w[l], 16)
                    down = moe_w_down[l].rearrange("e f d -> (e f) d")
                    act.dma_start(ov_dn, down[bass.ds(e * FE, P), :]).then_inc(ov_w[l], 16)
                    act.dma_start(ov_dn2, down[bass.ds(e * FE + P, P), :]).then_inc(ov_w[l], 16)
                    act.wait_ge(ov_pe[l], 5 * q + 2)
                    nc.scalar.activation(ov_xT, ps_t[:, :, :], ACT.Copy).then_inc(ov_act[l], 1)
                    act.wait_ge(ov_pe[l], 5 * q + 3)
                    nc.scalar.activation(sil[:, 0, :], ps_gu[:, 0:FE], ACT.Silu).then_inc(ov_act[l], 1)
                    act.wait_ge(ov_pe[l], 5 * q + 4)
                    nc.scalar.activation(ov_hT, ps_h[:, :, :], ACT.Copy).then_inc(ov_act[l], 1)
                    act.wait_ge(ov_pe[l], 5 * q + 5)
                    nc.scalar.activation(ov_y.rearrange("p (h n) -> p h n", h=2), ps_y[:, :, :],
                                         ACT.Copy).then_inc(ov_act[l], 1)

                further(act, l, more)
                for n, t in enumerate(moe_tiles(l)):
                    rsqrt(ln_st[:, 13:14], ln_st[:, 14:15])
                    act.wait_ge(h2_ready[l], n + 1)
                    if l == 0:
                        act.dma_start(h2_d[cols(t), :], zrow[:rows(t), n % 2, :]).then_inc(h2_stored[n % 2][l], 16)
                    else:
                        act.dma_start(out[0][cols(t), :], zrow[:rows(t), n % 2, :]).then_inc(h2_stored[n % 2][l], 16)
                    if l == 0:
                        act.wait_ge(h2_tp, n + 1)
                        nc.scalar.activation(xT_hi[:, :, cols(t)], ps_t[:, :, 0:rows(t)], ACT.Copy).then_inc(h2_hi, 1)

            moe_act(0, U_MOE0)
            for b in range(2):
                act.wait_ge(h2_stored[b][0], 16 * ((len(moe_tiles(0)) + 1 - b) // 2))

            def store_r(m):
                act.wait_ge(r_ready, m + 1)
                act.dma_start(r_d[cols(m % 4), 512 * (m // 4):512 * (m // 4) + 512], r_piece(m)
                              ).then_inc(r_stored[m % 4], 16)

            for u in (U_GL + 6, U_GL + 7):
                split_hi(u)
            act.wait_ge(glow_full, 1)
            nc.scalar.activation(gl_t[0:RANK, :].rearrange("p (h n) -> p h n", h=2), bank[0:RANK, 6:8, 0:HALF],
                                 ACT.Copy).then_inc(glow_out, 1)
            split_hi(U_GL + 8)
            act.wait_ge(gprm, 32)
            for h in range(GH):
                act.wait_ge(gate_full, h + 1)
                if h:
                    act.wait_ge(cum_done, h)
                nc.scalar.activation(la.rearrange("p (h n) -> p h n", h=2), bank[:, 0:2, 0:HALF], ACT.Abs,
                                     bias=bg[:, h:h + 1]).then_inc(abs_done, 1)
                act.wait_ge(abs_done, 2 * h + 1)
                nc.scalar.activation(la, la, ACT.Exp, scale=-1.0).then_inc(abs_done, 1)
                act.wait_ge(abs_done, 2 * h + 2)
                nc.scalar.activation(la, la, ACT.Ln, bias=1.0).then_inc(ln_done, 1)
                act.wait_ge(cum_done, h + 1)
                if h:
                    act.wait_ge(dec_done, h)
                nc.scalar.activation(eb, cb, ACT.Exp, scale=1.0 / TAU).then_inc(ef_done, 1)
                nc.scalar.activation(fb, cb, ACT.Exp, scale=-1.0 / TAU).then_inc(ef_done, 1)
                split_hi(U_GV + 2 * h)
                split_hi(U_GV + 2 * h + 1)
            act.wait_ge(dec_done, GH)
            n = 0
            for c in range(4):
                for t in ([MT] if c < 2 else []) + list(range(TILES)):
                    n += 1
                    act.wait_ge(gv_full, n)
                    src = bank[:, 6 + n % 2, :]
                    if c < 2:
                        dst = vm[:, 512 * c:512 * c + 512] if t == MT else gv[:, t, 512 * c:512 * c + 512]
                        nc.scalar.activation(dst, src[:rows(t), :], ACT.Copy).then_inc(gv_out, 1)
                    else:
                        m = n - 11
                        if m >= 4:
                            act.wait_ge(r_stored[m % 4], 16)
                        nc.scalar.activation(r_piece(m), src, ACT.Silu).then_inc(gv_out, 1)
                        if m:
                            store_r(m - 1)
                if c < 3:
                    for u in range(U_GR + 4 * c, U_GR + 4 * c + 4):
                        split_hi(u)
            store_r(7)
            for u in range(U_GO + 4, U_GO + 8):
                split_hi(u)
            act.wait_ge(kt_full, 1)
            nc.scalar.activation(rbuf[0:META, 0:GH * P], bank[0:META, 0, :], ACT.Copy).then_inc(ktok_done, 1)

            def k_tokens(m):
                act.wait_ge(kt_full, m + 2)
                if m:
                    act.wait_ge(ua_full, m)
                    ub_wait(act, m - 1)
                act.wait_ge(at_done, m + 1)
                nc.scalar.activation(ktok, bank[:, 0, P:2 * P], ACT.Copy).then_inc(ktok_done, 1)

            def g_copy(what, t):
                m = gtp_at[(what, t)]
                act.wait_ge(gtp_full, m + 1)
                if what == "o":
                    nc.scalar.activation(xT_hi[:, :, cols(t)], ps_t[:, :, :], ACT.Copy).then_inc(gtp_hi, 1)
                else:
                    nc.scalar.activation(gv[:, t, :].rearrange("p (k n) -> p k n", k=KD), ps_t[:, :, :],
                                         ACT.Copy).then_inc(gtp_hi, 1)

            def store_h3(t):
                act.wait_ge(h3_ready, t + 1)
                act.dma_start(h3_d[cols(t), :], zrow[:, t % 2, :]).then_inc(h3_stored[t % 2], 16)

            k_tokens(0)
            for m in range(GM):
                t, h = divmod(m, GH)
                if m + 1 < GM:
                    k_tokens(m + 1)
                if h == 0 and t:
                    rsqrt(ssq[:, 1, :], ssq[:, 2, :])
                act.wait_ge(go_full, m + 1)
                o = o_at(t)[:, h * DV:(h + 1) * DV]
                nc.scalar.activation(o, bank[:, 4, 0:DV], ACT.Copy).then_inc(o_copied, 1)
                act.wait_ge(o_copied, m + 1)
                nc.scalar.activation(junk, o, ACT.Square, accum_out=ssq[:, 0, h:h + 1]).then_inc(sq_done, 1)
                act.wait_ge(sq_done, m + 1)
                if h == 1 and t:
                    g_copy("o", t - 1)
                    if t >= 2:
                        rsqrt(ln_st[:, 13:14], ln_st[:, 14:15])
                if h == 2 and t >= 2:
                    store_h3(t - 2)
                if h == 3 and t >= 2:
                    g_copy("h", t - 2)
            rsqrt(ssq[:, 1, :], ssq[:, 2, :])
            g_copy("o", TILES - 1)
            rsqrt(ln_st[:, 13:14], ln_st[:, 14:15])
            store_h3(TILES - 2)
            for u in range(U_MOE1, U_MOE1 + RING):
                split_hi(u)
            g_copy("h", TILES - 2)
            rsqrt(ln_st[:, 13:14], ln_st[:, 14:15])
            store_h3(TILES - 1)
            g_copy("h", TILES - 1)
            for b in range(2):
                act.wait_ge(h3_stored[b], 16 * (TILES // 2))
            moe_act(1, U_MOE1)
            for b in range(2):
                act.wait_ge(h2_stored[b][1], 16 * (TILES // 2))

        @block.vector
        def _(dve):
            count, norms = [0], [0]

            def mark(ins):
                count[0] += 1
                return ins.then_inc(dve_order, 1)

            def settle():
                dve.wait_ge(dve_order, count[0])

            def split_lo(u):
                dve.wait_ge(hi_done, u + 1)
                nc.vector.tensor_tensor(split_unit(w_lo, u), raw_unit(u), split_unit(w_hi, u).bitcast(F32),
                                        ALU.subtract).then_inc(lo_done, 1)

            def x_lo(i):
                c, R = cols(order[i]), rows(order[i])
                dve.wait_ge(tp_hi, i + 1)
                nc.vector.tensor_tensor(xT_lo[:, :, c], ps_t[:, :, 0:R], xT_hi[:, :, c].bitcast(F32),
                                        ALU.subtract).then_inc(tp_lo, 1)

            nc.vector.memset(xT_hi[:, :, L:XW].bitcast(F32), 0.0)
            nc.vector.memset(xT_lo[:, :, L:XW].bitcast(F32), 0.0)
            nc.vector.memset(kside[:], 0.0)
            nc.vector.memset(vside[:], 0.0)
            mark(nc.vector.memset(tpose[:], 0.0))
            settle()
            nc.vector.memset(sm_st[:], 0.0).then_inc(zero_done, 1)
            u = 0
            for i in range(len(order)):
                x_lo(i)
                if i >= 1:
                    split_lo(u)
                    u += 1
            while u < RING:
                split_lo(u)
                u += 1
            dve.wait_ge(cst, 12 + 3 * TILES)
            for t in range(TILES):
                nc.vector.memset(dist[:, t, P + META:P + CHUNK], BIG)
                d = dist[:, t, 0:P + META]
                mark(nc.vector.scalar_tensor_tensor(out=d, in0=d, scalar=-1.0, in1=d, op0=ALU.mult, op1=ALU.max))
            settle()
            for t in range(TILES):
                nc.vector.memset(dist[0:CHUNK, t, CHUNK:P], BIG)
                nc.vector.memset(dist[CHUNK:P, t, P + CHUNK:2 * P], BIG)
                if t == 0:
                    nc.vector.memset(dist[0:CHUNK, t, P + CHUNK:2 * P], BIG)
            mark(nc.vector.memset(ln_st[:], 1.0))
            settle()
            while u < 18:
                split_lo(u)
                u += 1
            dve.wait_ge(q_out, 10)
            for t in range(TILES):
                nc.vector.tensor_copy(kside[:, t, :, 0:META], kT[:, :, SEQ:L])
                if t:
                    nc.vector.tensor_copy(kside[:, t, :, CHUNK:P], kT[:, :, t * P - CHUNK:t * P])
            for i in range(len(order)):
                t = order[i]
                R = rows(t)
                dve.wait_ge(kv_full, i + 1)
                v = bank[:R, 4 + i % 2, 0:256]
                last = nc.vector.tensor_copy(v_sb[:R, t, :], v)
                if t == MT:
                    for s in range(TILES):
                        last = nc.vector.tensor_copy(vside[0:META, s, :], v)
                elif t + 1 < TILES:
                    last = nc.vector.tensor_copy(vside[CHUNK:P, t + 1, :], bank[CHUNK:P, 4 + i % 2, 0:256])
                last.then_inc(v_out, 1)
            dve.wait_ge(v_out, len(order))
            nc.vector.memset(sm_st[:], 0.0).then_inc(side_done, 1)
            dve.wait_ge(prm[0], 16)

            def front(n):
                i, t, g = steps[n]
                R, W, b = rows(t), width(t), n % 2
                st = sm_st[:R, b, :]
                dve.wait_ge(s_full, n + 1)
                if n >= 2:
                    dve.wait_ge(tp_full, tp_at[("p", n - 2)] + 1)
                dt = t if t != MT else 0
                for j in range(GQ):
                    slope = 2.0 ** (-8.0 * (GQ * g + j + 1) / NH)
                    last = nc.vector.scalar_tensor_tensor(out=prob[:R, b, j, 0:W], in0=dist[:R, dt, 0:W],
                                                          scalar=-slope, in1=ps_s[:R, j, 0:W], op0=ALU.mult,
                                                          op1=ALU.add)
                last.then_inc(s_read, 1)
                dve.wait_ge(s_read, n + 1)
                mark(nc.vector.tensor_reduce(st[:, 0:4], prob[:R, b, :, 0:W], X, ALU.max))
                settle()
                mark(nc.vector.tensor_tensor(st[:, 4:8], st[:, 0:4], sink_b[:R, GQ * g:GQ * g + GQ], ALU.max))
                settle()
                nc.vector.tensor_scalar(st[:, 8:12], st[:, 4:8], -1.0, None, ALU.mult)
                nc.vector.tensor_tensor(st[:, 12:16], sink_b[:R, GQ * g:GQ * g + GQ], st[:, 4:8],
                                        ALU.subtract).then_inc(front_done, 1)

            def back(n):
                i, t, g = steps[n]
                R, W, b = rows(t), width(t), n % 2
                st = sm_st[:R, b, :]
                dve.wait_ge(exp_done, n + 1)
                mark(nc.vector.tensor_tensor(st[:, 0:4], st[:, 16:20], st[:, 12:16], ALU.add))
                settle()
                mark(nc.vector.reciprocal(st[:, 4:8], st[:, 0:4]))
                settle()
                for j in range(GQ):
                    last = nc.vector.tensor_scalar(prob[:R, b, j, 0:W], prob[:R, b, j, 0:W], st[:, 4 + j:5 + j],
                                                   None, ALU.mult)
                last.then_inc(p_ready, 1)

            def o_split(n):
                i, t, g = steps[n]
                c = cols(t)
                dve.wait_ge(o_hi, n + 1)
                nc.vector.tensor_tensor(xT_lo[:, 2 * g:2 * g + 2, c], ps_o[:, :, 0:rows(t)],
                                        xT_hi[:, 2 * g:2 * g + 2, c].bitcast(F32), ALU.subtract).then_inc(o_lo, 1)

            def refine(v, r, t):
                norms[0] += 1
                dve.wait_ge(rstd_ready, norms[0])
                mark(nc.vector.scalar_tensor_tensor(out=t, in0=r, scalar=r, in1=v, op0=ALU.mult, op1=ALU.mult))
                settle()
                mark(nc.vector.tensor_scalar(t, t, -0.5, 1.5, ALU.mult, ALU.add))
                settle()
                mark(nc.vector.tensor_tensor(r, r, t, ALU.mult))
                settle()

            def refine4(v, r, t):
                norms[0] += 1
                dve.wait_ge(rstd_ready, norms[0])
                mark(nc.vector.tensor_tensor(t, r, r, ALU.mult))
                settle()
                mark(nc.vector.tensor_tensor(t, t, v, ALU.mult))
                settle()
                mark(nc.vector.tensor_scalar(t, t, -0.5, 1.5, ALU.mult, ALU.add))
                settle()
                mark(nc.vector.tensor_tensor(r, r, t, ALU.mult))
                settle()

            def norm(z, R, y, residual, ready):
                residual(nc.vector.scalar_tensor_tensor(out=z, in0=z, scalar=ALPHA, in1=y, op0=ALU.mult, op1=ALU.add))
                st = ln_st[:R, :]
                for c in range(2):
                    last = nc.vector.bn_stats(st[:, 6 * c:6 * c + 6], z[:, c * 512:(c + 1) * 512])
                mark(last)
                settle()
                mark(nc.vector.bn_aggr(st[:, 12:14], st[:, 0:12]))
                settle()
                nc.vector.tensor_scalar(st[:, 13:14], st[:, 13:14], LN_EPS, None, ALU.add).then_inc(var_ready, 1)
                refine(st[:, 13:14], st[:, 14:15], st[:, 15:16])
                mark(nc.vector.tensor_scalar(z, z, st[:, 12:13], st[:, 14:15], ALU.subtract, ALU.mult))
                settle()
                mark(nc.vector.tensor_tensor(z, z, gb[:R, 0, :], ALU.mult))
                settle()
                ready(nc.vector.tensor_tensor(z, z, gb[:R, 1, :], ALU.add))

            def norm_attn(i):
                t = order[i]
                R = rows(t)
                dve.wait_ge(x_landed[i % 2], x_count(i, True))
                if i < len(order) - 1:
                    dve.wait_ge(y_full, i + 1)
                else:
                    dve.wait_ge(ao_used, KD)

                def read(ins):
                    ins.then_inc(y_read, 1)
                    dve.wait_ge(y_read, i + 1)

                norm(zrow[:R, i % 2, :], R, ps_y[:R, :, :].rearrange("p b n -> p (b n)"), read,
                     lambda ins: ins.then_inc(h_ready, 1))

            front(0)
            front(1)
            dve.wait_ge(prm[2], 32)
            for n in range(NS):
                back(n)
                if n >= 1:
                    o_split(n - 1)
                if n < 2:
                    split_lo(18 + n)
                if n + 2 < NS:
                    front(n + 2)
                if n % NKV == 3 and n >= 7:
                    norm_attn(n // NKV - 1)
            o_split(NS - 1)
            for u in range(U_MOE0, U_MOE0 + RING):
                split_lo(u)
            norm_attn(len(order) - 1)

            def lo_ahead(u0, b, c, j):
                r = RING + 6 * c + j
                s = (u0 + r) % RING
                dve.wait_ge(hi_done, u0 + r + 1 + 6 * (b - c))
                nc.vector.tensor_tensor(w_lo[:, s, :], w_raw[:, s, :], w_hi[:, s, :].bitcast(F32),
                                        ALU.subtract).then_inc(lo_done, 1)

            def first_max(v, m, c, oh):
                shape = list(v.shape)
                mark(nc.vector.tensor_reduce(m, v, X, ALU.max))
                settle()
                mark(nc.vector.tensor_tensor(c, v, m.to_broadcast(shape), ALU.is_equal))
                settle()
                mark(nc.vector.tensor_tensor(c, c, rev4[:].unsqueeze(1).to_broadcast(shape), ALU.mult))
                settle()
                mark(nc.vector.tensor_reduce(rt_m[:, 0:shape[1], :], c, X, ALU.max))
                settle()
                mark(nc.vector.tensor_tensor(oh, c, rt_m[:, 0:shape[1], :].to_broadcast(shape), ALU.is_equal))
                settle()

            def moe_dve(l, u0, logits):
                T = moe_tiles(l)
                NT = len(T)
                w = slice(0, NT)
                lg = rt_lg[:, w, :]
                mark(nc.vector.tensor_tensor(lg, logits,
                                             b_rt[:, l, :].unsqueeze(1).to_broadcast([P, NT, 20]), ALU.add))
                settle()
                first_max(lg[:, :, 0:NG], rt_g[:, w, :], rt_c[:, w, :], rt_ohg[:, w, :])
                nc.vector.tensor_tensor(rt_dg[:, w, :], lg[:, :, 0:NG], rt_g[:, w, :].to_broadcast([P, NT, NG]),
                                        ALU.subtract).then_inc(exp_asked[l], 1)
                mark(nc.vector.tensor_tensor(rt_pr[:, w], lg[:, :, NG:].rearrange("p t (g e) -> p t g e", g=NG),
                                             rt_ohg[:, w, :].unsqueeze(3).to_broadcast([P, NT, NG, EPG]), ALU.mult))
                settle()
                mark(nc.vector.tensor_reduce(rt_z[:, w, :], rt_pr[:, w].rearrange("p t g e -> p t e g"), X, ALU.add))
                settle()
                first_max(rt_z[:, w, :], rt_m1[:, w, :], rt_c[:, w, :], rt_oh[0][:, w, :])
                mark(nc.vector.scalar_tensor_tensor(out=rt_a[:, w, :], in0=rt_oh[0][:, w, :], scalar=-3e38,
                                                    in1=rt_z[:, w, :], op0=ALU.mult, op1=ALU.add))
                settle()
                first_max(rt_a[:, w, :], rt_m2[:, w, :], rt_c[:, w, :], rt_oh[1][:, w, :])
                nc.vector.tensor_tensor(rt_dm[:, w, :], rt_m2[:, w, :], rt_m1[:, w, :],
                                        ALU.subtract).then_inc(exp_asked[l], 1)
                for k in range(2):
                    last = nc.vector.tensor_tensor(rt_M[k][:, w, :].rearrange("p t (g e) -> p t g e", g=NG),
                                                   rt_ohg[:, w, :].unsqueeze(3).to_broadcast([P, NT, NG, EPG]),
                                                   rt_oh[k][:, w, :].unsqueeze(2).to_broadcast([P, NT, NG, EPG]),
                                                   ALU.mult)
                mark(last)
                settle()
                nc.vector.tensor_tensor(rt_Mb[:, w, :], rt_M[0][:, w, :], rt_M[1][:, w, :],
                                        ALU.add).then_inc(chosen[l], 1)
                dve.wait_ge(exp_given[l], 2)
                mark(nc.vector.tensor_reduce(rt_gt[:, w, :], rt_dg[:, w, :], X, ALU.add))
                mark(nc.vector.tensor_scalar(rt_m[:, w, :], rt_dm[:, w, :], 1.0, None, ALU.add))
                settle()
                mark(nc.vector.tensor_tensor(rt_gt[:, w, :], rt_gt[:, w, :], rt_m[:, w, :], ALU.mult))
                settle()
                mark(nc.vector.reciprocal(wgt[:, w, 0:1], rt_gt[:, w, :]))
                settle()
                mark(nc.vector.tensor_tensor(wgt[:, w, 1:2], wgt[:, w, 0:1], rt_dm[:, w, :], ALU.mult))
                if l == 0:
                    mark(nc.vector.memset(xg[:], 0.0))
                dve.wait_ge(rank_full[l], 1)
                mark(nc.vector.tensor_copy(rt_rank[:, w, :], ps_rank[:, w, :]))
                settle()
                mark(nc.vector.tensor_reduce(rt_p[:, 0, 0:1], ps_rank[:, NT, :], X, ALU.max))
                settle()
                for j in range(1, ROUNDS):
                    mark(nc.vector.tensor_scalar(rt_dg[:, 0, j - 1:j], rt_p[:, 0, 0:1], float(P * j), None, ALU.is_gt))
                settle()
                mark(nc.vector.tensor_reduce(rt_p[:, 0, 1:2], rt_dg[:, 0, 0:ROUNDS - 1], X, ALU.add))
                settle()
                mark(nc.vector.tensor_copy(rounds[:], rt_p[:, 0, 1:2]))
                mark(nc.vector.scalar_tensor_tensor(out=rt_rm[:, w, :], in0=rt_rank[:, w, :], scalar=1.0,
                                                    in1=rt_Mb[:, w, :], op0=ALU.add, op1=ALU.mult))
                settle()
                mark(nc.vector.tensor_scalar(rt_rm[:, w, :], rt_rm[:, w, :], -1.0, None, ALU.add))
                settle()
                mark(nc.vector.tensor_scalar(ids[:, w, :, 2], rt_M[1][:, w, :], float(L), None, ALU.mult))
                for n in range(NT):
                    for e in range(NE):
                        last = nc.vector.tensor_scalar(hot[:, n, e, :], slot_id[:], rt_rm[:, n, e:e + 1], None,
                                                       ALU.is_equal)
                    last.then_inc(hot_ready[l], 1)
                dve.wait_ge(tab_full[l], 1)
                tab = rt_q[:, 0:3, :].rearrange("p t (e c) -> p (t e c)", c=1).rearrange("p (e c) -> p e c", c=3)
                mark(nc.vector.tensor_copy(tab, ps_tab))
                settle()
                mark(nc.vector.tensor_tensor(tab[:, :, 1:2], tab[:, :, 0:1], tab[:, :, 1:2], ALU.add))
                settle()
                mark(nc.vector.tensor_scalar(idx[:, 0, :].unsqueeze(2), tab[:, :, 1:2], -1.0, None, ALU.add))
                nc.vector.scalar_tensor_tensor(out=idx[:, 1, :].unsqueeze(2), in0=tab[:, :, 1:2], scalar=-1.0,
                                               in1=tab[:, :, 2:3], op0=ALU.add, op1=ALU.add).then_inc(idx_ready[l], 1)

                def x_low(b):
                    c = slice((b % 2) * P, (b % 2) * P + P)
                    dve.wait_ge(x_hi_done, NE * l + b + 1)
                    nc.vector.tensor_tensor(xT_lo[:, :, c], ps_t[:, :, :], xT_hi[:, :, c].bitcast(F32),
                                            ALU.subtract).then_inc(x_lo_done, 1)

                x_low(0)
                for b in range(NE):
                    dve.wait_ge(silu_done, NE * l + b + 1)
                    if b >= 2:
                        dve.wait_ge(ht_full, NE * l + b - 1)
                    nc.vector.tensor_tensor(hid[:, b % 2, :], sil[:, b % 2, :], ps_gu[:, FE:2 * FE],
                                            ALU.mult).then_inc(mul_done, 1)
                    if b + 1 < NE:
                        x_low(b + 1)
                    js = [j for j in range(6) if l == 0 or 8 + 6 * b + j < 6 * NE]
                    if b == NE - 1:
                        js = [j for j in js if j < 4]
                    for j in js[0:4]:
                        lo_ahead(u0, b, b % 4, j)
                    dve.wait_ge(h_hi_done, NE * l + b + 1)
                    c = slice((2 + b % 2) * P, (3 + b % 2) * P)
                    nc.vector.tensor_tensor(xT_lo[:, 0:KF, c], ps_h[:, :, :], xT_hi[:, 0:KF, c].bitcast(F32),
                                            ALU.subtract).then_inc(h_lo_done, 1)
                    for j in js[4:6]:
                        lo_ahead(u0, b, b % 4, j)

                def more(r, e):
                    q = e + NE * (r - 1)
                    n_d = [0]

                    def own(ins):
                        n_d[0] += 1
                        return ins.then_inc(ov_dve[l], 1)

                    def own_done():
                        dve.wait_ge(ov_dve[l], 9 * q + n_d[0])

                    own(nc.vector.tensor_copy(ov_rm[:, 0:NT].unsqueeze(2), rt_rm[:, w, bass.ds(e, 1)]))
                    own(nc.vector.tensor_copy(ov_ids[:, 0:NT, :].unsqueeze(2), ids[:, w, bass.ds(e, 1), :]))
                    own_done()
                    own(nc.vector.tensor_scalar(ov_rm[:, 0:NT], ov_rm[:, 0:NT], float(P * r), None, ALU.subtract))
                    own_done()
                    for n in range(NT):
                        last = nc.vector.tensor_scalar(ov_hot[:, n, :], slot_id[:], ov_rm[:, n:n + 1], None,
                                                       ALU.is_equal)
                    own(last)
                    dve.wait_ge(ov_pe[l], 5 * q + 1)
                    own(nc.vector.tensor_copy(ov_tab[:, 0:3], bank[:, 4, 256:259]))
                    own_done()
                    own(nc.vector.tensor_tensor(ov_tab[:, 1:2], ov_tab[:, 0:1], ov_tab[:, 1:2], ALU.add))
                    own_done()
                    own(nc.vector.tensor_scalar(ov_idx[:, 0:1], ov_tab[:, 1:2], -1.0, None, ALU.add))
                    own(nc.vector.scalar_tensor_tensor(out=ov_idx[:, 1:2], in0=ov_tab[:, 1:2], scalar=-1.0,
                                                       in1=ov_tab[:, 2:3], op0=ALU.add, op1=ALU.add))
                    dve.wait_ge(ov_act[l], 4 * q + 2)
                    own(nc.vector.tensor_tensor(hid[:, 0, :], sil[:, 0, :], ps_gu[:, FE:2 * FE], ALU.mult))
                    dve.wait_ge(ov_s[l], 16 * q + 16)

                further(dve, l, more)
                dve.wait_ge(gb_landed[l], 32)
                for n, t in enumerate(T):
                    R = rows(t)
                    z, y = zrow[:R, n % 2, :], ycomb[:R, n % 2]
                    dve.wait_ge(comb_landed[n % 2][l], 48 * (n // 2 + 1))
                    mark(nc.vector.tensor_scalar(y[:, 0, :], y[:, 0, :], wgt[:R, n, 0:1], None, ALU.mult))
                    settle()
                    mark(nc.vector.scalar_tensor_tensor(out=y[:, 0, :], in0=y[:, 1, :], scalar=wgt[:R, n, 1:2],
                                                        in1=y[:, 0, :], op0=ALU.mult, op1=ALU.add))
                    settle()

                    def read(ins):
                        mark(ins)
                        settle()

                    norm(z, R, y[:, 0, :], read, lambda ins: ins.then_inc(h2_ready[l], 1))
                    if l == 0:
                        dve.wait_ge(h2_hi, n + 1)
                        nc.vector.tensor_tensor(xT_lo[:, :, cols(t)], ps_t[:, :, 0:R], xT_hi[:, :, cols(t)].bitcast(F32),
                                                ALU.subtract).then_inc(h2_lo, 1)

            dve.wait_ge(rt_full, len(order))
            moe_dve(0, U_MOE0, ps_r[:, 0:RTW * 20].rearrange("p (t e) -> p t e", e=20))

            mark(nc.vector.memset(scan0, 1.0))
            settle()
            mark(nc.vector.memset(scan0[:, 0:L:CHUNK], 0.0))
            settle()
            for u in (U_GL + 6, U_GL + 7, U_GL + 8):
                split_lo(u)
            dve.wait_ge(gprm, 32)
            for h in range(GH):
                dve.wait_ge(abs_done, 2 * h + 1)
                nc.vector.tensor_scalar(lm.rearrange("p (h n) -> p h n", h=2), bank[:, 0:2, 0:HALF], bg[:, h:h + 1],
                                        0.0, ALU.add, ALU.min).then_inc(lm_done, 1)
                dve.wait_ge(lm_done, h + 1)
                dve.wait_ge(ln_done, h + 1)
                mark(nc.vector.tensor_tensor(lm, lm, la, ALU.subtract))
                settle()
                if h:
                    dve.wait_ge(ef_done, 2 * h)
                nc.vector.tensor_tensor_scan(cb, scan0, lm, 0.0, ALU.mult, ALU.add).then_inc(cum_done, 1)
                dve.wait_ge(qk_full, 2 * h + 1)
                dve.wait_ge(ef_done, 2 * h + 1)
                for c in range(2):
                    s = slice(c * HALF, (c + 1) * HALF)
                    last = nc.vector.scalar_tensor_tensor(out=qdec[:, h, s], in0=bank[:, 2 + c, 0:HALF],
                                                          scalar=DK ** -0.5, in1=eb[:, s], op0=ALU.mult, op1=ALU.mult)
                last.then_inc(qd_done, 1)
                dve.wait_ge(qk_full, 2 * h + 2)
                dve.wait_ge(ef_done, 2 * h + 2)
                for c in range(2):
                    s = slice(c * HALF, (c + 1) * HALF)
                    nc.vector.tensor_tensor(kinv[:, h, s], bank[:, 4 + c, 0:HALF], fb[:, s], ALU.mult)
                nc.vector.tensor_copy(dec[:, h, 0:GCH], eb[:, CHUNK - 1:SEQ:CHUNK])
                nc.vector.tensor_copy(dec[:, h, GCH:], eb[:, L - 1:L]).then_inc(dec_done, 1)
                split_lo(U_GV + 2 * h)
                split_lo(U_GV + 2 * h + 1)
            nc.vector.memset(at_sb, 0.0)
            dve.wait_ge(gb_ng, 16)
            for c in range(4):
                if c >= 2:
                    for m in range(4 * c - 8, 4 * c - 4):
                        dve.wait_ge(gv_out, 11 + m)
                        nc.vector.tensor_tensor(r_piece(m), r_piece(m), gb[:, 0, 512 * (m // 4):512 * (m // 4) + 512],
                                                ALU.mult).then_inc(r_ready, 1)
                for u in range(U_GR + 4 * c, U_GR + 4 * c + 4):
                    split_lo(u)

            def keys_to_end(m):
                t, h = divmod(m, GH)
                if m:
                    dve.wait_ge(kt_full, m + 1)
                nc.vector.tensor_tensor(kend.rearrange("p (c n) -> p c n", c=2),
                                        kinv[:, h, cols(t)].rearrange("p (c n) -> p c n", c=2),
                                        dec[:, h, 2 * t:2 * t + 2].unsqueeze(2).to_broadcast([P, 2, CHUNK]),
                                        ALU.mult).then_inc(kend_done, 1)

            def causal_scores(m):
                dve.wait_ge(kt_full, m + 2)
                if m >= 2:
                    dve.wait_ge(go_full, m - 1)
                nc.vector.copy_predicated(at_sb[:, m % 2, :], causal[:].bitcast(mybir.dt.uint16), bank[:, 0, 0:P]
                                          ).then_inc(at_done, 1)

            dve.wait_ge(dec_done, GH)
            keys_to_end(0)
            for h in range(GH):
                dve.wait_ge(um_full, h + 1)
                nc.vector.tensor_scalar(state[:, h, :], bank[:, (1, 5)[h % 2], 0:DV], dec[:, h, GCH:], None,
                                        ALU.mult).then_inc(sb_done, 1)
            causal_scores(0)

            def g_var():
                nc.vector.tensor_scalar(ssq[:, 1, :], ssq[:, 0, :], 1.0 / DV, RMS_EPS, ALU.mult,
                                        ALU.add).then_inc(var_ready, 1)

            def g_gate(t):
                refine4(ssq[:, 1, :], ssq[:, 2, :], ln_st[:, 16:20])
                dve.wait_ge(r_landed, 16 * (t + 1))
                for h in range(GH):
                    o, s = o_at(t)[:, h * DV:(h + 1) * DV], slice(h * DV, (h + 1) * DV)
                    last = nc.vector.scalar_tensor_tensor(out=o, in0=o, scalar=ssq[:, 2, h:h + 1], in1=rbuf[:, s],
                                                          op0=ALU.mult, op1=ALU.mult)
                last.then_inc(gated, 1)

            def g_low(t):
                dve.wait_ge(gtp_hi, gtp_at[("o", t)] + 1)
                nc.vector.tensor_tensor(xT_lo[:, :, cols(t)], ps_t[:, :, :], xT_hi[:, :, cols(t)].bitcast(F32),
                                        ALU.subtract).then_inc(gtp_lo, 1)

            def norm_gla(t):
                dve.wait_ge(z_landed[t % 2], 16 * (t // 2 + 1))
                if t < TILES - 1:
                    dve.wait_ge(gy_full, t + 1)
                else:
                    dve.wait_ge(go_used, KD)

                def read(ins):
                    ins.then_inc(gy_read, 1)
                    dve.wait_ge(gy_read, t + 1)

                norm(zrow[:, t % 2, :], P, ps_y[:, :, :].rearrange("p b n -> p (b n)"), read,
                     lambda ins: ins.then_inc(h3_ready, 1))

            def g_logits(t):
                dve.wait_ge(lg_full, t + 1)
                nc.vector.tensor_copy(lg_sb[:, t, :], bank[:, 2, 0:NG + NE]).then_inc(lg_read, 1)

            for m in range(GM):
                t, h = divmod(m, GH)
                if h == 0 and t:
                    dve.wait_ge(sq_done, m)
                    g_var()
                if m + 1 < GM:
                    keys_to_end(m + 1)
                S = state[:, h, :]
                dve.wait_ge(o_part, m + 1)
                dve.wait_ge(ua_full, m + 1)
                nc.vector.scalar_tensor_tensor(out=S, in0=S, scalar=dec[:, h, 2 * t:2 * t + 1], in1=bank[:, 1, 0:DV],
                                               op0=ALU.mult, op1=ALU.add).then_inc(sa_done, 1)
                if m + 1 < GM:
                    causal_scores(m + 1)
                if t < TILES - 1:
                    ub_wait(dve, m)
                    dve.wait_ge(go_full, m + 1)
                    nc.vector.scalar_tensor_tensor(out=S, in0=S, scalar=dec[:, h, 2 * t + 1:2 * t + 2],
                                                   in1=bank[:, 5, 0:DV], op0=ALU.mult, op1=ALU.add
                                                   ).then_inc(sb_done, 1)
                if h == 0 and t:
                    g_gate(t - 1)
                    if t == 1:
                        dve.wait_ge(gb_l3, 32)
                    if t == 3:
                        g_logits(0)
                if h == 1 and t:
                    g_low(t - 1)
                    if t >= 2:
                        norm_gla(t - 2)
            dve.wait_ge(sq_done, GM)
            g_var()
            g_gate(TILES - 1)
            g_logits(1)
            g_low(TILES - 1)
            norm_gla(TILES - 2)
            for u in range(U_MOE1, U_MOE1 + RING):
                split_lo(u)
            norm_gla(TILES - 1)
            for t in (TILES - 2, TILES - 1):
                g_logits(t)
            dve.wait_ge(lg_read, TILES)
            moe_dve(1, U_MOE1, lg_sb[:, 0:TILES, :])

        @block.tensor
        def _(pe):
            def tp_free(m):
                if m:
                    pe.wait_ge(tp_hi, m)
                if 0 < m <= len(order):
                    pe.wait_ge(tp_lo, m)

            pe.wait_ge(cst, 5)
            for i in range(len(order)):
                t = order[i]
                R = rows(t)
                pe.wait_ge(x_landed[i % 2], x_count(i, False))
                tp_free(i)
                for k in range(KD):
                    last = nc.tensor.transpose(ps_t[:, k, 0:R], zrow[:R, i % 2, k * P:(k + 1) * P], ident[:R, :R])
                last.then_inc(tp_full, 1)
            pe.wait_ge(tp_lo, len(order))

            def three(acc, a_hi, a_lo, b_hi, b_lo, first, last):
                nc.tensor.matmul(acc, a_hi, b_hi, start=first, stop=False)
                nc.tensor.matmul(acc, a_lo, b_hi, start=False, stop=False)
                return nc.tensor.matmul(acc, a_hi, b_lo, start=False, stop=last)

            for f in range(10):
                if f < 8:
                    ua = 2 * (f // 2)
                    pe.wait_ge(lo_done, ua + 2)

                    def stat(w, k):
                        return w[:, ua % RING + f % 2, k * P:(k + 1) * P]
                else:
                    ua = U_K + f - 8
                    pe.wait_ge(lo_done, ua + 1)

                    def stat(w, k):
                        return w[:, ua % RING, k * P:(k + 1) * P]
                if f >= 2:
                    pe.wait_ge(q_out, f - 1)
                for h in range(2):
                    for k in range(KD):
                        c = slice(h * HALF, (h + 1) * HALF)
                        last = three(ps_q[f % 2][:, h, 0:HALF], stat(w_hi, k), stat(w_lo, k), xT_hi[:, k, c],
                                     xT_lo[:, k, c], k == 0, k == KD - 1)
                last.then_inc(q_full, 1)
            pe.wait_ge(lo_done, U_V + 2)
            for i in range(len(order)):
                t = order[i]
                if i >= 2:
                    pe.wait_ge(v_out, i - 1)
                for k in range(KD):
                    s = (U_V + k // 4) % RING
                    c = slice(t * P, t * P + P)
                    w = slice(256 * (k % 4), 256 * (k % 4) + 256)
                    last = three(bank[:, 4 + i % 2, 0:256], xT_hi[:, k, c], xT_lo[:, k, c], w_hi[:, s, w],
                                 w_lo[:, s, w], k == 0, k == KD - 1)
                last.then_inc(kv_full, 1)

            def scores(n):
                i, t, g = steps[n]
                R = rows(t)
                if n:
                    pe.wait_ge(s_read, n)
                for j in range(GQ):
                    h = GQ * g + j
                    f, base = 4 * (g // 2) + j, 64 * (g % 2)
                    q = qT[base:base + HD, f, cols(t)]
                    last = nc.tensor.matmul(ps_s[:R, j, 0:R], q, kT[base:base + HD, g // 2, cols(t)],
                                            start=True, stop=True)
                    if t != MT:
                        last = nc.tensor.matmul(ps_s[:R, j, P:2 * P], q, kside[base:base + HD, t, g // 2, :],
                                                start=True, stop=True)
                last.then_inc(s_full, 1)

            def out_part(i, g):
                t = order[i]
                if g == 0 and i:
                    pe.wait_ge(y_read, i)
                pe.wait_ge(o_lo, NKV * i + g + 1)
                for k in (2 * g, 2 * g + 1):
                    pe.wait_ge(lo_done, U_AO + k + 1)
                    s = (U_AO + k) % RING
                    c = slice(t * P, t * P + P)
                    for h in range(2):
                        w = slice(512 * h, 512 * h + 512)
                        last = three(ps_y[:, h, :], xT_hi[:, k, c], xT_lo[:, k, c], w_hi[:, s, w], w_lo[:, s, w],
                                     k == 0, k == KD - 1)
                    if i == len(order) - 1:
                        last.then_inc(ao_used, 1)
                if g == NKV - 1 and i < len(order) - 1:
                    last.then_inc(y_full, 1)

            def p_transpose(n):
                i, t, g = steps[n]
                R = rows(t)
                pe.wait_ge(p_ready, n + 1)
                tp_free(tp_at[("p", n)])
                for j in range(GQ):
                    for b in range(blocks(t)):
                        w = min(P, width(t))
                        last = nc.tensor.transpose(ps_t[:w, 2 * j + b, 0:R], prob[:R, n % 2, j, P * b:P * b + w],
                                                   ident[:R, :R])
                last.then_inc(tp_full, 1)

            def values(n):
                i, t, g = steps[n]
                R = rows(t)
                m = tp_at[("p", n)]
                pe.wait_ge(tp_hi, m + 1)
                if n:
                    pe.wait_ge(o_lo, n)
                for j in range(GQ):
                    base = 64 * (j % 2)
                    o = ps_o[base:base + HD, j // 2, 0:R]
                    K = META if t == MT else P
                    last = nc.tensor.matmul(o, v_sb[:K, t, g * HD:(g + 1) * HD], tpose[:K, 2 * j, 0:R],
                                            start=True, stop=(t == MT))
                    if t != MT:
                        last = nc.tensor.matmul(o, vside[:, t, g * HD:(g + 1) * HD], tpose[:, 2 * j + 1, 0:R],
                                                start=False, stop=True)
                last.then_inc(o_full, 1)

            def h_transpose(j):
                R = rows(order[j])
                pe.wait_ge(h_ready, j + 1)
                tp_free(tp_at[("h", j)])
                for k in range(KD):
                    last = nc.tensor.transpose(ps_t[:, k, 0:R], zrow[:R, j % 2, k * P:(k + 1) * P], ident[:R, :R])
                last.then_inc(tp_full, 1)

            def route(j):
                pe.wait_ge(tp_hi, tp_at[("h", j)] + 1)
                t = order[j]
                for k in range(KD):
                    last = nc.tensor.matmul(ps_r[:, t * 20:t * 20 + 20], tpose[:, k, :], w_rt[:, 0, k, :],
                                            start=(k == 0), stop=(k == KD - 1))
                last.then_inc(rt_full, 1)

            pe.wait_ge(side_done, 1)
            scores(0)
            scores(1)
            pe.wait_ge(prm[1], 16 * 14)
            for n in range(NS):
                i, t, g = steps[n]
                if n + 2 < NS:
                    scores(n + 2)
                p_transpose(n)
                if i:
                    out_part(i - 1, g)
                values(n)
                if n % NKV == 1 and n >= 9:
                    h_transpose(n // NKV - 2)
                    route(n // NKV - 2)
            for g in range(NKV):
                out_part(len(order) - 1, g)
            for j in (len(order) - 2, len(order) - 1):
                h_transpose(j)
                route(j)

            def moe_pe(l, u0):
                T = moe_tiles(l)
                NT = len(T)
                pe.wait_ge(chosen[l], 1)
                for n in range(NT):
                    for m in range(n + 1):
                        K = rows(T[m])
                        last = nc.tensor.matmul(ps_rank[:, n, :], (tri if m == n else ones)[:K, :], rt_Mb[:K, m, :],
                                                start=(m == 0), stop=(m == n))
                for m in range(NT):
                    K = rows(T[m])
                    last = nc.tensor.matmul(ps_rank[:, NT, :], ones[:K, :], rt_Mb[:K, m, :], start=(m == 0),
                                            stop=(m == NT - 1))
                last.then_inc(rank_full[l], 1)
                pe.wait_ge(hot_ready[l], NT)
                for e in range(NE):
                    for n in range(NT):
                        K = rows(T[n])
                        last = nc.tensor.matmul(ps_tab[:, e, :], hot[:K, n, e, :], ids[:K, n, e, :], start=(n == 0),
                                                stop=(n == NT - 1))
                last.then_inc(tab_full[l], 1)

                def x_turn(b):
                    pe.wait_ge(gathered[b % 2], 8 * NE * l + 16 * (b // 2 + 1))
                    if not (isinstance(b, int) and b == 0):
                        pe.wait_ge(x_lo_done, NE * l + b)
                    for k in range(KD):
                        last = nc.tensor.transpose(ps_t[:, k, :], xg[:, b % 2, k * P:(k + 1) * P], ident[:])
                    last.then_inc(xt_full, 1)

                def gate_up(b, r):
                    pe.wait_ge(x_lo_done, NE * l + b + 1)
                    if b:
                        pe.wait_ge(mul_done, NE * l + b)
                    c = slice((b % 2) * P, (b % 2) * P + P)
                    for j in range(4):
                        s = (u0 + r + j) % RING
                        pe.wait_ge(lo_done, u0 + r + j + 1)
                        for i in range(2):
                            k = 2 * j + i
                            w = slice(512 * i, 512 * i + 512)
                            last = three(ps_gu, xT_hi[:, k, c], xT_lo[:, k, c], w_hi[:, s, w], w_lo[:, s, w],
                                         k == 0, k == KD - 1)
                        last.then_inc(gu_used, 1)

                def h_turn(b):
                    pe.wait_ge(mul_done, NE * l + b + 1)
                    if b:
                        pe.wait_ge(h_lo_done, NE * l + b)
                    for f in range(KF):
                        last = nc.tensor.transpose(ps_h[:, f, :], hid[:, b % 2, f * P:(f + 1) * P], ident[:])
                    last.then_inc(ht_full, 1)

                def down(b, r):
                    pe.wait_ge(h_lo_done, NE * l + b + 1)
                    if b:
                        pe.wait_ge(y_out, NE * l + b)
                    c = slice((2 + b % 2) * P, (3 + b % 2) * P)
                    for f in range(KF):
                        s = (u0 + r + f) % RING
                        pe.wait_ge(lo_done, u0 + r + f + 1)
                        for h in range(2):
                            w = slice(512 * h, 512 * h + 512)
                            last = three(ps_y[:, h, :], xT_hi[:, f, c], xT_lo[:, f, c], w_hi[:, s, w], w_lo[:, s, w],
                                         f == 0, f == KF - 1)
                        last.then_inc(dn_used, 1)

                x_turn(0)
                gate_up(0, 0)
                for b in range(NE):
                    r = 4 if b == 0 else 8 + 6 * (b - 1)
                    if b + 1 < NE:
                        x_turn(b + 1)
                    if b:
                        down(b - 1, r)
                        r += 2
                    h_turn(b)
                    if b + 1 < NE:
                        gate_up(b + 1, r)
                down(NE - 1, 6 * NE - 2)

                def more(r, e):
                    q = e + NE * (r - 1)
                    pe.wait_ge(ov_dve[l], 9 * q + 4)
                    for n in range(NT):
                        K = rows(T[n])
                        last = nc.tensor.matmul(bank[:, 4, 256:259], ov_hot[:K, n, :], ov_ids[:K, n, :],
                                                start=(n == 0), stop=(n == NT - 1))
                    last.then_inc(ov_pe[l], 1)
                    pe.wait_ge(ov_g[l], 16 * q + 16)
                    for k in range(KD):
                        last = nc.tensor.transpose(ps_t[:, k, :], ov_y[:, k * P:(k + 1) * P], ident[:])
                    last.then_inc(ov_pe[l], 1)
                    pe.wait_ge(ov_act[l], 4 * q + 1)
                    pe.wait_ge(ov_w[l], 64 * q + 64)
                    for k in range(KD):
                        last = nc.tensor.matmul(ps_gu, ov_xT[:, k, :], ov_gu[:, k, :, :].rearrange("p m c -> p (m c)"),
                                                start=(k == 0), stop=(k == KD - 1))
                    last.then_inc(ov_pe[l], 1)
                    pe.wait_ge(ov_dve[l], 9 * q + 9)
                    for f in range(KF):
                        last = nc.tensor.transpose(ps_h[:, f, :], hid[:, 0, f * P:(f + 1) * P], ident[:])
                    last.then_inc(ov_pe[l], 1)
                    pe.wait_ge(ov_act[l], 4 * q + 3)
                    for f, dn in enumerate((ov_dn, ov_dn2)):
                        for h in range(2):
                            last = nc.tensor.matmul(ps_y[:, h, :], ov_hT[:, f, :], dn[:, 512 * h:512 * h + 512],
                                                    start=(f == 0), stop=(f == KF - 1))
                    last.then_inc(ov_pe[l], 1)

                further(pe, l, more)

            moe_pe(0, U_MOE0)
            for n, t in enumerate(moe_tiles(0)):
                R = rows(t)
                pe.wait_ge(h2_ready[0], n + 1)
                if n:
                    pe.wait_ge(h2_lo, n)
                for k in range(KD):
                    last = nc.tensor.transpose(ps_t[:, k, 0:R], zrow[:R, n % 2, k * P:(k + 1) * P], ident[:R, :R])
                last.then_inc(h2_tp, 1)

            pe.wait_ge(h2_lo, len(order))
            pe.wait_ge(lo_done, U_GL + 1)
            for h in range(2):
                for k in range(KD):
                    c, s = slice(h * HALF, (h + 1) * HALF), U_GL % RING
                    w = slice(k * P, (k + 1) * P)
                    last = three(ps_y[:, h, 0:HALF], w_hi[:, s, w], w_lo[:, s, w], xT_hi[:, k, c], xT_lo[:, k, c],
                                 k == 0, k == KD - 1)
            last.then_inc(glow_full, 1)
            pe.wait_ge(gprm, 32)
            pe.wait_ge(glow_out, 1)
            for h in range(GH):
                if h:
                    pe.wait_ge(lm_done, h)
                for c in range(2):
                    last = nc.tensor.matmul(bank[:, c, 0:HALF], gup[:, h * P:(h + 1) * P],
                                            gl_t[0:RANK, c * HALF:(c + 1) * HALF], start=True, stop=True)
                last.then_inc(gate_full, 1)
                for i in range(2):
                    u = U_GL + 1 + 2 * h + i
                    pe.wait_ge(lo_done, u + 1)
                    if h:
                        pe.wait_ge((qd_done, dec_done)[i], h)
                    for c in range(2):
                        for k in range(KD):
                            w = slice(k * P, (k + 1) * P)
                            n = slice(c * HALF, (c + 1) * HALF)
                            last = three(bank[:, 2 + 2 * i + c, 0:HALF], w_hi[:, u % RING, w], w_lo[:, u % RING, w],
                                         xT_hi[:, k, n], xT_lo[:, k, n], k == 0, k == KD - 1)
                    last.then_inc(qk_full, 1)
            n = 0
            for q in range(4):
                pe.wait_ge(lo_done, U_GV + 4 * q + 4)
                for t in ([MT] if q < 2 else []) + list(range(TILES)):
                    n += 1
                    if n > 2:
                        pe.wait_ge(gv_out, n - 2)
                    for k in range(KD):
                        s = (U_GV + 4 * q + k // 2) % RING
                        w = slice(512 * (k % 2), 512 * (k % 2) + 512)
                        c = slice(t * P, t * P + P)
                        last = three(bank[:, 6 + n % 2, :], xT_hi[:, k, c], xT_lo[:, k, c], w_hi[:, s, w],
                                     w_lo[:, s, w], k == 0, k == KD - 1)
                    last.then_inc(gv_full, 1)
            pe.wait_ge(dec_done, GH)
            for h in range(GH):
                last = nc.tensor.transpose(bank[0:META, 0, h * P:(h + 1) * P], kinv[:, h, SEQ:L], ident[:])
            last.then_inc(kt_full, 1)
            pe.wait_ge(ktok_done, 1)
            pe.wait_ge(gv_out, n)
            for h in range(GH):
                if h >= 2:
                    pe.wait_ge(sb_done, h - 1)
                nc.tensor.matmul(bank[:, (1, 5)[h % 2], 0:DV], rbuf[0:META, h * P:(h + 1) * P],
                                 vm[:, h * DV:(h + 1) * DV], start=True, stop=True).then_inc(um_full, 1)

            def g_scores(m):
                t, h = divmod(m, GH)
                if m:
                    pe.wait_ge(at_done, m)
                    pe.wait_ge(ktok_done, m + 1)
                nc.tensor.matmul(bank[:, 0, 0:P], kinv[:, h, cols(t)], qdec[:, h, cols(t)], start=True, stop=True)
                pe.wait_ge(kend_done, m + 1)
                nc.tensor.transpose(bank[:, 0, P:2 * P], kend, ident[:]).then_inc(kt_full, 1)

            def g_step(m):
                t, h = divmod(m, GH)
                a, b = (slice(t * P + c * CHUNK, t * P + c * CHUNK + CHUNK) for c in range(2))
                v = slice(h * DV, (h + 1) * DV)
                S = state[:, h, :]
                O = bank[:, 4, 0:DV]
                pe.wait_ge(at_done, m + 1)
                if m:
                    pe.wait_ge(o_copied, m)
                nc.tensor.matmul(O, at_sb[:, m % 2, :], gv[:, t, v], start=True, stop=False)
                pe.wait_ge(sb_done, m + 1)
                nc.tensor.matmul(O[0:CHUNK], qdec[:, h, a], S, start=False, stop=True).then_inc(o_part, 1)
                pe.wait_ge(ktok_done, m + 2)
                pe.wait_ge(sb_done, GH)
                if m:
                    pe.wait_ge(sa_done, m)
                nc.tensor.matmul(bank[:, 1, 0:DV], ktok[0:CHUNK, :], gv[0:CHUNK, t, v], start=True,
                                 stop=True).then_inc(ua_full, 1)
                if t < TILES - 1:
                    pe.wait_ge(sb_done, GH + m)
                    nc.tensor.matmul(bank[:, 5, 0:DV], ktok[CHUNK:P, :], gv[CHUNK:P, t, v], start=True,
                                     stop=True).then_inc(ub_full, 1)
                if m + 1 < GM:
                    g_scores(m + 1)
                pe.wait_ge(sa_done, m + 1)
                nc.tensor.matmul(O[CHUNK:P], qdec[:, h, b], S, start=False, stop=True).then_inc(go_full, 1)

            def g_free(m):
                if m:
                    n_o = len([k for k in gtp_order[:m] if k[0] == "o"])
                    pe.wait_ge(gtp_hi, m)
                    pe.wait_ge(gtp_lo, n_o)
                    if m > n_o:
                        pe.wait_ge(lg_read, m - n_o)

            def g_turn_o(t):
                pe.wait_ge(gated, t + 1)
                g_free(gtp_at[("o", t)])
                for k in range(KD):
                    last = nc.tensor.transpose(ps_t[:, k, :], o_at(t)[:, k * P:(k + 1) * P], ident[:])
                last.then_inc(gtp_full, 1)

            def g_out(t, ks):
                if ks[0] == 0:
                    pe.wait_ge(gtp_lo, t + 1)
                    if t:
                        pe.wait_ge(gy_read, t)
                for k in ks:
                    pe.wait_ge(lo_done, U_GO + k + 1)
                    s = (U_GO + k) % RING
                    for h in range(2):
                        w = slice(512 * h, 512 * h + 512)
                        last = three(ps_y[:, h, :], xT_hi[:, k, cols(t)], xT_lo[:, k, cols(t)], w_hi[:, s, w],
                                     w_lo[:, s, w], k == 0, k == KD - 1)
                    if t == TILES - 1:
                        last.then_inc(go_used, 1)
                    elif k == KD - 1:
                        last.then_inc(gy_full, 1)

            def g_turn_h(t):
                pe.wait_ge(h3_ready, t + 1)
                g_free(gtp_at[("h", t)])
                for k in range(KD):
                    last = nc.tensor.transpose(ps_t[:, k, :], zrow[:, t % 2, k * P:(k + 1) * P], ident[:])
                last.then_inc(gtp_full, 1)
                pe.wait_ge(gtp_hi, gtp_at[("h", t)] + 1)
                for k in range(KD):
                    last = nc.tensor.matmul(bank[:, 2, 0:NG + NE], gv[:, t, k * P:(k + 1) * P], w_rt[:, 1, k, :],
                                            start=(k == 0), stop=(k == KD - 1))
                last.then_inc(lg_full, 1)

            g_scores(0)
            for m in range(GM):
                t, h = divmod(m, GH)
                g_step(m)
                if t:
                    if h == 1:
                        g_turn_o(t - 1)
                    if h == 2:
                        g_out(t - 1, (0, 1, 2, 3))
                    if h == 3:
                        g_out(t - 1, (4, 5, 6, 7))
                        if t >= 2:
                            g_turn_h(t - 2)
            g_turn_o(TILES - 1)
            g_out(TILES - 1, tuple(range(KD)))
            for t in (TILES - 2, TILES - 1):
                g_turn_h(t)
            moe_pe(1, U_MOE1)


INPUTS = ["x", "meta_tokens", "attn_w_in", "attn_sinks", "attn_w_out", "gla_w_in", "gla_w_gate_up", "gla_b_gate",
          "gla_norm_g", "gla_w_out", "moe_w_group", "moe_b_group", "moe_w_router", "moe_b_router", "moe_w_gate",
          "moe_w_up", "moe_w_down", "ln_g", "ln_b"]


def kernel(**inputs):
    import numpy as np
    from concourse import bacc
    from concourse.bass_utils import run_bass_kernel_spmd

    nc = bacc.Bacc("TRN2", target_bir_lowering=False, num_devices=1)
    arrays, args = {}, []
    for name in INPUTS:
        a = np.ascontiguousarray(inputs[name])
        arrays[f"in_{name}_dram"] = a
        args.append(nc.dram_tensor(f"in_{name}_dram", a.shape, mybir.dt.from_np(a.dtype),
                                   kind="ExternalInput").ap())
    args.append(nc.dram_tensor("out_0_dram", (1, SEQ, D), F32, kind="ExternalOutput").ap())
    build_trunk(nc, *args)
    r = run_bass_kernel_spmd(nc, [arrays], core_ids=[0])
    return r.results[0]["out_0_dram"]
```

```python
from contextlib import ExitStack

import concourse.bass as bass
from concourse import mybir

F32 = mybir.dt.float32
F32R = mybir.dt.float32r
BF16 = mybir.dt.bfloat16
I32 = mybir.dt.int32
U32 = mybir.dt.uint32
ALU = mybir.AluOpType
ACT = mybir.ActivationFunctionType
X = mybir.AxisListType.X

P = 128
D = 1024
KD = D // P
SEQ = 512
META = 16
L = SEQ + META
TILES = SEQ // P
MT = TILES
HALF = L // 2
XW = SEQ + P
NH = 16
NKV = 4
GQ = NH // NKV
HD = 64
CHUNK = 64
ALPHA = 4 ** 0.25
LN_EPS = 1e-5
RMS_EPS = 1e-6
NG = 4
EPG = 4
NE = NG * EPG
FE = 256
KF = FE // P
GH = 4
DK = 128
DV = 256
GCH = SEQ // CHUNK
RANK = 16
GLA_LOW = 2 * GH * DK + 2 * GH * DV
TAU = 16.0
ROUNDS = -(-L // P)
BIG = 1e30

RING = 8
UNIT = 1024

U_K = 8
U_V = 10
U_AO = 12
U_MOE0 = 20
U_GV = U_MOE0 + 6 * NE
U_GL = U_GV + 8
U_GR = U_GL + 9
U_GO = U_GR + 8
U_MOE1 = U_GO + 8


def build_trunk(nc, x, meta_tokens, attn_w_in, attn_sinks, attn_w_out, gla_w_in, gla_w_gate_up, gla_b_gate,
                gla_norm_g, gla_w_out, moe_w_group, moe_b_group, moe_w_router, moe_b_router, moe_w_gate,
                moe_w_up, moe_w_down, ln_g, ln_b, out):
    ctx = ExitStack()
    with ctx:
        def sb(name, shape, dt):
            return ctx.enter_context(nc.sbuf_tensor(name, shape, dt))



        def sem(name):

            return ctx.enter_context(nc.semaphore(name))

        def scratch(name, shape):
            return nc.dram_tensor(name, shape, F32, kind="Internal").ap()

        h1_d = scratch("h1_d", (L, D))
        h2_d = scratch("h2_d", (L, D))
        h3_d = scratch("h3_d", (SEQ, D))
        r_d = scratch("r_d", (SEQ, D))
        y_d = [scratch(f"y{l}_d", (2 * L, D)) for l in range(2)]

        w_raw = sb("w_raw", [P, RING, UNIT], F32)
        w_hi = sb("w_hi", [P, RING, UNIT], F32R)
        w_lo = sb("w_lo", [P, RING, UNIT], F32R)
        xT_hi = sb("xT_hi", [P, KD, XW], F32R)
        xT_lo = sb("xT_lo", [P, KD, XW], F32R)
        ident = sb("ident", [P, P], F32)
        tri = sb("tri", [P, P], BF16)
        ones = sb("ones", [P, P], BF16)
        ids = sb("ids", [P, TILES + 1, 2], BF16)
        slot_id = sb("slot_id", [P, P], BF16)
        rev4 = sb("rev4", [P, EPG], F32)
        wgt = sb("wgt", [P, TILES + 1, 2], F32)
        rounds = sb("rounds", [P, 1], I32)
        idx = sb("idx", [P, 2, NE], I32)
        causal = sb("causal", [P, P], BF16)
        lg_sb = sb("lg_sb", [P, TILES + 1, NG + NE], F32)
        w_rt = sb("w_rt", [P, 2, KD, NG + NE], F32)
        b_rt = sb("b_rt", [P, 2, NG + NE], F32)
        sink_b = sb("sink_b", [P, NH], F32)
        zrow = sb("zrow", [P, 2, D], F32)
        gb = sb("gb", [P, 2, D], F32)
        ln_st = sb("ln_st", [P, 24], F32)
        ARENA = 13056
        arena = sb("arena", [P, ARENA], F32)

        def carve():
            at = [0]

            def take(n):
                a = arena[:, at[0]:at[0] + n]
                at[0] += n
                assert at[0] <= ARENA, at[0]
                return a
            return take

        take = carve()
        qT = take(8 * L).rearrange("p (f n) -> p f n", f=8)
        kT = take(2 * L).rearrange("p (f n) -> p f n", f=2)
        kside = take(TILES * 2 * P).rearrange("p (t f n) -> p t f n", t=TILES, f=2)
        v_at = take((TILES + 1) * 256)
        v_sb = v_at.rearrange("p (t n) -> p t n", t=TILES + 1)
        vside = take(TILES * 256).rearrange("p (t n) -> p t n", t=TILES)
        dist = take(TILES * 256).rearrange("p (t n) -> p t n", t=TILES)
        prob_at = take(2 * GQ * 256)
        prob = prob_at.rearrange("p (b j n) -> p b j n", b=2, j=GQ)
        tpose = take(KD * P).rearrange("p (k n) -> p k n", k=KD)
        sm_st = take(2 * 24).rearrange("p (b n) -> p b n", b=2)

        take = carve()
        xg = take(2 * D).rearrange("p (b n) -> p b n", b=2)
        sil = take(2 * FE).rearrange("p (b n) -> p b n", b=2)
        hid = take(2 * FE).rearrange("p (b n) -> p b n", b=2)
        rt = take(2048)
        slots = take(2 * (TILES + 1) * P // 2).bitcast(BF16).rearrange("p (k t n) -> p k t n", k=2, t=TILES + 1)
        entry = take(2 * (TILES + 1) * NE * 3 // 2).bitcast(BF16).rearrange("p (k t e c) -> p k t e c", k=2,
                                                                            t=TILES + 1, e=NE)
        weights_at = take(KD * 2 * FE)
        ysb = weights_at[:, 0:2 * D].rearrange("p (b n) -> p b n", b=2)
        ov_gu = weights_at.rearrange("p (k m c) -> p k m c", k=KD, m=2)
        ov_dn = [take(D) for _ in range(KF)]
        ov_hT = take(KF * P).rearrange("p (f n) -> p f n", f=KF)
        ov_y = xg[:, 0, :]
        ov_xT = xg[:, 1, :].rearrange("p (k n) -> p k n", k=KD)

        take = carve()
        ycomb = take(TILES * 2 * D).rearrange("p (b k n) -> p b k n", b=TILES, k=2)
        zcomb = take((TILES - 1) * D).rearrange("p (b n) -> p b n", b=TILES - 1)
        comb_st = take(2 * 24).rearrange("p (b n) -> p b n", b=2)

        take = carve()
        halves = take(TILES * 2 * D).rearrange("p (t h n) -> p t h n", t=TILES, h=2)
        gv = halves[:, :, 0, :]
        o_sb = halves[:, 0, 1, :]
        vm = o_sb[0:META, :]
        state = halves[:, 1, 1, :].rearrange("p (h n) -> p h n", h=GH)
        rbuf = halves[:, 2, 1, :]
        at_sb = halves[:, 3, 1, 0:2 * P].rearrange("p (b n) -> p b n", b=2)
        ktok = halves[:, 3, 1, 2 * P:3 * P]
        kend = halves[:, 3, 1, 3 * P:4 * P]
        junk = halves[:, 3, 1, 4 * P:4 * P + DV]
        la, lm, cb = (halves[:, t, 1, 0:L] for t in range(1, TILES))
        eb, fb, scan0 = (zrow[:].rearrange("p b n -> p (b n)")[:, i * L:(i + 1) * L] for i in range(3))
        gl_t = gb[:, 1, 0:L]
        qdec = take(GH * L).rearrange("p (h n) -> p h n", h=GH)
        kinv = take(GH * L).rearrange("p (h n) -> p h n", h=GH)
        gup = take(GH * DK)[0:RANK, :]
        bg = take(GH)
        dec = take(GH * (GCH + 1)).rearrange("p (h c) -> p h c", h=GH)
        ssq = take(3 * GH).rearrange("p (k h) -> p k h", k=3)

        bank = ctx.enter_context(nc.psum_tensor("bank", [P, 8, 512], F32))
        ps_q = [bank[:, 2 * b:2 * b + 2, :] for b in range(2)]
        ps_s = bank[:, 0:2, :].rearrange("p b (j n) -> p (b j) n", j=2)
        ps_t = bank[:, 2:4, :].rearrange("p b (k n) -> p (b k) n", k=4)
        ps_o = bank[:, 4, 0:2 * P].rearrange("p (j n) -> p j n", j=2)
        ps_r = bank[:, 5, :]
        ps_y = bank[:, 6:8, :]
        ps_x = (ps_t, ps_y.rearrange("p b (k n) -> p (b k) n", k=4))
        ps_gu = bank[:, 0, :]
        ps_h = bank[:, 1, 0:2 * P].rearrange("p (f n) -> p f n", f=KF)
        ps_rank = bank[:, 4, 0:(TILES + 2) * NE].rearrange("p (t e) -> p t e", e=NE)
        ps_tab = bank[:, 4, 256:256 + 3 * NE].rearrange("p (e c) -> p e c", c=3)

        raw_landed = [sem(f"raw_landed{s}") for s in range(RING)]
        hi_done = sem("hi_done")
        lo_done = sem("lo_done")
        ao_used = sem("ao_used")
        var_ready = sem("var_ready")
        rstd_ready = sem("rstd_ready")

        def unit_src(u):
            if u < U_K:
                a = (u // 2) % 2 + 4 * (u // 4) + 2 * (u % 2)
                return attn_w_in[0][:, a * P:(a + 1) * P].rearrange("(k p) c -> p k c", p=P), (KD, P)
            if u < U_V:
                c = NH * HD + (u - U_K) * P
                return attn_w_in[0][:, c:c + P].rearrange("(k p) c -> p k c", p=P), (KD, P)
            if u < U_AO:
                c = (NH + NKV) * HD
                k = 4 * (u - U_V)
                return attn_w_in[0][k * P:(k + 4) * P, c:c + 256].rearrange("(k p) c -> p k c", p=P), (4, 256)
            if u < U_MOE0:
                k = u - U_AO
                return attn_w_out[0][k * P:(k + 1) * P, :], None
            g = u - U_GL
            if g == 0:
                return gla_w_in[0][:, GLA_LOW:GLA_LOW + RANK].rearrange("(k p) c -> p k c", p=P), (KD, P)
            if U_GL < u < U_GR:
                c = (g - 1) % 2 * GH * DK + (g - 1) // 2 * DK
                return gla_w_in[0][:, c:c + P].rearrange("(k p) c -> p k c", p=P), (KD, P)
            if u < U_GO:
                v = u - U_GV if u < U_GL else u - U_GR + 8
                c = 2 * GH * DK + 512 * (v // 4)
                k = 2 * (v % 4)
                return gla_w_in[0][k * P:(k + 2) * P, c:c + 512].rearrange("(k p) c -> p k c", p=P), (2, 512)
            k = u - U_GO
            return gla_w_out[0][k * P:(k + 1) * P, :], None

        order = [MT] + list(range(TILES))
        steps = [(i, order[i], g) for i in range(len(order)) for g in range(NKV)]
        NS = len(steps)

        def rows(t):
            return META if t == MT else P

        def cols(t):
            return slice(t * P, t * P + rows(t))

        def blocks(t):
            return 1 if t == MT else 2

        def width(t):
            return META if t == MT else 2 * P

        tp_order = [("x", t) for t in order]
        for n in range(NS):
            tp_order.append(("p", n))
            if n % NKV == 2 and n >= 10:
                tp_order.append(("h", n // NKV - 2))
        tp_order += [("h", len(order) - 2), ("h", len(order) - 1)]
        tp_at = {k: n for n, k in enumerate(tp_order)}

        def step_unit(b):
            return 4 if b == 0 else 2 + 6 * b

        x_landed = [sem(f"x_landed{i}") for i in range(TILES + 1)]
        z_again = [sem(f"z_again{i}") for i in range(2)]
        cst = sem("cst")
        prm = [sem(f"prm{i}") for i in range(4)]
        tp_full = sem("tp_full")
        tp_hi = sem("tp_hi")
        tp_lo = sem("tp_lo")
        q_full = sem("q_full")
        q_out = sem("q_out")
        kv_full = sem("kv_full")
        v_out = sem("v_out")
        side_done = sem("side_done")
        s_full = sem("s_full")
        s_read = sem("s_read")
        front_done = sem("front_done")
        exp_done = sem("exp_done")
        p_ready = sem("p_ready")
        o_full = sem("o_full")
        o_hi = sem("o_hi")
        o_lo = sem("o_lo")
        y_full = sem("y_full")
        y_read = sem("y_read")
        h_ready = sem("h_ready")
        h_stored = [sem(f"h_stored{i}") for i in range(2)]
        rt_full = sem("rt_full")
        dve_order = sem("dve_order")

        def per_layer(name):
            return [sem(f"{name}{l}") for l in range(2)]

        exp_asked = sem("exp_asked")
        exp_given = sem("exp_given")
        chosen = sem("chosen")
        rank_full = sem("rank_full")
        hot_ready = sem("hot_ready")
        tab_full = per_layer("tab_full")
        idx_ready = per_layer("idx_ready")
        gathered = [sem(f"gathered{b}") for b in range(2)]
        xt_full = sem("xt_full")
        x_hi_done = sem("x_hi_done")
        x_lo_done = sem("x_lo_done")
        gu_used = sem("gu_used")
        silu_done = sem("silu_done")
        mul_done = sem("mul_done")
        ht_full = sem("ht_full")
        h_hi_done = sem("h_hi_done")
        h_lo_done = sem("h_lo_done")
        dn_used = sem("dn_used")
        y_out = sem("y_out")
        y_stored = [sem(f"y_stored{b}") for b in range(2)]
        comb_z = [sem(f"comb_z{b}") for b in range(TILES)]
        comb_y = [sem(f"comb_y{b}") for b in range(TILES)]
        xg_zero = sem("xg_zero")
        comb_used = sem("comb_used")
        weighed = sem("weighed")
        normed = sem("normed")
        centred = sem("centred")
        gained = sem("gained")
        norms_before = (len(order), 2 * len(order) + TILES)
        h2_ready = per_layer("h2_ready")
        h2_stored = per_layer("h2_stored")
        ov_w = per_layer("ov_w")
        ov_g = per_layer("ov_g")
        ov_s = per_layer("ov_s")
        ov_set = per_layer("ov_set")
        ov_dve = per_layer("ov_dve")
        ov_pe = per_layer("ov_pe")
        ov_act = per_layer("ov_act")
        h2_tp = sem("h2_tp")
        h2_hi = sem("h2_hi")
        h2_lo = sem("h2_lo")

        gprm = sem("gprm")
        gb_ng = sem("gb_ng")
        glow_full = sem("glow_full")
        glow_out = sem("glow_out")
        gate_full = sem("gate_full")
        qk_full = sem("qk_full")
        abs_done = sem("abs_done")
        ln_done = sem("ln_done")
        cum_done = sem("cum_done")
        ef_done = sem("ef_done")
        dec_done = sem("dec_done")
        gv_full = sem("gv_full")
        gv_out = sem("gv_out")
        r_ready = sem("r_ready")
        r_stored = [sem(f"r_stored{i}") for i in range(4)]
        r_landed = sem("r_landed")
        kend_done = sem("kend_done")
        kt_full = sem("kt_full")
        ktok_done = sem("ktok_done")
        at_done = sem("at_done")
        o_part = sem("o_part")
        ua_full = sem("ua_full")
        ub_full = sem("ub_full")
        sa_done = sem("sa_done")
        sb_done = sem("sb_done")
        go_full = sem("go_full")
        o_copied = sem("o_copied")
        sq_done = sem("sq_done")
        gated = sem("gated")
        gtp_full = sem("gtp_full")
        gtp_hi = sem("gtp_hi")
        gtp_lo = sem("gtp_lo")
        gy_full = sem("gy_full")
        gy_read = sem("gy_read")
        go_used = sem("go_used")
        z_landed = [sem(f"z_landed{i}") for i in range(2)]
        gb_l3 = sem("gb_l3")
        h3_ready = sem("h3_ready")
        lm_done = sem("lm_done")
        qd_done = sem("qd_done")
        um_full = sem("um_full")
        h3_stored = [sem(f"h3_stored{i}") for i in range(2)]
        lg_full = sem("lg_full")
        lg_read = sem("lg_read")
        gtp_order = []
        for t in range(TILES):
            if t >= 3:
                gtp_order.append(("h", t - 3))
            if t >= 1:
                gtp_order.append(("o", t - 1))
        gtp_order += [("o", TILES - 1), ("h", TILES - 3), ("h", TILES - 2), ("h", TILES - 1)]
        gtp_at = {k: n for n, k in enumerate(gtp_order)}
        GM = TILES * GH

        def ub_wait(eng, m):
            if m // GH < TILES - 1:
                eng.wait_ge(ub_full, m + 1)

        def o_at(t):
            return o_sb if t == 0 else gv[:, t - 1, :]

        def r_piece(m):
            return zrow[:, (m % 4) // 2, 512 * (m % 2):512 * (m % 2) + 512]

        turn = [0]

        def B(b):
            return b + 4 * turn[0]

        def B2(b):
            return b // 2 + 2 * turn[0]

        Y_COUNT = 16 + 16 * NE // 2

        def moe_steps(eng, step):
            step(0)
            step(1)
            with eng.Fori(0, (NE - 4) // 4) as it:
                turn[0] = it
                for b in range(2, 6):
                    step(b)
                turn[0] = 0
            step(NE - 2)
            step(NE - 1)

        def z_rows(n):
            return zrow[:, n, :] if n < 2 else zcomb[:, n - 2, :]

        def y_rows(n, k):
            return ycomb[:, n, k, :] if n < TILES else ycomb[:, k, 1, :]

        def load_y(eng, l, n):
            t = moe_tiles(l)[n]
            for k in range(2):
                eng.dma_start(y_rows(n, k)[:rows(t)], y_d[l][k * L + t * P:k * L + t * P + rows(t), :]
                              ).then_inc(comb_y[n % TILES], 16)

        def comb_wait(eng, l, n):
            seen = n // TILES + (2 * l if n % TILES == 0 else l)
            eng.wait_ge(comb_z[n % TILES], 16 * (1 + seen))
            eng.wait_ge(comb_y[n % TILES], 32 * (1 + seen))

        def further(eng, l, body, unroll=False, stored=False, start=None):
            eng.wait_ge(idx_ready[l], 1)
            n = eng.value_load(rounds[0:1, 0:1], min_val=0, max_val=ROUNDS - 1)
            for r in range(1, ROUNDS):
                with eng.If(n >= r):
                    if start:
                        start(r)
                    if unroll:
                        for e in range(NE):
                            body(r, e)
                    else:
                        with eng.Fori(0, NE) as e:
                            body(r, e)
                        if stored:
                            eng.wait_ge(ov_s[l], 16 * NE * r)

        def moe_tiles(l):
            return list(range(TILES)) + ([MT] if l == 0 else [])

        block = ctx.enter_context(nc.Block())

        @block.sync
        def _(sp):
            def load_unit(u):
                s = u % RING
                if u >= RING:
                    sp.wait_ge(lo_done, u - RING + 1)
                src, shape = unit_src(u)
                dst = w_raw[:, s, :]
                if shape:
                    n = shape[0] // 2
                    dst = dst.rearrange("p (k c) -> p k c", k=shape[0])[:, :, 0:src.shape[2]]
                    halves = [(dst[:, h * n:h * n + n, :], src[:, h * n:h * n + n, :]) for h in range(2)]
                else:
                    n = UNIT // 2
                    halves = [(dst[:, h * n:h * n + n], src[:, h * n:h * n + n]) for h in range(2)]
                for d, a in halves:
                    sp.dma_start(d, a).then_inc(raw_landed[s], 16)

            def load_gu(l, s, e, j, ready):
                sp.wait_ge(lo_done, ready)
                dst = w_raw[:, s, :].rearrange("p (k m c) -> p k m c", k=2, m=2)
                for m, w in enumerate((moe_w_gate, moe_w_up)):
                    src = w[l].rearrange("e d f -> (e d) f")[bass.ds(e * D + 2 * j * P, 2 * P), :]
                    sp.dma_start(dst[:, :, m, :], src.rearrange("(k p) c -> p k c", p=P)).then_inc(raw_landed[s], 16)

            def load_dn(l, s, e, f, ready):
                sp.wait_ge(lo_done, ready)
                down = moe_w_down[l].rearrange("e f d -> (e f) d")
                for h in range(2):
                    src = down[bass.ds(e * FE + f * P, P), h * 512:h * 512 + 512]
                    sp.dma_start(w_raw[:, s, h * 512:h * 512 + 512], src).then_inc(raw_landed[s], 16)

            def load_moe(l):
                u0 = (U_MOE0, U_MOE1)[l]

                def load(kind, b, j, r):
                    kind(l, (u0 + r) % RING, B(b), j, u0 + r - RING + 1 + 24 * turn[0])

                def step(b):
                    r = step_unit(b)
                    if b:
                        for f in range(KF):
                            load(load_dn, b - 1, f, r)
                            r += 1
                    if b + 1 < NE:
                        for j in range(4):
                            load(load_gu, b + 1, j, r)
                            r += 1

                for j in range(4):
                    load(load_gu, 0, j, j)
                moe_steps(sp, step)
                for f in range(KF):
                    load(load_dn, NE - 1, f, 6 * NE - KF + f)

            for u in range(U_MOE0):
                load_unit(u)
            load_moe(0)
            with nc.allow_non_contiguous_dma(reason="the low-rank gate's 16 columns"):
                for u in range(U_GV, U_MOE1):
                    load_unit(u)
            load_moe(1)

        @block.gpsimd
        def _(pool):
            nc.gpsimd.memset(ident[:], 0.0).then_inc(cst, 1)
            nc.gpsimd.memset(tri[:], 1.0).then_inc(cst, 1)
            nc.gpsimd.memset(ones[:], 1.0).then_inc(cst, 1)
            pool.wait_ge(cst, 3)
            nc.gpsimd.affine_select(out=ident[:], in_=ident[:], compare_op=ALU.not_equal, fill=1.0, base=0,
                                    pattern=[[-1, P]], channel_multiplier=1).then_inc(cst, 1)
            nc.gpsimd.affine_select(out=tri[:], in_=tri[:], compare_op=ALU.is_gt, fill=0.0, base=0,
                                    pattern=[[1, P]], channel_multiplier=-1).then_inc(cst, 1)
            for t in range(TILES):
                nc.gpsimd.iota(dist[:, t, 0:P], [[-1, P]], base=0, channel_multiplier=1,
                               allow_small_or_imprecise_dtypes=True).then_inc(cst, 1)
                nc.gpsimd.iota(dist[:, t, P:P + META], [[-1, META]], base=META + P * t, channel_multiplier=1,
                               allow_small_or_imprecise_dtypes=True).then_inc(cst, 1)
                nc.gpsimd.iota(dist[:, t, P + CHUNK:2 * P], [[-1, CHUNK]], base=CHUNK, channel_multiplier=1,
                               allow_small_or_imprecise_dtypes=True).then_inc(cst, 1)
            nc.gpsimd.memset(causal[:], 1.0).then_inc(cst, 1)
            pool.wait_ge(cst, 6 + 3 * TILES)
            nc.gpsimd.affine_select(out=causal[:], in_=causal[:], compare_op=ALU.is_ge, fill=0.0, base=0,
                                    pattern=[[1, P]], channel_multiplier=-1).then_inc(cst, 1)
            pool.wait_ge(cst, 7 + 3 * TILES)
            nc.gpsimd.memset(causal[0:CHUNK, CHUNK:P], 0.0).then_inc(cst, 1)
            nc.gpsimd.iota(slot_id[:], [[1, P]], base=0, channel_multiplier=0,
                           allow_small_or_imprecise_dtypes=True).then_inc(cst, 1)
            nc.gpsimd.iota(rev4[:], [[-1, EPG]], base=EPG, channel_multiplier=0,
                           allow_small_or_imprecise_dtypes=True).then_inc(cst, 1)
            nc.gpsimd.iota(ids[:, :, 0], [[P, TILES + 1]], base=0, channel_multiplier=0,
                           allow_small_or_imprecise_dtypes=True).then_inc(cst, 1)
            nc.gpsimd.iota(ids[:, :, 1], [[0, TILES + 1]], base=1, channel_multiplier=1,
                           allow_small_or_imprecise_dtypes=True).then_inc(cst, 1)
            pool.dma_start(sink_b[:], attn_sinks.rearrange("a h -> (a h)").partition_broadcast(P)).then_inc(prm[0], 16)

            def load_router(l, done):
                with nc.allow_non_contiguous_dma(reason="router columns"):
                    pool.dma_start(w_rt[:, l, :, 0:NG],
                                   moe_w_group[l].rearrange("(k p) c -> p k c", p=P)).then_inc(done, 16)
                    for g in range(NG):
                        pool.dma_start(w_rt[:, l, :, NG + EPG * g:NG + EPG * g + EPG],
                                       moe_w_router[l, g].rearrange("(k p) c -> p k c", p=P)).then_inc(done, 16)
                pool.dma_start(b_rt[:, l, 0:NG], moe_b_group[l].partition_broadcast(P)).then_inc(done, 16)
                pool.dma_start(b_rt[:, l, NG:], moe_b_router[l].rearrange("g e -> (g e)").partition_broadcast(P)
                               ).then_inc(done, 16)

            pool.wait_ge(q_full, 1)
            load_router(0, prm[1])
            pool.dma_start(gb[:, 0, :], ln_g[0, 0].partition_broadcast(P)).then_inc(prm[2], 16)
            pool.dma_start(gb[:, 1, :], ln_b[0, 0].partition_broadcast(P)).then_inc(prm[2], 16)
            load_router(1, prm[3])

            def affine(z, R, n):
                pool.wait_ge(normed, n)
                nc.gpsimd.tensor_tensor(z, z, gb[:R, 0, :], ALU.mult).then_inc(gained, 1)
                gains[0] += 1
                pool.wait_ge(gained, gains[0])
                return nc.gpsimd.tensor_tensor(z, z, gb[:R, 1, :], ALU.add)

            gains = [0]
            pool.wait_ge(prm[2], 32)
            for i in range(len(order)):
                t = order[i]
                if i < len(order) - 1:
                    affine(zrow[:rows(t), i % 2, :], rows(t), i + 1).then_inc(h_ready, 1)
                if i + 2 < len(order):
                    pool.wait_ge(h_stored[i % 2], 16 * (i // 2 + 1))
                    pool.wait_ge(tp_full, tp_at[("h", i)] + 1)
                    pool.dma_start(zrow[:, i % 2, :], x[0][cols(order[i + 2]), :]).then_inc(z_again[i % 2], 16)

            def moe_pool(l, src, before):
                before()
                pool.dma_start(gb[:, 0, :], ln_g[l, 1].partition_broadcast(P)).then_inc(y_stored[0], 16)
                pool.dma_start(gb[:, 1, :], ln_b[l, 1].partition_broadcast(P)).then_inc(y_stored[1], 16)

                def load_z(n):
                    t = moe_tiles(l)[n]
                    pool.dma_start(z_rows(n)[:rows(t)], src[cols(t), :]).then_inc(comb_z[n % TILES], 16)

                load_z(0)
                load_z(1)
                if l == 0:
                    nc.gpsimd.memset(xg[:], 0.0).then_inc(xg_zero, 1)
                    pool.wait_ge(xg_zero, 1)
                pool.wait_ge(idx_ready[l], 1)

                def gather(b):
                    if b >= 2:
                        pool.wait_ge(xt_full, NE * l + b - 1)
                    pool.indirect_dma_start(xg[:, b % 2, :], None, src,
                                            bass.IndirectOffsetOnAxis(ap=idx[:, 0, b:b + 1].bitcast(U32), axis=0),
                                            bounds_check=src.shape[0] - 1, oob_is_err=False).then_inc(gathered[b % 2], 16)

                gather(0)
                gather(1)
                gather(2)
                for b in range(NE):
                    if b + 3 < NE:
                        gather(b + 3)
                    pool.wait_ge(y_out, NE * l + b + 1)
                    pool.indirect_dma_start(y_d[l], bass.IndirectOffsetOnAxis(ap=idx[:, 1, b:b + 1].bitcast(U32),
                                                                              axis=0),
                                            ysb[:, b % 2, :], None, bounds_check=2 * L - 1,
                                            oob_is_err=False).then_inc(y_stored[b % 2], 16)
                for b in range(2):
                    pool.wait_ge(y_stored[b], Y_COUNT * (l + 1))

                def more(r, e):
                    q = e + NE * (r - 1)
                    if e == 0:
                        pool.wait_ge(idx_ready[l], r + 1)
                    if q:
                        pool.wait_ge(ov_s[l], 16 * q)
                    pool.indirect_dma_start(ov_y, None, src,
                                            bass.IndirectOffsetOnAxis(ap=idx[:, 0, e:e + 1].bitcast(U32), axis=0),
                                            bounds_check=src.shape[0] - 1, oob_is_err=False).then_inc(ov_g[l], 16)
                    pool.wait_ge(ov_act[l], 4 * q + 4)
                    pool.indirect_dma_start(y_d[l], bass.IndirectOffsetOnAxis(ap=idx[:, 1, e:e + 1].bitcast(U32),
                                                                              axis=0),
                                            ov_y, None, bounds_check=2 * L - 1,
                                            oob_is_err=False).then_inc(ov_s[l], 16)
                    if e == NE - 1:
                        pool.wait_ge(ov_s[l], 16 * q + 16)

                further(pool, l, more, unroll=True)
                pool.wait_ge(weighed, len(order) * l + 1)
                for n in (2, 3):
                    load_z(n)
                if l == 0:
                    pool.wait_ge(comb_used, 1)
                    load_z(TILES)
                for n, t in enumerate(moe_tiles(l)[:-1]):
                    affine(z_rows(n)[:rows(t)], rows(t), norms_before[l] + n + 1).then_inc(h2_ready[l], 1)

            def norm0_done():
                pool.wait_ge(h_ready, len(order))
                for b in range(2):
                    pool.wait_ge(h_stored[b], 16 * ((len(order) + 1 - b) // 2))
                pool.wait_ge(tp_full, len(tp_order))

            moe_pool(0, h1_d, norm0_done)

            pool.wait_ge(h2_ready[0], len(order))
            pool.wait_ge(h2_stored[0], 16 * len(order))
            pool.dma_start(gb[:, 0, :], gla_norm_g[0].partition_broadcast(P)).then_inc(gb_ng, 16)
            pool.dma_start(gup, gla_w_gate_up[0]).then_inc(gprm, 16)
            with nc.allow_non_contiguous_dma(reason="the gate's bias, by partition"):
                pool.dma_start(bg, gla_b_gate[0].rearrange("(h p) -> p h", p=P)).then_inc(gprm, 16)
            pool.wait_ge(r_ready, 8)
            for c in range(2):
                src = (ln_g, ln_b)[c]
                pool.dma_start(gb[:, c, :], src[1, 0].partition_broadcast(P)).then_inc(gb_l3, 16)
            for i in range(4):
                pool.wait_ge(r_stored[i], 32)
            pool.wait_ge(sb_done, GH)
            pool.dma_start(rbuf, r_d[0:P, :]).then_inc(r_landed, 16)
            for t in range(2):
                pool.dma_start(zrow[:, t, :], h2_d[cols(t), :]).then_inc(z_landed[t], 16)
            for t in range(TILES):
                if t >= 2:
                    affine(zrow[:, t % 2, :], P, 2 * len(order) + t - 1).then_inc(h3_ready, 1)
                    pool.wait_ge(h3_stored[t % 2], 16 * (t // 2))
                    pool.wait_ge(gtp_full, gtp_at[("h", t - 2)] + 1)
                    pool.dma_start(zrow[:, t % 2, :], h2_d[cols(t), :]).then_inc(z_landed[t % 2], 16)
                if t + 1 < TILES:
                    pool.wait_ge(gated, t + 1)
                    pool.dma_start(rbuf, r_d[cols(t + 1), :]).then_inc(r_landed, 16)
            affine(zrow[:, (TILES - 2) % 2, :], P, 2 * len(order) + TILES - 1).then_inc(h3_ready, 1)

            def norm2_done():
                pool.wait_ge(h3_ready, TILES)
                for b in range(2):
                    pool.wait_ge(h3_stored[b], 16 * (TILES // 2))
                pool.wait_ge(gtp_full, len(gtp_order))

            moe_pool(1, h3_d, norm2_done)

        def x_rows(i):
            return (zrow[:, 0, :], zrow[:, 1, :], prob_at[:, 0:D], prob_at[:, D:2 * D], v_at[:, 0:D])[i]

        def raw_unit(u):
            raw = w_raw[:, u % RING, :]
            return raw.rearrange("p (k f c) -> p f k c", k=KD, f=2) if u < U_K else raw

        def split_unit(w, u):
            s = u % RING
            if u >= U_K:
                return w[:, s, :]
            pair = w[:, s - u % 2:s - u % 2 + 2, :]
            return pair.rearrange("p f (k h c) -> p f k h c", h=2, c=HD)[:, :, :, u % 2, :]

        def unit_used(eng, u):
            if u < U_K:
                eng.wait_ge(q_full, 2 * (u // 2) + 2)
            elif u < U_V:
                eng.wait_ge(q_full, u + 1)
            elif u < U_AO:
                eng.wait_ge(kv_full, len(order))
            elif u < U_MOE0:
                eng.wait_ge(ao_used, u - U_AO + 1)
            elif u < U_GV:
                eng.wait_ge(dn_used, 2 * NE - (U_GV - 1 - u))
            elif u < U_GL:
                eng.wait_ge(gv_full, 9 + (u - U_GV) // 4)
            elif u == U_GL:
                eng.wait_ge(glow_full, 1)
            elif u < U_GR:
                eng.wait_ge(qk_full, u - U_GL)
            elif u < U_GO:
                eng.wait_ge(gv_full, 14 + 4 * ((u - U_GR) // 4))
            elif u < U_MOE1:
                eng.wait_ge(go_used, u - U_GO + 1)

        def ahead_used(eng, l, b, j):
            if j >= 4:
                eng.wait_ge(gu_used, 4 * NE * l + 4 * B(b) + j + 1)
            elif b == 0:
                eng.wait_ge(gu_used, 4 * NE * l + j + 1)
            elif j >= 2:
                eng.wait_ge(dn_used, 2 * NE * l + 2 * B(b) + j - 3)
            else:
                eng.wait_ge(gu_used, 4 * NE * l + 4 * B(b) + j + 3)

        RTW = TILES + 1
        rt_at = [0]

        def rt_take(*shape):
            n = 1
            for d in shape:
                n *= d
            a = rt[:, rt_at[0]:rt_at[0] + n]
            rt_at[0] += n
            names = "abcd"[:len(shape)]
            if len(shape) > 1:
                a = a.rearrange(f"p ({' '.join(names)}) -> p {' '.join(names)}", **dict(zip(names, shape)))
            return a

        rt_lg = rt_take(RTW, NG + NE)
        rt_g = rt_take(RTW, 1)
        rt_a = rt_take(RTW, EPG)
        rt_c = rt_take(RTW, EPG)
        rt_m = rt_take(RTW, 1)
        rt_ohg = rt_take(RTW, NG)
        rt_dg = rt_take(RTW, NG)
        rt_pr = rt_take(RTW, NG, EPG)
        rt_z = rt_take(RTW, EPG)
        rt_m1 = rt_take(RTW, 1)
        rt_m2 = rt_take(RTW, 1)
        rt_oh = [rt_take(RTW, EPG) for _ in range(2)]
        rt_dm = rt_take(RTW, 1)
        rt_gt = rt_take(RTW, 1)
        rt_M = [rt_take(RTW, NE) for _ in range(2)]
        rt_rank = rt_take(RTW + 1, NE)
        rt_q = rt_take(RTW, NE)
        rt_q2 = rt_take(RTW, NE)
        rt_p = rt_take(RTW, 2)
        rt_place = rt_take(2, RTW)
        rt_round = rt_take(2, RTW)
        rt_Mb = rt_take(RTW * NE // 2).bitcast(BF16).rearrange("p (t e) -> p t e", e=NE)

        def rt_exp(k, NT):
            return (rt_dg[:, 0:NT, :], rt_dm[:, 0:NT, :])[k]

        def store_h(act, j):
            t = order[j]
            act.wait_ge(h_ready, j + 1)
            act.dma_start(h1_d[cols(t), :], zrow[:rows(t), j % 2, :]).then_inc(h_stored[j % 2], 16)

        @block.scalar
        def _(act):
            norms = [0]

            def rsqrt(v, r):
                norms[0] += 1
                act.wait_ge(var_ready, norms[0])
                nc.scalar.activation(r, v, ACT.Sqrt).then_inc(rstd_ready, 1)

            norm_no = [0]

            def normalize(z, st):
                norm_no[0] += 1
                act.wait_ge(centred, norm_no[0])
                nc.scalar.activation(z, z, ACT.Identity, bias=st[:, 15:16], scale=st[:, 14:15]).then_inc(normed, 1)

            def split_hi(u):
                s = u % RING
                act.wait_ge(raw_landed[s], 32 * (u // RING + 1))
                if u >= RING:
                    unit_used(act, u - RING)
                nc.scalar.activation(split_unit(w_hi, u), raw_unit(u), ACT.Copy).then_inc(hi_done, 1)

            def x_hi(i):
                act.wait_ge(tp_full, i + 1)
                nc.scalar.activation(xT_hi[:, :, cols(order[i])], ps_x[i % 2][:, :, 0:rows(order[i])],
                                     ACT.Copy).then_inc(tp_hi, 1)

            for i in range(len(order)):
                t = order[i]
                act.dma_start(x_rows(i)[:rows(t)], meta_tokens if t == MT else x[0][cols(t), :]
                              ).then_inc(x_landed[i], 16)
            u = 0
            for i in range(len(order)):
                x_hi(i)
                if i >= 1:
                    split_hi(u)
                    u += 1
            while u < RING:
                split_hi(u)
                u += 1
            for f in range(8):
                act.wait_ge(q_full, f + 1)
                nc.scalar.activation(qT[:, f, :].rearrange("p (h n) -> p h n", h=2), ps_q[f % 2][:, :, 0:HALF],
                                     ACT.Copy, scale=HD ** -0.5).then_inc(q_out, 1)
                if f % 2:
                    split_hi(u)
                    split_hi(u + 1)
                    u += 2
            for f in range(2):
                act.wait_ge(q_full, 9 + f)
                nc.scalar.activation(kT[:, f, :].rearrange("p (h n) -> p h n", h=2), ps_q[f % 2][:, :, 0:HALF],
                                     ACT.Copy).then_inc(q_out, 1)
                split_hi(u)
                u += 1
            assert u == 18

            def exps(n):
                i, t, g = steps[n]
                R, W = rows(t), width(t)
                act.wait_ge(front_done, n + 1)
                for j in range(GQ):
                    nc.scalar.activation(prob[:R, n % 2, j, 0:W], prob[:R, n % 2, j, 0:W], ACT.Exp,
                                         bias=sm_st[:R, n % 2, 8 + j:9 + j],
                                         accum_out=sm_st[:R, n % 2, 16 + j:17 + j])
                nc.scalar.activation(sm_st[:R, n % 2, 12:16], sm_st[:R, n % 2, 12:16], ACT.Exp).then_inc(exp_done, 1)

            def copy_t(key, R, sub=None):
                m = tp_at[key]
                act.wait_ge(tp_full, m + 1)
                what, k = tp_order[m - 1]
                if what == "p":
                    act.wait_ge(o_full, k + 1)
                elif what == "h":
                    act.wait_ge(rt_full, k + 1)
                if sub:
                    src, dst = ps_t[0:META, 0::2, 0:R], tpose[0:META, 0::2, 0:R]
                else:
                    src, dst = ps_t[:, :, 0:R], tpose[:, :, 0:R]
                nc.scalar.activation(dst, src, ACT.Copy).then_inc(tp_hi, 1)

            act.wait_ge(side_done, 1)
            exps(0)
            for n in range(NS):
                i, t, g = steps[n]
                if n + 1 < NS:
                    exps(n + 1)
                if g == 0 and i >= 2:
                    rsqrt(ln_st[:, 13:14], ln_st[:, 14:15])
                copy_t(("p", n), rows(t), sub=(t == MT))
                act.wait_ge(o_full, n + 1)
                nc.scalar.activation(xT_hi[:, 2 * g:2 * g + 2, cols(t)], ps_o[:, :, 0:rows(t)],
                                     ACT.Copy).then_inc(o_hi, 1)
                if n < 2:
                    split_hi(18 + n)
                if g == 0 and i >= 2:
                    normalize(zrow[:rows(order[i - 2]), i % 2, :], ln_st[:rows(order[i - 2]), :])
                if n % NKV == 2 and n >= 10:
                    j = n // NKV - 2
                    store_h(act, j)
                    copy_t(("h", j), rows(order[j]))
            j = len(order) - 2
            rsqrt(ln_st[:, 13:14], ln_st[:, 14:15])
            normalize(zrow[:, j % 2, :], ln_st[:, :])
            for u in range(U_MOE0, U_MOE0 + RING):
                split_hi(u)
            store_h(act, j)
            copy_t(("h", j), P)
            rsqrt(ln_st[:, 13:14], ln_st[:, 14:15])
            normalize(zrow[:, (j + 1) % 2, :], ln_st[:, :])
            store_h(act, j + 1)
            copy_t(("h", j + 1), P)
            for b in range(2):
                act.wait_ge(h_stored[b], 16 * ((len(order) + 1 - b) // 2))

            def hi_ahead(l, u0, b, j):
                r = RING + 6 * b + j
                s = (u0 + r) % RING
                act.wait_ge(raw_landed[s], 32 * ((u0 + r) // RING + 1) + 96 * turn[0])
                ahead_used(act, l, b, j)
                nc.scalar.activation(w_hi[:, s, :], w_raw[:, s, :], ACT.Copy).then_inc(hi_done, 1)

            def moe_act(l, u0):
                NT = len(moe_tiles(l))
                for k in range(2):
                    act.wait_ge(exp_asked, 2 * l + k + 1)
                    e = rt_exp(k, NT)
                    nc.scalar.activation(e, e, ACT.Exp).then_inc(exp_given, 1)

                def x_high(b):
                    act.wait_ge(xt_full, NE * l + B(b) + 1)
                    c = slice((b % 2) * P, (b % 2) * P + P)
                    nc.scalar.activation(xT_hi[:, :, c], ps_t[:, :, :], ACT.Copy).then_inc(x_hi_done, 1)

                def y_evac(b):
                    act.wait_ge(dn_used, 2 * NE * l + 2 * B(b) + 2)
                    act.wait_ge(y_stored[b % 2], 16 + Y_COUNT * l + 16 * B2(b))
                    nc.scalar.activation(ysb[:, b % 2, :].rearrange("p (h n) -> p h n", h=2), ps_y[:, :, :],
                                         ACT.Copy).then_inc(y_out, 1)

                def h_high(b):
                    act.wait_ge(ht_full, NE * l + B(b) + 1)
                    c = slice((2 + b % 2) * P, (3 + b % 2) * P)
                    nc.scalar.activation(xT_hi[:, 0:KF, c], ps_h[:, :, :], ACT.Copy).then_inc(h_hi_done, 1)

                x_high(0)

                def step(b):
                    act.wait_ge(gu_used, 4 * NE * l + 4 * B(b) + 4)
                    if b >= 2:
                        act.wait_ge(mul_done, NE * l + B(b) - 1)
                    nc.scalar.activation(sil[:, b % 2, :], ps_gu[:, 0:FE], ACT.Silu).then_inc(silu_done, 1)
                    if b + 1 < NE:
                        x_high(b + 1)
                    js = [j for j in range(6) if l == 0 or 8 + 6 * b + j < 6 * NE]
                    if b == NE - 1:
                        js = [j for j in js if j < 4]
                    if b:
                        y_evac(b - 1)
                    h_high(b)
                    for j in js:
                        hi_ahead(l, u0, b, j)

                moe_steps(act, step)
                y_evac(NE - 1)
                for b in range(2):
                    act.wait_ge(y_stored[b], Y_COUNT * (l + 1))

                def more(r, e):
                    q = e + NE * (r - 1)
                    for m, w in enumerate((moe_w_gate, moe_w_up)):
                        rows_e = w[l].rearrange("e d f -> (e d) f")[bass.ds(e * D, D), :]
                        act.dma_start(ov_gu[:, :, m, :], rows_e.rearrange("(k p) c -> p k c", p=P)
                                      ).then_inc(ov_w[l], 16)
                    down = moe_w_down[l].rearrange("e f d -> (e f) d")
                    for f in range(KF):
                        act.dma_start(ov_dn[f], down[bass.ds(e * FE + f * P, P), :]).then_inc(ov_w[l], 16)
                    act.wait_ge(ov_pe[l], 4 * q + 1)
                    nc.scalar.activation(ov_xT, ps_t[:, :, :], ACT.Copy).then_inc(ov_act[l], 1)
                    act.wait_ge(ov_pe[l], 4 * q + 2)
                    nc.scalar.activation(sil[:, 0, :], ps_gu[:, 0:FE], ACT.Silu).then_inc(ov_act[l], 1)
                    act.wait_ge(ov_pe[l], 4 * q + 3)
                    nc.scalar.activation(ov_hT, ps_h[:, :, :], ACT.Copy).then_inc(ov_act[l], 1)
                    act.wait_ge(ov_pe[l], 4 * q + 4)
                    nc.scalar.activation(ov_y.rearrange("p (h n) -> p h n", h=2), ps_y[:, :, :],
                                         ACT.Copy).then_inc(ov_act[l], 1)

                further(act, l, more, stored=True)
                for n in range(TILES):
                    load_y(act, l, n)
                nc.scalar.activation(ln_st[:, 21:22], ln_st[:, 20:21], ACT.Sqrt)

                def weigh(n):
                    R = rows(T[n])
                    comb_wait(act, l, n)
                    y = y_rows(n, 0)[:R]
                    nc.scalar.activation(y, y, ACT.Copy, scale=wgt[:R, n, 0:1]).then_inc(weighed, 1)

                def finish(n):
                    t = T[n]
                    act.wait_ge(h2_ready[l], n + 1)
                    dst = h2_d if l == 0 else out[0]
                    act.dma_start(dst[cols(t), :], z_rows(n)[:rows(t)]).then_inc(h2_stored[l], 16)
                    if l == 0:
                        act.wait_ge(h2_tp, n + 1)
                        nc.scalar.activation(xT_hi[:, :, cols(t)], ps_t[:, :, 0:rows(t)], ACT.Copy).then_inc(h2_hi, 1)

                def values_out(n, c):
                    t = T[n]
                    act.wait_ge(gv_full, 2 * n + c + 1)
                    act.wait_ge(comb_used, n + 1)
                    dst = vm[:, 512 * c:512 * c + 512] if t == MT else gv[:, t, 512 * c:512 * c + 512]
                    nc.scalar.activation(dst, bank[:rows(t), 6 + (c + 1) % 2, :], ACT.Copy).then_inc(gv_out, 1)

                T = moe_tiles(l)
                if l == 0:
                    split_hi(U_GV + 6)
                    split_hi(U_GV + 7)
                weigh(0)
                for n in range(len(T)):
                    if n + 1 == TILES and l == 0:
                        act.wait_ge(comb_used, 2)
                        load_y(act, l, TILES)
                    if n + 1 < len(T):
                        weigh(n + 1)
                    if n >= 2:
                        finish(n - 2)
                    if n >= 3 and l == 0:
                        values_out(n - 3, 0)
                        values_out(n - 3, 1)
                    R = rows(T[n])
                    st = comb_st[:R, n % 2, :]
                    rsqrt(st[:, 13:14], st[:, 14:15])
                    normalize(z_rows(n)[:R], st)
                for n in range(len(T) - 2, len(T)):
                    finish(n)
                    if l == 0:
                        values_out(n - 1, 0)
                        values_out(n - 1, 1)
                if l == 0:
                    for c in range(2):
                        values_out(len(T) - 1, c)
                        for u in range(U_GL + 4 * c, U_GL + 4 * c + 4):
                            split_hi(u)

            moe_act(0, U_MOE0)
            act.wait_ge(h2_stored[0], 16 * len(moe_tiles(0)))

            def store_r(m):
                act.wait_ge(r_ready, m + 1)
                act.dma_start(r_d[cols(m % 4), 512 * (m // 4):512 * (m // 4) + 512], r_piece(m)
                              ).then_inc(r_stored[m % 4], 16)

            act.wait_ge(glow_full, 1)
            nc.scalar.activation(gl_t[0:RANK, :].rearrange("p (h n) -> p h n", h=2), bank[0:RANK, 6:8, 0:HALF],
                                 ACT.Copy).then_inc(glow_out, 1)
            split_hi(U_GL + 8)
            act.wait_ge(gprm, 32)
            for h in range(GH):
                act.wait_ge(gate_full, h + 1)
                if h:
                    act.wait_ge(cum_done, h)
                nc.scalar.activation(la.rearrange("p (h n) -> p h n", h=2), bank[:, 0:2, 0:HALF], ACT.Abs,
                                     bias=bg[:, h:h + 1]).then_inc(abs_done, 1)
                act.wait_ge(abs_done, 2 * h + 1)
                nc.scalar.activation(la, la, ACT.Exp, scale=-1.0).then_inc(abs_done, 1)
                act.wait_ge(abs_done, 2 * h + 2)
                nc.scalar.activation(la, la, ACT.Ln, bias=1.0).then_inc(ln_done, 1)
                act.wait_ge(cum_done, h + 1)
                if h:
                    act.wait_ge(dec_done, h)
                nc.scalar.activation(eb, cb, ACT.Exp, scale=1.0 / TAU).then_inc(ef_done, 1)
                nc.scalar.activation(fb, cb, ACT.Exp, scale=-1.0 / TAU).then_inc(ef_done, 1)
                split_hi(U_GR + 2 * h)
                split_hi(U_GR + 2 * h + 1)
            act.wait_ge(dec_done, GH)
            for m in range(2 * TILES):
                act.wait_ge(gv_full, m + 11)
                if m >= 4:
                    act.wait_ge(r_stored[m % 4], 16)
                nc.scalar.activation(r_piece(m), bank[:, 6 + (m + 1) % 2, :], ACT.Silu).then_inc(gv_out, 1)
                if m:
                    store_r(m - 1)
                if m == 3:
                    for u in range(U_GO, U_GO + 4):
                        split_hi(u)
            store_r(7)
            for u in range(U_GO + 4, U_GO + 8):
                split_hi(u)
            act.wait_ge(kt_full, 1)
            nc.scalar.activation(rbuf[0:META, 0:GH * P], bank[0:META, 0, :], ACT.Copy).then_inc(ktok_done, 1)

            def k_tokens(m):
                act.wait_ge(kt_full, m + 2)
                if m:
                    act.wait_ge(ua_full, m)
                    ub_wait(act, m - 1)
                act.wait_ge(at_done, m + 1)
                nc.scalar.activation(ktok, bank[:, 0, P:2 * P], ACT.Copy).then_inc(ktok_done, 1)

            def g_copy(what, t):
                m = gtp_at[(what, t)]
                act.wait_ge(gtp_full, m + 1)
                if what == "o":
                    nc.scalar.activation(xT_hi[:, :, cols(t)], ps_t[:, :, :], ACT.Copy).then_inc(gtp_hi, 1)
                else:
                    nc.scalar.activation(gv[:, t, :].rearrange("p (k n) -> p k n", k=KD), ps_t[:, :, :],
                                         ACT.Copy).then_inc(gtp_hi, 1)

            def store_h3(t):
                act.wait_ge(h3_ready, t + 1)
                act.dma_start(h3_d[cols(t), :], zrow[:, t % 2, :]).then_inc(h3_stored[t % 2], 16)

            k_tokens(0)
            for m in range(GM):
                t, h = divmod(m, GH)
                if m + 1 < GM:
                    k_tokens(m + 1)
                if h == 0 and t:
                    rsqrt(ssq[:, 1, :], ssq[:, 2, :])
                act.wait_ge(go_full, m + 1)
                o = o_at(t)[:, h * DV:(h + 1) * DV]
                nc.scalar.activation(o, bank[:, 4, 0:DV], ACT.Copy).then_inc(o_copied, 1)
                act.wait_ge(o_copied, m + 1)
                nc.scalar.activation(junk, o, ACT.Square, accum_out=ssq[:, 0, h:h + 1]).then_inc(sq_done, 1)
                act.wait_ge(sq_done, m + 1)
                if h == 0 and t >= 3:
                    store_h3(t - 3)
                    g_copy("h", t - 3)
                if h == 1 and t:
                    g_copy("o", t - 1)
                if h == 2 and t >= 2:
                    rsqrt(ln_st[:, 13:14], ln_st[:, 14:15])
                if h == 3 and t >= 2:
                    normalize(zrow[:, t % 2, :], ln_st[:, :])
            rsqrt(ssq[:, 1, :], ssq[:, 2, :])
            g_copy("o", TILES - 1)
            store_h3(TILES - 3)
            g_copy("h", TILES - 3)
            rsqrt(ln_st[:, 13:14], ln_st[:, 14:15])
            normalize(zrow[:, (TILES - 2) % 2, :], ln_st[:, :])
            for u in range(U_MOE1, U_MOE1 + RING):
                split_hi(u)
            store_h3(TILES - 2)
            g_copy("h", TILES - 2)
            rsqrt(ln_st[:, 13:14], ln_st[:, 14:15])
            normalize(zrow[:, (TILES - 1) % 2, :], ln_st[:, :])
            store_h3(TILES - 1)
            g_copy("h", TILES - 1)
            for b in range(2):
                act.wait_ge(h3_stored[b], 16 * (TILES // 2))
            moe_act(1, U_MOE1)
            act.wait_ge(h2_stored[1], 16 * TILES)

        @block.vector
        def _(dve):
            count, norms = [0], [0]

            def mark(ins):
                count[0] += 1
                return ins.then_inc(dve_order, 1)

            def settle():
                dve.wait_ge(dve_order, count[0])

            def split_lo(u):
                dve.wait_ge(hi_done, u + 1)
                nc.vector.tensor_tensor(split_unit(w_lo, u), raw_unit(u), split_unit(w_hi, u).bitcast(F32),
                                        ALU.subtract).then_inc(lo_done, 1)

            def x_lo(i):
                c, R = cols(order[i]), rows(order[i])
                dve.wait_ge(tp_hi, i + 1)
                nc.vector.tensor_tensor(xT_lo[:, :, c], ps_x[i % 2][:, :, 0:R], xT_hi[:, :, c].bitcast(F32),
                                        ALU.subtract).then_inc(tp_lo, 1)

            nc.vector.memset(xT_hi[:, :, L:XW].bitcast(F32), 0.0)
            nc.vector.memset(xT_lo[:, :, L:XW].bitcast(F32), 0.0)
            u = 0
            for i in range(len(order)):
                x_lo(i)
                if i >= 1:
                    split_lo(u)
                    u += 1
            while u < RING:
                split_lo(u)
                u += 1
            nc.vector.memset(kside[:], 0.0)
            nc.vector.memset(vside[:], 0.0)
            mark(nc.vector.memset(tpose[:], 0.0))
            settle()
            dve.wait_ge(cst, 12 + 3 * TILES)
            for t in range(TILES):
                nc.vector.memset(dist[:, t, P + META:P + CHUNK], BIG)
                d = dist[:, t, 0:P + META]
                mark(nc.vector.scalar_tensor_tensor(out=d, in0=d, scalar=-1.0, in1=d, op0=ALU.mult, op1=ALU.max))
            settle()
            for t in range(TILES):
                nc.vector.memset(dist[0:CHUNK, t, CHUNK:P], BIG)
                nc.vector.memset(dist[CHUNK:P, t, P + CHUNK:2 * P], BIG)
                if t == 0:
                    nc.vector.memset(dist[0:CHUNK, t, P + CHUNK:2 * P], BIG)
            mark(nc.vector.memset(ln_st[:], 1.0))
            settle()
            while u < 18:
                split_lo(u)
                u += 1
            dve.wait_ge(q_out, 10)
            for t in range(TILES):
                nc.vector.tensor_copy(kside[:, t, :, 0:META], kT[:, :, SEQ:L])
                if t:
                    nc.vector.tensor_copy(kside[:, t, :, CHUNK:P], kT[:, :, t * P - CHUNK:t * P])
            for i in range(len(order)):
                t = order[i]
                R = rows(t)
                dve.wait_ge(kv_full, i + 1)
                v = bank[:R, 4 + i % 2, 0:256]
                last = nc.vector.tensor_copy(v_sb[:R, t, :], v)
                if t == MT:
                    for s in range(TILES):
                        last = nc.vector.tensor_copy(vside[0:META, s, :], v)
                elif t + 1 < TILES:
                    last = nc.vector.tensor_copy(vside[CHUNK:P, t + 1, :], bank[CHUNK:P, 4 + i % 2, 0:256])
                last.then_inc(v_out, 1)
            dve.wait_ge(v_out, len(order))
            nc.vector.memset(sm_st[:], 0.0).then_inc(side_done, 1)
            dve.wait_ge(prm[0], 16)

            def front(n):
                i, t, g = steps[n]
                R, W, b = rows(t), width(t), n % 2
                st = sm_st[:R, b, :]
                dve.wait_ge(s_full, n + 1)
                if n >= 2:
                    dve.wait_ge(tp_full, tp_at[("p", n - 2)] + 1)
                dt = t if t != MT else 0
                for j in range(GQ):
                    slope = 2.0 ** (-8.0 * (GQ * g + j + 1) / NH)
                    last = nc.vector.scalar_tensor_tensor(out=prob[:R, b, j, 0:W], in0=dist[:R, dt, 0:W],
                                                          scalar=-slope, in1=ps_s[:R, j, 0:W], op0=ALU.mult,
                                                          op1=ALU.add)
                last.then_inc(s_read, 1)
                dve.wait_ge(s_read, n + 1)
                mark(nc.vector.tensor_reduce(st[:, 0:4], prob[:R, b, :, 0:W], X, ALU.max))
                settle()
                mark(nc.vector.tensor_tensor(st[:, 4:8], st[:, 0:4], sink_b[:R, GQ * g:GQ * g + GQ], ALU.max))
                settle()
                nc.vector.tensor_scalar(st[:, 8:12], st[:, 4:8], -1.0, None, ALU.mult)
                nc.vector.tensor_tensor(st[:, 12:16], sink_b[:R, GQ * g:GQ * g + GQ], st[:, 4:8],
                                        ALU.subtract).then_inc(front_done, 1)

            def back(n):
                i, t, g = steps[n]
                R, W, b = rows(t), width(t), n % 2
                st = sm_st[:R, b, :]
                dve.wait_ge(exp_done, n + 1)
                mark(nc.vector.tensor_tensor(st[:, 0:4], st[:, 16:20], st[:, 12:16], ALU.add))
                settle()
                mark(nc.vector.reciprocal(st[:, 4:8], st[:, 0:4]))
                settle()
                for j in range(GQ):
                    last = nc.vector.tensor_scalar(prob[:R, b, j, 0:W], prob[:R, b, j, 0:W], st[:, 4 + j:5 + j],
                                                   None, ALU.mult)
                last.then_inc(p_ready, 1)

            def o_split(n):
                i, t, g = steps[n]
                c = cols(t)
                dve.wait_ge(o_hi, n + 1)
                nc.vector.tensor_tensor(xT_lo[:, 2 * g:2 * g + 2, c], ps_o[:, :, 0:rows(t)],
                                        xT_hi[:, 2 * g:2 * g + 2, c].bitcast(F32), ALU.subtract).then_inc(o_lo, 1)

            def refine(v, r, t):
                norms[0] += 1
                dve.wait_ge(rstd_ready, norms[0])
                mark(nc.vector.reciprocal(r, r))
                settle()
                mark(nc.vector.scalar_tensor_tensor(out=t, in0=r, scalar=r, in1=v, op0=ALU.mult, op1=ALU.mult))
                settle()
                mark(nc.vector.tensor_scalar(t, t, -0.5, 1.5, ALU.mult, ALU.add))
                settle()
                mark(nc.vector.tensor_tensor(r, r, t, ALU.mult))
                settle()

            def refine4(v, r, t):
                norms[0] += 1
                dve.wait_ge(rstd_ready, norms[0])
                mark(nc.vector.reciprocal(r, r))
                settle()
                mark(nc.vector.tensor_tensor(t, r, r, ALU.mult))
                settle()
                mark(nc.vector.tensor_tensor(t, t, v, ALU.mult))
                settle()
                mark(nc.vector.tensor_scalar(t, t, -0.5, 1.5, ALU.mult, ALU.add))
                settle()
                mark(nc.vector.tensor_tensor(r, r, t, ALU.mult))
                settle()

            def moments(z, st):
                for c in range(2):
                    last = nc.vector.bn_stats(st[:, 6 * c:6 * c + 6], z[:, c * 512:(c + 1) * 512])
                mark(last)
                settle()
                mark(nc.vector.bn_aggr(st[:, 12:14], st[:, 0:12]))
                settle()
                nc.vector.tensor_scalar(st[:, 13:14], st[:, 13:14], LN_EPS, None, ALU.add).then_inc(var_ready, 1)

            def residual_moments(z, R, y, residual):
                residual(nc.vector.scalar_tensor_tensor(out=z, in0=z, scalar=ALPHA, in1=y, op0=ALU.mult, op1=ALU.add))
                st = ln_st[:R, :]
                moments(z, st)

            def centre(st):
                refine(st[:, 13:14], st[:, 14:15], st[:, 15:16])
                nc.vector.scalar_tensor_tensor(out=st[:, 15:16], in0=st[:, 12:13], scalar=-1.0, in1=st[:, 14:15],
                                               op0=ALU.mult, op1=ALU.mult).then_inc(centred, 1)

            def affine(z, R, n):
                dve.wait_ge(normed, n)
                mark(nc.vector.tensor_tensor(z, z, gb[:R, 0, :], ALU.mult))
                settle()
                return nc.vector.tensor_tensor(z, z, gb[:R, 1, :], ALU.add)

            def norm_attn(i):
                t = order[i]
                R = rows(t)
                if i >= 2:
                    dve.wait_ge(z_again[i % 2], 16 * (i // 2))
                if i < len(order) - 1:
                    dve.wait_ge(y_full, i + 1)
                else:
                    dve.wait_ge(ao_used, KD)

                def read(ins):
                    ins.then_inc(y_read, 1)
                    dve.wait_ge(y_read, i + 1)

                if i:
                    dve.wait_ge(normed, i)
                residual_moments(zrow[:R, i % 2, :], R, ps_y[:R, :, :].rearrange("p b n -> p (b n)"), read)

            front(0)
            front(1)
            dve.wait_ge(prm[2], 32)
            for n in range(NS):
                back(n)
                if n >= 1:
                    o_split(n - 1)
                if n < 2:
                    split_lo(18 + n)
                if n + 2 < NS:
                    front(n + 2)
                if n % NKV == 3 and n >= 7:
                    norm_attn(n // NKV - 1)
                if n % NKV == 0 and n >= 8:
                    centre(ln_st[:rows(order[n // NKV - 2]), :])
            o_split(NS - 1)
            centre(ln_st[:, :])
            for u in range(U_MOE0, U_MOE0 + RING):
                split_lo(u)
            norm_attn(len(order) - 1)
            centre(ln_st[:, :])
            i = len(order) - 1
            dve.wait_ge(h_ready, i)
            affine(zrow[:, i % 2, :], P, i + 1).then_inc(h_ready, 1)

            def lo_ahead(u0, b, j):
                r = RING + 6 * b + j
                s = (u0 + r) % RING
                dve.wait_ge(hi_done, u0 + r + 1 + 24 * turn[0])
                nc.vector.tensor_tensor(w_lo[:, s, :], w_raw[:, s, :], w_hi[:, s, :].bitcast(F32),
                                        ALU.subtract).then_inc(lo_done, 1)

            def first_max(v, m, c, oh):
                shape = list(v.shape)
                mark(nc.vector.tensor_reduce(m, v, X, ALU.max))
                settle()
                mark(nc.vector.tensor_tensor(c, v, m.to_broadcast(shape), ALU.is_equal))
                settle()
                mark(nc.vector.tensor_tensor(c, c, rev4[:].unsqueeze(1).to_broadcast(shape), ALU.mult))
                settle()
                mark(nc.vector.tensor_reduce(rt_m[:, 0:shape[1], :], c, X, ALU.max))
                settle()
                mark(nc.vector.tensor_tensor(oh, c, rt_m[:, 0:shape[1], :].to_broadcast(shape), ALU.is_equal))
                settle()

            def moe_dve(l, u0, logits):
                T = moe_tiles(l)
                NT = len(T)
                w = slice(0, NT)
                lg = rt_lg[:, w, :]
                mark(nc.vector.tensor_tensor(lg, logits,
                                             b_rt[:, l, :].unsqueeze(1).to_broadcast([P, NT, 20]), ALU.add))
                settle()
                first_max(lg[:, :, 0:NG], rt_g[:, w, :], rt_c[:, w, :], rt_ohg[:, w, :])
                nc.vector.tensor_tensor(rt_dg[:, w, :], lg[:, :, 0:NG], rt_g[:, w, :].to_broadcast([P, NT, NG]),
                                        ALU.subtract).then_inc(exp_asked, 1)
                mark(nc.vector.tensor_tensor(rt_pr[:, w], lg[:, :, NG:].rearrange("p t (g e) -> p t g e", g=NG),
                                             rt_ohg[:, w, :].unsqueeze(3).to_broadcast([P, NT, NG, EPG]), ALU.mult))
                settle()
                mark(nc.vector.tensor_reduce(rt_z[:, w, :], rt_pr[:, w].rearrange("p t g e -> p t e g"), X, ALU.add))
                settle()
                first_max(rt_z[:, w, :], rt_m1[:, w, :], rt_c[:, w, :], rt_oh[0][:, w, :])
                mark(nc.vector.scalar_tensor_tensor(out=rt_a[:, w, :], in0=rt_oh[0][:, w, :], scalar=-3e38,
                                                    in1=rt_z[:, w, :], op0=ALU.mult, op1=ALU.add))
                settle()
                first_max(rt_a[:, w, :], rt_m2[:, w, :], rt_c[:, w, :], rt_oh[1][:, w, :])
                nc.vector.tensor_tensor(rt_dm[:, w, :], rt_m2[:, w, :], rt_m1[:, w, :],
                                        ALU.subtract).then_inc(exp_asked, 1)
                for k in range(2):
                    last = nc.vector.tensor_tensor(rt_M[k][:, w, :].rearrange("p t (g e) -> p t g e", g=NG),
                                                   rt_ohg[:, w, :].unsqueeze(3).to_broadcast([P, NT, NG, EPG]),
                                                   rt_oh[k][:, w, :].unsqueeze(2).to_broadcast([P, NT, NG, EPG]),
                                                   ALU.mult)
                mark(last)
                settle()
                nc.vector.tensor_tensor(rt_Mb[:, w, :], rt_M[0][:, w, :], rt_M[1][:, w, :],
                                        ALU.add).then_inc(chosen, 1)
                for k in range(2):
                    M = rt_M[k][:, w, :]
                    for c in range(2):
                        nc.vector.tensor_tensor(entry[:, k, w, :, c], M, ids[:, w, c:c + 1].to_broadcast([P, NT, NE]),
                                                ALU.mult)
                    mark(nc.vector.tensor_scalar(entry[:, k, w, :, 2], M, float(k * L), None, ALU.mult))
                dve.wait_ge(rank_full, l + 1)
                mark(nc.vector.tensor_copy(rt_rank[:, 0:NT + 1, :], ps_rank[:, 0:NT + 1, :]))
                settle()
                for k in range(2):
                    mark(nc.vector.tensor_tensor((rt_q, rt_q2)[k][:, w, :], rt_rank[:, w, :], rt_M[k][:, w, :],
                                                 ALU.mult))
                settle()
                for k in range(2):
                    mark(nc.vector.tensor_reduce(rt_place[:, k, w].unsqueeze(2), (rt_q, rt_q2)[k][:, w, :], X,
                                                 ALU.add))
                settle()

                def fill(place, done):
                    for k in range(2):
                        for n in range(NT):
                            last = nc.vector.tensor_scalar(slots[:, k, n, :], slot_id[:], place[:, k, n:n + 1], None,
                                                           ALU.is_equal)
                    last.then_inc(done, 1)

                def read_tables(own, own_done):
                    tab = rt_q[:, 0:3, :].rearrange("p t (e c) -> p (t e c)", c=1).rearrange("p (e c) -> p e c", c=3)
                    own(nc.vector.tensor_copy(tab, ps_tab))
                    own_done()
                    own(nc.vector.tensor_tensor(tab[:, :, 1:2], tab[:, :, 0:1], tab[:, :, 1:2], ALU.add))
                    own_done()
                    own(nc.vector.tensor_scalar(idx[:, 0, :].unsqueeze(2), tab[:, :, 1:2], -1.0, None, ALU.add))
                    own_done()
                    nc.vector.scalar_tensor_tensor(out=idx[:, 1, :].unsqueeze(2), in0=tab[:, :, 1:2], scalar=-1.0,
                                                   in1=tab[:, :, 2:3], op0=ALU.add, op1=ALU.add
                                                   ).then_inc(idx_ready[l], 1)

                fill(rt_place, hot_ready)
                mark(nc.vector.tensor_reduce(rt_p[:, 0, 0:1], rt_rank[:, NT, :], X, ALU.max))
                settle()
                for j in range(1, ROUNDS):
                    mark(nc.vector.tensor_scalar(rt_c[:, 0, j - 1:j], rt_p[:, 0, 0:1], float(P * j), None, ALU.is_gt))
                settle()
                mark(nc.vector.tensor_reduce(rt_p[:, 0, 1:2], rt_c[:, 0, 0:ROUNDS - 1], X, ALU.add))
                settle()
                mark(nc.vector.tensor_copy(rounds[:], rt_p[:, 0, 1:2]))
                dve.wait_ge(tab_full[l], 1)
                read_tables(mark, settle)

                dve.wait_ge(exp_given, 2 * l + 2)
                mark(nc.vector.tensor_reduce(rt_gt[:, w, :], rt_dg[:, w, :], X, ALU.add))
                mark(nc.vector.tensor_scalar(rt_m[:, w, :], rt_dm[:, w, :], 1.0, None, ALU.add))
                settle()
                mark(nc.vector.tensor_tensor(rt_gt[:, w, :], rt_gt[:, w, :], rt_m[:, w, :], ALU.mult))
                settle()
                mark(nc.vector.reciprocal(wgt[:, w, 0:1], rt_gt[:, w, :]))
                settle()
                mark(nc.vector.tensor_tensor(wgt[:, w, 1:2], wgt[:, w, 0:1], rt_dm[:, w, :], ALU.mult))
                def x_low(b):
                    c = slice((b % 2) * P, (b % 2) * P + P)
                    dve.wait_ge(x_hi_done, NE * l + B(b) + 1)
                    nc.vector.tensor_tensor(xT_lo[:, :, c], ps_t[:, :, :], xT_hi[:, :, c].bitcast(F32),
                                            ALU.subtract).then_inc(x_lo_done, 1)

                x_low(0)

                def step(b):
                    dve.wait_ge(silu_done, NE * l + B(b) + 1)
                    if b >= 2:
                        dve.wait_ge(ht_full, NE * l + B(b) - 1)
                    nc.vector.tensor_tensor(hid[:, b % 2, :], sil[:, b % 2, :], ps_gu[:, FE:2 * FE],
                                            ALU.mult).then_inc(mul_done, 1)
                    if b + 1 < NE:
                        x_low(b + 1)
                    js = [j for j in range(6) if l == 0 or 8 + 6 * b + j < 6 * NE]
                    if b == NE - 1:
                        js = [j for j in js if j < 4]
                    dve.wait_ge(h_hi_done, NE * l + B(b) + 1)
                    c = slice((2 + b % 2) * P, (3 + b % 2) * P)
                    nc.vector.tensor_tensor(xT_lo[:, 0:KF, c], ps_h[:, :, :], xT_hi[:, 0:KF, c].bitcast(F32),
                                            ALU.subtract).then_inc(h_lo_done, 1)
                    for j in js:
                        lo_ahead(u0, b, j)

                moe_steps(dve, step)

                def start(r):
                    n_own = [5 * (r - 1)]

                    def own(ins):
                        n_own[0] += 1
                        ins.then_inc(ov_set[l], 1)

                    def own_done():
                        dve.wait_ge(ov_set[l], n_own[0])

                    if r > 1:
                        dve.wait_ge(ov_s[l], 16 * NE * (r - 1))
                    else:
                        for b in range(2):
                            dve.wait_ge(y_stored[b], Y_COUNT * (l + 1))
                    own(nc.vector.tensor_scalar(rt_round[:, :, w], rt_place[:, :, w], float(P * r), None, ALU.subtract))
                    own_done()
                    n_own[0] += 1
                    fill(rt_round, ov_set[l])
                    dve.wait_ge(tab_full[l], r + 1)
                    read_tables(own, own_done)

                def more(r, e):
                    q = e + NE * (r - 1)
                    dve.wait_ge(ov_act[l], 4 * q + 2)
                    nc.vector.tensor_tensor(hid[:, 0, :], sil[:, 0, :], ps_gu[:, FE:2 * FE],
                                            ALU.mult).then_inc(ov_dve[l], 1)

                further(dve, l, more, start=start)
                for b in range(2):
                    dve.wait_ge(y_stored[b], Y_COUNT * (l + 1))

                def low(n):
                    t = T[n]
                    dve.wait_ge(h2_hi, n + 1)
                    nc.vector.tensor_tensor(xT_lo[:, :, cols(t)], ps_t[:, :, 0:rows(t)],
                                            xT_hi[:, :, cols(t)].bitcast(F32), ALU.subtract).then_inc(h2_lo, 1)

                if l == 0:
                    split_lo(U_GV + 6)
                    split_lo(U_GV + 7)
                for n in range(NT):
                    R = rows(T[n])
                    z, st = z_rows(n)[:R], comb_st[:R, n % 2, :]
                    y0, y1 = (y_rows(n, k)[:R] for k in range(2))
                    dve.wait_ge(weighed, len(order) * l + n + 1)
                    mark(nc.vector.scalar_tensor_tensor(out=y0, in0=y1, scalar=wgt[:R, n, 1:2], in1=y0, op0=ALU.mult, op1=ALU.add))
                    settle()
                    nc.vector.scalar_tensor_tensor(out=z, in0=z, scalar=ALPHA, in1=y0, op0=ALU.mult,
                                                   op1=ALU.add).then_inc(comb_used, 1)
                    dve.wait_ge(comb_used, len(order) * l + n + 1)
                    moments(z, st)
                    if l == 0 and n >= 2:
                        low(n - 2)
                    centre(st)
                dve.wait_ge(h2_ready[l], NT - 1)
                affine(z_rows(NT - 1)[:rows(T[-1])], rows(T[-1]), norms_before[l] + NT).then_inc(h2_ready[l], 1)
                if l == 0:
                    low(NT - 2)
                    low(NT - 1)

            dve.wait_ge(rt_full, len(order))
            moe_dve(0, U_MOE0, ps_r[:, 0:RTW * 20].rearrange("p (t e) -> p t e", e=20))

            dve.wait_ge(h2_stored[0], 16 * len(order))
            mark(nc.vector.memset(scan0, 1.0))
            settle()
            mark(nc.vector.memset(scan0[:, 0:L:CHUNK], 0.0))
            settle()
            for u in range(U_GL, U_GR):
                split_lo(u)
            dve.wait_ge(gprm, 32)
            for h in range(GH):
                dve.wait_ge(abs_done, 2 * h + 1)
                nc.vector.tensor_scalar(lm.rearrange("p (h n) -> p h n", h=2), bank[:, 0:2, 0:HALF], bg[:, h:h + 1],
                                        0.0, ALU.add, ALU.min).then_inc(lm_done, 1)
                dve.wait_ge(lm_done, h + 1)
                dve.wait_ge(ln_done, h + 1)
                mark(nc.vector.tensor_tensor(lm, lm, la, ALU.subtract))
                settle()
                if h:
                    dve.wait_ge(ef_done, 2 * h)
                nc.vector.tensor_tensor_scan(cb, scan0, lm, 0.0, ALU.mult, ALU.add).then_inc(cum_done, 1)
                dve.wait_ge(qk_full, 2 * h + 1)
                dve.wait_ge(ef_done, 2 * h + 1)
                for c in range(2):
                    s = slice(c * HALF, (c + 1) * HALF)
                    last = nc.vector.scalar_tensor_tensor(out=qdec[:, h, s], in0=bank[:, 2 + c, 0:HALF],
                                                          scalar=DK ** -0.5, in1=eb[:, s], op0=ALU.mult, op1=ALU.mult)
                last.then_inc(qd_done, 1)
                dve.wait_ge(qk_full, 2 * h + 2)
                dve.wait_ge(ef_done, 2 * h + 2)
                for c in range(2):
                    s = slice(c * HALF, (c + 1) * HALF)
                    nc.vector.tensor_tensor(kinv[:, h, s], bank[:, 4 + c, 0:HALF], fb[:, s], ALU.mult)
                nc.vector.tensor_copy(dec[:, h, 0:GCH], eb[:, CHUNK - 1:SEQ:CHUNK])
                nc.vector.tensor_copy(dec[:, h, GCH:], eb[:, L - 1:L]).then_inc(dec_done, 1)
                split_lo(U_GR + 2 * h)
                split_lo(U_GR + 2 * h + 1)
            nc.vector.memset(at_sb, 0.0)
            dve.wait_ge(gb_ng, 16)
            for c in range(2):
                for m in range(4 * c, 4 * c + 4):
                    dve.wait_ge(gv_out, 11 + m)
                    nc.vector.tensor_tensor(r_piece(m), r_piece(m), gb[:, 0, 512 * c:512 * c + 512],
                                            ALU.mult).then_inc(r_ready, 1)
                for u in range(U_GO + 4 * c, U_GO + 4 * c + 4):
                    split_lo(u)

            def keys_to_end(m):
                t, h = divmod(m, GH)
                if m:
                    dve.wait_ge(kt_full, m + 1)
                nc.vector.tensor_tensor(kend.rearrange("p (c n) -> p c n", c=2),
                                        kinv[:, h, cols(t)].rearrange("p (c n) -> p c n", c=2),
                                        dec[:, h, 2 * t:2 * t + 2].unsqueeze(2).to_broadcast([P, 2, CHUNK]),
                                        ALU.mult).then_inc(kend_done, 1)

            def causal_scores(m):
                dve.wait_ge(kt_full, m + 2)
                if m >= 2:
                    dve.wait_ge(go_full, m - 1)
                nc.vector.copy_predicated(at_sb[:, m % 2, :], causal[:].bitcast(mybir.dt.uint16), bank[:, 0, 0:P]
                                          ).then_inc(at_done, 1)

            dve.wait_ge(dec_done, GH)
            keys_to_end(0)
            for h in range(GH):
                dve.wait_ge(um_full, h + 1)
                nc.vector.tensor_scalar(state[:, h, :], bank[:, (1, 5)[h % 2], 0:DV], dec[:, h, GCH:], None,
                                        ALU.mult).then_inc(sb_done, 1)
            causal_scores(0)

            def g_var():
                nc.vector.tensor_scalar(ssq[:, 1, :], ssq[:, 0, :], 1.0 / DV, RMS_EPS, ALU.mult,
                                        ALU.add).then_inc(var_ready, 1)

            def g_gate(t):
                refine4(ssq[:, 1, :], ssq[:, 2, :], ln_st[:, 16:20])
                dve.wait_ge(r_landed, 16 * (t + 1))
                for h in range(GH):
                    o, s = o_at(t)[:, h * DV:(h + 1) * DV], slice(h * DV, (h + 1) * DV)
                    last = nc.vector.scalar_tensor_tensor(out=o, in0=o, scalar=ssq[:, 2, h:h + 1], in1=rbuf[:, s],
                                                          op0=ALU.mult, op1=ALU.mult)
                last.then_inc(gated, 1)

            def g_low(t):
                dve.wait_ge(gtp_hi, gtp_at[("o", t)] + 1)
                nc.vector.tensor_tensor(xT_lo[:, :, cols(t)], ps_t[:, :, :], xT_hi[:, :, cols(t)].bitcast(F32),
                                        ALU.subtract).then_inc(gtp_lo, 1)

            def norm_gla(t):
                dve.wait_ge(z_landed[t % 2], 16 * (t // 2 + 1))
                if t < TILES - 1:
                    dve.wait_ge(gy_full, t + 1)
                else:
                    dve.wait_ge(go_used, KD)

                def read(ins):
                    ins.then_inc(gy_read, 1)
                    dve.wait_ge(gy_read, t + 1)

                if t:
                    dve.wait_ge(normed, 2 * len(order) + t)
                residual_moments(zrow[:, t % 2, :], P, ps_y[:, :, :].rearrange("p b n -> p (b n)"), read)

            def g_logits(t):
                dve.wait_ge(lg_full, t + 1)
                nc.vector.tensor_copy(lg_sb[:, t, :], bank[:, 2, 0:NG + NE]).then_inc(lg_read, 1)

            for m in range(GM):
                t, h = divmod(m, GH)
                if h == 0 and t:
                    dve.wait_ge(sq_done, m)
                    g_var()
                if m + 1 < GM:
                    keys_to_end(m + 1)
                S = state[:, h, :]
                dve.wait_ge(o_part, m + 1)
                dve.wait_ge(ua_full, m + 1)
                nc.vector.scalar_tensor_tensor(out=S, in0=S, scalar=dec[:, h, 2 * t:2 * t + 1], in1=bank[:, 1, 0:DV],
                                               op0=ALU.mult, op1=ALU.add).then_inc(sa_done, 1)
                if m + 1 < GM:
                    causal_scores(m + 1)
                if t < TILES - 1:
                    ub_wait(dve, m)
                    dve.wait_ge(go_full, m + 1)
                    nc.vector.scalar_tensor_tensor(out=S, in0=S, scalar=dec[:, h, 2 * t + 1:2 * t + 2],
                                                   in1=bank[:, 5, 0:DV], op0=ALU.mult, op1=ALU.add
                                                   ).then_inc(sb_done, 1)
                if h == 0 and t:
                    g_gate(t - 1)
                    if t == 1:
                        dve.wait_ge(gb_l3, 32)
                    if t == 3:
                        g_logits(0)
                if h == 1 and t:
                    g_low(t - 1)
                if h == 2 and t >= 2:
                    norm_gla(t - 2)
                if h == 3 and t >= 2:
                    centre(ln_st[:, :])
            dve.wait_ge(sq_done, GM)
            g_var()
            g_gate(TILES - 1)
            g_low(TILES - 1)
            norm_gla(TILES - 2)
            g_logits(TILES - 3)
            centre(ln_st[:, :])
            for u in range(U_MOE1, U_MOE1 + RING):
                split_lo(u)
            norm_gla(TILES - 1)
            centre(ln_st[:, :])
            dve.wait_ge(h3_ready, TILES - 1)
            affine(zrow[:, (TILES - 1) % 2, :], P, norms_before[1]).then_inc(h3_ready, 1)
            for t in (TILES - 2, TILES - 1):
                g_logits(t)
            dve.wait_ge(lg_read, TILES)
            moe_dve(1, U_MOE1, lg_sb[:, 0:TILES, :])

        @block.tensor
        def _(pe):
            def tp_free(m):
                if m:
                    pe.wait_ge(tp_hi, m)
                if 0 < m <= len(order):
                    pe.wait_ge(tp_lo, m)

            pe.wait_ge(cst, 5)
            for i in range(len(order)):
                t = order[i]
                R = rows(t)
                pe.wait_ge(x_landed[i], 16)
                if i >= 2:
                    pe.wait_ge(tp_hi, i - 1)
                    pe.wait_ge(tp_lo, i - 1)
                for k in range(KD):
                    last = nc.tensor.transpose(ps_x[i % 2][:, k, 0:R], x_rows(i)[:R, k * P:(k + 1) * P], ident[:R, :R])
                last.then_inc(tp_full, 1)
            pe.wait_ge(tp_lo, len(order))

            def three(acc, a_hi, a_lo, b_hi, b_lo, first, last):
                nc.tensor.matmul(acc, a_hi, b_hi, start=first, stop=False)
                nc.tensor.matmul(acc, a_lo, b_hi, start=False, stop=False)
                return nc.tensor.matmul(acc, a_hi, b_lo, start=False, stop=last)

            for f in range(10):
                if f < 8:
                    ua = 2 * (f // 2)
                    pe.wait_ge(lo_done, ua + 2)

                    def stat(w, k):
                        return w[:, ua % RING + f % 2, k * P:(k + 1) * P]
                else:
                    ua = U_K + f - 8
                    pe.wait_ge(lo_done, ua + 1)

                    def stat(w, k):
                        return w[:, ua % RING, k * P:(k + 1) * P]
                if f >= 2:
                    pe.wait_ge(q_out, f - 1)
                for h in range(2):
                    for k in range(KD):
                        c = slice(h * HALF, (h + 1) * HALF)
                        last = three(ps_q[f % 2][:, h, 0:HALF], stat(w_hi, k), stat(w_lo, k), xT_hi[:, k, c],
                                     xT_lo[:, k, c], k == 0, k == KD - 1)
                last.then_inc(q_full, 1)
            pe.wait_ge(lo_done, U_V + 2)
            for i in range(len(order)):
                t = order[i]
                if i >= 2:
                    pe.wait_ge(v_out, i - 1)
                for k in range(KD):
                    s = (U_V + k // 4) % RING
                    c = slice(t * P, t * P + P)
                    w = slice(256 * (k % 4), 256 * (k % 4) + 256)
                    last = three(bank[:, 4 + i % 2, 0:256], xT_hi[:, k, c], xT_lo[:, k, c], w_hi[:, s, w],
                                 w_lo[:, s, w], k == 0, k == KD - 1)
                last.then_inc(kv_full, 1)

            def scores(n):
                i, t, g = steps[n]
                R = rows(t)
                if n:
                    pe.wait_ge(s_read, n)
                for j in range(GQ):
                    h = GQ * g + j
                    f, base = 4 * (g // 2) + j, 64 * (g % 2)
                    q = qT[base:base + HD, f, cols(t)]
                    last = nc.tensor.matmul(ps_s[:R, j, 0:R], q, kT[base:base + HD, g // 2, cols(t)],
                                            start=True, stop=True)
                    if t != MT:
                        last = nc.tensor.matmul(ps_s[:R, j, P:2 * P], q, kside[base:base + HD, t, g // 2, :],
                                                start=True, stop=True)
                last.then_inc(s_full, 1)

            def out_part(i, g):
                t = order[i]
                if g == 0 and i:
                    pe.wait_ge(y_read, i)
                pe.wait_ge(o_lo, NKV * i + g + 1)
                for k in (2 * g, 2 * g + 1):
                    pe.wait_ge(lo_done, U_AO + k + 1)
                    s = (U_AO + k) % RING
                    c = slice(t * P, t * P + P)
                    for h in range(2):
                        w = slice(512 * h, 512 * h + 512)
                        last = three(ps_y[:, h, :], xT_hi[:, k, c], xT_lo[:, k, c], w_hi[:, s, w], w_lo[:, s, w],
                                     k == 0, k == KD - 1)
                    if i == len(order) - 1:
                        last.then_inc(ao_used, 1)
                if g == NKV - 1 and i < len(order) - 1:
                    last.then_inc(y_full, 1)

            def p_transpose(n):
                i, t, g = steps[n]
                R = rows(t)
                pe.wait_ge(p_ready, n + 1)
                tp_free(tp_at[("p", n)])
                for j in range(GQ):
                    for b in range(blocks(t)):
                        w = min(P, width(t))
                        last = nc.tensor.transpose(ps_t[:w, 2 * j + b, 0:R], prob[:R, n % 2, j, P * b:P * b + w],
                                                   ident[:R, :R])
                last.then_inc(tp_full, 1)

            def values(n):
                i, t, g = steps[n]
                R = rows(t)
                m = tp_at[("p", n)]
                pe.wait_ge(tp_hi, m + 1)
                if n:
                    pe.wait_ge(o_lo, n)
                for j in range(GQ):
                    base = 64 * (j % 2)
                    o = ps_o[base:base + HD, j // 2, 0:R]
                    K = META if t == MT else P
                    last = nc.tensor.matmul(o, v_sb[:K, t, g * HD:(g + 1) * HD], tpose[:K, 2 * j, 0:R],
                                            start=True, stop=(t == MT))
                    if t != MT:
                        last = nc.tensor.matmul(o, vside[:, t, g * HD:(g + 1) * HD], tpose[:, 2 * j + 1, 0:R],
                                                start=False, stop=True)
                last.then_inc(o_full, 1)

            def h_transpose(j):
                R = rows(order[j])
                pe.wait_ge(h_ready, j + 1)
                tp_free(tp_at[("h", j)])
                for k in range(KD):
                    last = nc.tensor.transpose(ps_t[:, k, 0:R], zrow[:R, j % 2, k * P:(k + 1) * P], ident[:R, :R])
                last.then_inc(tp_full, 1)

            def route(j):
                pe.wait_ge(tp_hi, tp_at[("h", j)] + 1)
                t = order[j]
                for k in range(KD):
                    last = nc.tensor.matmul(ps_r[:, t * 20:t * 20 + 20], tpose[:, k, :], w_rt[:, 0, k, :],
                                            start=(k == 0), stop=(k == KD - 1))
                last.then_inc(rt_full, 1)

            pe.wait_ge(side_done, 1)
            scores(0)
            scores(1)
            pe.wait_ge(prm[1], 16 * 7)
            for n in range(NS):
                i, t, g = steps[n]
                if n + 2 < NS:
                    scores(n + 2)
                p_transpose(n)
                if i:
                    out_part(i - 1, g)
                values(n)
                if n % NKV == 2 and n >= 10:
                    h_transpose(n // NKV - 2)
                    route(n // NKV - 2)
            for g in range(NKV):
                out_part(len(order) - 1, g)
            for j in (len(order) - 2, len(order) - 1):
                h_transpose(j)
                route(j)

            def moe_pe(l, u0):
                T = moe_tiles(l)
                NT = len(T)
                pe.wait_ge(chosen, l + 1)
                for n in range(NT):
                    for m in range(n + 1):
                        K = rows(T[m])
                        last = nc.tensor.matmul(ps_rank[:, n, :], (tri if m == n else ones)[:K, :], rt_Mb[:K, m, :],
                                                start=(m == 0), stop=(m == n))
                for m in range(NT):
                    K = rows(T[m])
                    last = nc.tensor.matmul(ps_rank[:, NT, :], ones[:K, :], rt_Mb[:K, m, :], start=(m == 0),
                                            stop=(m == NT - 1))
                last.then_inc(rank_full, 1)
                def tables():
                    for k in range(2):
                        for n in range(NT):
                            K = rows(T[n])
                            last = nc.tensor.matmul(ps_tab.rearrange("p e c -> p (e c)"), slots[:K, k, n, :],
                                                    entry[:K, k, n, :, :].rearrange("p e c -> p (e c)"),
                                                    start=(k == 0 and n == 0), stop=(k == 1 and n == NT - 1))
                    last.then_inc(tab_full[l], 1)

                pe.wait_ge(hot_ready, l + 1)
                tables()

                def x_turn(b):
                    pe.wait_ge(gathered[b % 2], 8 * NE * l + 16 * (B2(b) + 1))
                    if b:
                        pe.wait_ge(x_lo_done, NE * l + B(b))
                    for k in range(KD):
                        last = nc.tensor.transpose(ps_t[:, k, :], xg[:, b % 2, k * P:(k + 1) * P], ident[:])
                    last.then_inc(xt_full, 1)

                def gate_up(b, r):
                    pe.wait_ge(x_lo_done, NE * l + B(b) + 1)
                    if b:
                        pe.wait_ge(mul_done, NE * l + B(b))
                    c = slice((b % 2) * P, (b % 2) * P + P)
                    for j in range(4):
                        s = (u0 + r + j) % RING
                        pe.wait_ge(lo_done, u0 + r + j + 1 + 24 * turn[0])
                        for i in range(2):
                            k = 2 * j + i
                            w = slice(512 * i, 512 * i + 512)
                            last = three(ps_gu, xT_hi[:, k, c], xT_lo[:, k, c], w_hi[:, s, w], w_lo[:, s, w],
                                         k == 0, k == KD - 1)
                        last.then_inc(gu_used, 1)

                def h_turn(b):
                    pe.wait_ge(mul_done, NE * l + B(b) + 1)
                    if b:
                        pe.wait_ge(h_lo_done, NE * l + B(b))
                    for f in range(KF):
                        last = nc.tensor.transpose(ps_h[:, f, :], hid[:, b % 2, f * P:(f + 1) * P], ident[:])
                    last.then_inc(ht_full, 1)

                def down(b, r):
                    pe.wait_ge(h_lo_done, NE * l + B(b) + 1)
                    if b:
                        pe.wait_ge(y_out, NE * l + B(b))
                    c = slice((2 + b % 2) * P, (3 + b % 2) * P)
                    for f in range(KF):
                        s = (u0 + r + f) % RING
                        pe.wait_ge(lo_done, u0 + r + f + 1 + 24 * turn[0])
                        for h in range(2):
                            w = slice(512 * h, 512 * h + 512)
                            last = three(ps_y[:, h, :], xT_hi[:, f, c], xT_lo[:, f, c], w_hi[:, s, w], w_lo[:, s, w],
                                         f == 0, f == KF - 1)
                        last.then_inc(dn_used, 1)

                x_turn(0)
                gate_up(0, 0)

                def step(b):
                    r = step_unit(b)
                    if b + 1 < NE:
                        x_turn(b + 1)
                    if b:
                        down(b - 1, r)
                        r += 2
                    h_turn(b)
                    if b + 1 < NE:
                        gate_up(b + 1, r)

                moe_steps(pe, step)
                down(NE - 1, 6 * NE - 2)

                def more(r, e):
                    q = e + NE * (r - 1)
                    pe.wait_ge(ov_g[l], 16 * q + 16)
                    for k in range(KD):
                        last = nc.tensor.transpose(ps_t[:, k, :], ov_y[:, k * P:(k + 1) * P], ident[:])
                    last.then_inc(ov_pe[l], 1)
                    pe.wait_ge(ov_act[l], 4 * q + 1)
                    pe.wait_ge(ov_w[l], 64 * q + 64)
                    for k in range(KD):
                        last = nc.tensor.matmul(ps_gu, ov_xT[:, k, :], ov_gu[:, k, :, :].rearrange("p m c -> p (m c)"),
                                                start=(k == 0), stop=(k == KD - 1))
                    last.then_inc(ov_pe[l], 1)
                    pe.wait_ge(ov_dve[l], q + 1)
                    for f in range(KF):
                        last = nc.tensor.transpose(ps_h[:, f, :], hid[:, 0, f * P:(f + 1) * P], ident[:])
                    last.then_inc(ov_pe[l], 1)
                    pe.wait_ge(ov_act[l], 4 * q + 3)
                    for f, dn in enumerate(ov_dn):
                        for h in range(2):
                            last = nc.tensor.matmul(ps_y[:, h, :], ov_hT[:, f, :], dn[:, 512 * h:512 * h + 512],
                                                    start=(f == 0), stop=(f == KF - 1))
                    last.then_inc(ov_pe[l], 1)

                def start(r):
                    pe.wait_ge(ov_set[l], 5 * (r - 1) + 2)
                    tables()

                further(pe, l, more, start=start)

            moe_pe(0, U_MOE0)

            def g_project(n, t, u0):
                pe.wait_ge(lo_done, u0 + 4)
                if n > 2:
                    pe.wait_ge(gv_out, n - 2)
                for k in range(KD):
                    s = (u0 + k // 2) % RING
                    w = slice(512 * (k % 2), 512 * (k % 2) + 512)
                    c = slice(t * P, t * P + P)
                    last = three(bank[:, 6 + n % 2, :], xT_hi[:, k, c], xT_lo[:, k, c], w_hi[:, s, w], w_lo[:, s, w],
                                 k == 0, k == KD - 1)
                last.then_inc(gv_full, 1)

            def g_values(i):
                pe.wait_ge(h2_lo, i + 1)
                for c in range(2):
                    g_project(2 * i + c + 1, moe_tiles(0)[i], U_GV + 4 * c)

            for n, t in enumerate(moe_tiles(0)):
                R = rows(t)
                pe.wait_ge(h2_ready[0], n + 1)
                if n:
                    pe.wait_ge(h2_lo, n)
                for k in range(KD):
                    last = nc.tensor.transpose(ps_t[:, k, 0:R], z_rows(n)[:R, k * P:(k + 1) * P], ident[:R, :R])
                last.then_inc(h2_tp, 1)
                if n:
                    g_values(n - 1)
            g_values(TILES)

            pe.wait_ge(gv_out, 10)
            pe.wait_ge(lo_done, U_GL + 1)
            for h in range(2):
                for k in range(KD):
                    c, s = slice(h * HALF, (h + 1) * HALF), U_GL % RING
                    w = slice(k * P, (k + 1) * P)
                    last = three(ps_y[:, h, 0:HALF], w_hi[:, s, w], w_lo[:, s, w], xT_hi[:, k, c], xT_lo[:, k, c],
                                 k == 0, k == KD - 1)
            last.then_inc(glow_full, 1)
            pe.wait_ge(gprm, 32)
            pe.wait_ge(glow_out, 1)
            for h in range(GH):
                if h:
                    pe.wait_ge(lm_done, h)
                for c in range(2):
                    last = nc.tensor.matmul(bank[:, c, 0:HALF], gup[:, h * P:(h + 1) * P],
                                            gl_t[0:RANK, c * HALF:(c + 1) * HALF], start=True, stop=True)
                last.then_inc(gate_full, 1)
                for i in range(2):
                    u = U_GL + 1 + 2 * h + i
                    pe.wait_ge(lo_done, u + 1)
                    if h:
                        pe.wait_ge((qd_done, dec_done)[i], h)
                    for c in range(2):
                        for k in range(KD):
                            w = slice(k * P, (k + 1) * P)
                            n = slice(c * HALF, (c + 1) * HALF)
                            last = three(bank[:, 2 + 2 * i + c, 0:HALF], w_hi[:, u % RING, w], w_lo[:, u % RING, w],
                                         xT_hi[:, k, n], xT_lo[:, k, n], k == 0, k == KD - 1)
                    last.then_inc(qk_full, 1)
            for c in range(2):
                for t in range(TILES):
                    g_project(4 * c + t + 11, t, U_GR + 4 * c)
            pe.wait_ge(dec_done, GH)
            for h in range(GH):
                last = nc.tensor.transpose(bank[0:META, 0, h * P:(h + 1) * P], kinv[:, h, SEQ:L], ident[:])
            last.then_inc(kt_full, 1)
            pe.wait_ge(ktok_done, 1)
            pe.wait_ge(gv_out, 18)
            for h in range(GH):
                if h >= 2:
                    pe.wait_ge(sb_done, h - 1)
                nc.tensor.matmul(bank[:, (1, 5)[h % 2], 0:DV], rbuf[0:META, h * P:(h + 1) * P],
                                 vm[:, h * DV:(h + 1) * DV], start=True, stop=True).then_inc(um_full, 1)

            def g_scores(m):
                t, h = divmod(m, GH)
                if m:
                    pe.wait_ge(at_done, m)
                    pe.wait_ge(ktok_done, m + 1)
                nc.tensor.matmul(bank[:, 0, 0:P], kinv[:, h, cols(t)], qdec[:, h, cols(t)], start=True, stop=True)
                pe.wait_ge(kend_done, m + 1)
                nc.tensor.transpose(bank[:, 0, P:2 * P], kend, ident[:]).then_inc(kt_full, 1)

            def g_step(m):
                t, h = divmod(m, GH)
                a, b = (slice(t * P + c * CHUNK, t * P + c * CHUNK + CHUNK) for c in range(2))
                v = slice(h * DV, (h + 1) * DV)
                S = state[:, h, :]
                O = bank[:, 4, 0:DV]
                pe.wait_ge(at_done, m + 1)
                if m:
                    pe.wait_ge(o_copied, m)
                nc.tensor.matmul(O, at_sb[:, m % 2, :], gv[:, t, v], start=True, stop=False)
                pe.wait_ge(sb_done, m + 1)
                nc.tensor.matmul(O[0:CHUNK], qdec[:, h, a], S, start=False, stop=True).then_inc(o_part, 1)
                pe.wait_ge(ktok_done, m + 2)
                pe.wait_ge(sb_done, GH)
                if m:
                    pe.wait_ge(sa_done, m)
                nc.tensor.matmul(bank[:, 1, 0:DV], ktok[0:CHUNK, :], gv[0:CHUNK, t, v], start=True,
                                 stop=True).then_inc(ua_full, 1)
                if t < TILES - 1:
                    pe.wait_ge(sb_done, GH + m)
                    nc.tensor.matmul(bank[:, 5, 0:DV], ktok[CHUNK:P, :], gv[CHUNK:P, t, v], start=True,
                                     stop=True).then_inc(ub_full, 1)
                if m + 1 < GM:
                    g_scores(m + 1)
                pe.wait_ge(sa_done, m + 1)
                nc.tensor.matmul(O[CHUNK:P], qdec[:, h, b], S, start=False, stop=True).then_inc(go_full, 1)

            def g_free(m):
                if m:
                    n_o = len([k for k in gtp_order[:m] if k[0] == "o"])
                    pe.wait_ge(gtp_hi, m)
                    pe.wait_ge(gtp_lo, n_o)
                    if m > n_o:
                        pe.wait_ge(lg_read, m - n_o)

            def g_turn_o(t):
                pe.wait_ge(gated, t + 1)
                g_free(gtp_at[("o", t)])
                for k in range(KD):
                    last = nc.tensor.transpose(ps_t[:, k, :], o_at(t)[:, k * P:(k + 1) * P], ident[:])
                last.then_inc(gtp_full, 1)

            def g_out(t, ks):
                if ks[0] == 0:
                    pe.wait_ge(gtp_lo, t + 1)
                    if t:
                        pe.wait_ge(gy_read, t)
                for k in ks:
                    pe.wait_ge(lo_done, U_GO + k + 1)
                    s = (U_GO + k) % RING
                    for h in range(2):
                        w = slice(512 * h, 512 * h + 512)
                        last = three(ps_y[:, h, :], xT_hi[:, k, cols(t)], xT_lo[:, k, cols(t)], w_hi[:, s, w],
                                     w_lo[:, s, w], k == 0, k == KD - 1)
                    if t == TILES - 1:
                        last.then_inc(go_used, 1)
                    elif k == KD - 1:
                        last.then_inc(gy_full, 1)

            def g_turn_h(t):
                pe.wait_ge(h3_ready, t + 1)
                g_free(gtp_at[("h", t)])
                for k in range(KD):
                    last = nc.tensor.transpose(ps_t[:, k, :], zrow[:, t % 2, k * P:(k + 1) * P], ident[:])
                last.then_inc(gtp_full, 1)
                pe.wait_ge(gtp_hi, gtp_at[("h", t)] + 1)
                for k in range(KD):
                    last = nc.tensor.matmul(bank[:, 2, 0:NG + NE], gv[:, t, k * P:(k + 1) * P], w_rt[:, 1, k, :],
                                            start=(k == 0), stop=(k == KD - 1))
                last.then_inc(lg_full, 1)

            g_scores(0)
            pe.wait_ge(prm[3], 16 * 7)
            for m in range(GM):
                t, h = divmod(m, GH)
                g_step(m)
                if h < 2 and t >= 2:
                    g_out(t - 2, (2 * h + 4, 2 * h + 5))
                if h >= 2 and t:
                    g_out(t - 1, (2 * h - 4, 2 * h - 3))
                if h == 0 and t >= 3:
                    g_turn_h(t - 3)
                if h == 1 and t:
                    g_turn_o(t - 1)
            g_out(TILES - 2, (4, 5, 6, 7))
            g_turn_o(TILES - 1)
            g_turn_h(TILES - 3)
            g_out(TILES - 1, tuple(range(KD)))
            for t in (TILES - 2, TILES - 1):
                g_turn_h(t)
            moe_pe(1, U_MOE1)


INPUTS = ["x", "meta_tokens", "attn_w_in", "attn_sinks", "attn_w_out", "gla_w_in", "gla_w_gate_up", "gla_b_gate",
          "gla_norm_g", "gla_w_out", "moe_w_group", "moe_b_group", "moe_w_router", "moe_b_router", "moe_w_gate",
          "moe_w_up", "moe_w_down", "ln_g", "ln_b"]


def kernel(**inputs):
    import numpy as np
    from concourse import bacc
    from concourse.bass_utils import run_bass_kernel_spmd

    nc = bacc.Bacc("TRN2", target_bir_lowering=False, num_devices=1)
    arrays, args = {}, []
    for name in INPUTS:
        a = np.ascontiguousarray(inputs[name])
        arrays[f"in_{name}_dram"] = a
        args.append(nc.dram_tensor(f"in_{name}_dram", a.shape, mybir.dt.from_np(a.dtype),
                                   kind="ExternalInput").ap())
    args.append(nc.dram_tensor("out_0_dram", (1, SEQ, D), F32, kind="ExternalOutput").ap())
    build_trunk(nc, *args)
    r = run_bass_kernel_spmd(nc, [arrays], core_ids=[0])
    return r.results[0]["out_0_dram"]
```
